# Optimizing a Trainium2 kernel written in Bass

```python
import math
import jax, jax.numpy as jnp
from jax import lax
import numpy as np

D_MODEL = 1024
BATCH = 1
SEQ = 1024
DEPTH = 4

N_MIXERS = 3
D_PLE = 256
RMS_EPS = 1e-6
LN_EPS = 1e-5
NEG_INF = -1e30

GDN_HEAD_DIM = 128
GDN_HEADS = D_MODEL // GDN_HEAD_DIM
GDN_WIDTH = GDN_HEADS * GDN_HEAD_DIM
GDN_CONV = 4
GDN_CHUNK = 64
GDN_IN = 4 * GDN_WIDTH + 2 * GDN_HEADS

CC_WIDTH = D_MODEL
CC_CONV = 31
CC_IN = 3 * CC_WIDTH

SWA_HEAD_DIM = 64
SWA_Q_HEADS = D_MODEL // SWA_HEAD_DIM
SWA_KV_HEADS = SWA_Q_HEADS // 8
SWA_GROUP = SWA_Q_HEADS // SWA_KV_HEADS
SWA_WIDTH = SWA_Q_HEADS * SWA_HEAD_DIM
SWA_KV_WIDTH = SWA_KV_HEADS * SWA_HEAD_DIM
SWA_WINDOW = 128
SWA_BLOCK = 128
SWA_IN = 2 * SWA_WIDTH + 2 * SWA_KV_WIDTH
REL_BUCKETS = 32
REL_MAX_DIST = 128

N_GDN_LAYERS = (DEPTH + 2) // 3
N_CC_LAYERS = (DEPTH + 1) // 3
N_SWA_LAYERS = DEPTH // 3

kernel_name = 'hybrid_gdn_conformer_swa_trunk'

def _rmsnorm(x, g):
    xf = x.astype(jnp.float32)
    y = xf * lax.rsqrt(jnp.mean(xf * xf, axis=-1, keepdims=True) + RMS_EPS)
    return (y * g.astype(jnp.float32)).astype(x.dtype)

def _l2norm(x):
    return x * lax.rsqrt(jnp.sum(x * x, axis=-1, keepdims=True) + RMS_EPS)

def _causal_dwconv(x, w):
    K, C = w.shape
    return lax.conv_general_dilated(
        x, w[:, None, :].astype(x.dtype), window_strides=(1,), padding=[(K - 1, 0)],
        dimension_numbers=('NWC', 'WIO', 'NWC'), feature_group_count=C)

def _chunked_gated_delta_rule(q, k, v, g, beta):
    B, T, H, dk = q.shape
    dv = v.shape[-1]
    C = GDN_CHUNK
    N = T // C
    q = q * dk ** -0.5

    def chunk(t):
        return t.reshape(B, N, C, H, -1).transpose(0, 1, 3, 2, 4)

    qc, kc, vc = chunk(q), chunk(k), chunk(v)
    gcum = jnp.cumsum(g.reshape(B, N, C, H).transpose(0, 1, 3, 2), axis=-1)
    bc = beta.reshape(B, N, C, H).transpose(0, 1, 3, 2)[..., None]
    causal = jnp.tril(jnp.ones((C, C), dtype=bool))
    strict = jnp.tril(jnp.ones((C, C), dtype=bool), k=-1)
    decay = jnp.exp(jnp.where(causal, gcum[..., :, None] - gcum[..., None, :], -jnp.inf))
    kb = kc * bc
    lower = jnp.where(strict, jnp.einsum('bnhcd,bnhed->bnhce', kb, kc) * decay, 0.0)
    eye = jnp.eye(C, dtype=jnp.float32)
    rhs = jnp.concatenate([vc * bc, kb * jnp.exp(gcum)[..., None]], axis=-1)
    sol = lax.linalg.triangular_solve(eye + lower, rhs, left_side=True, lower=True, unit_diagonal=True)
    u, w = sol[..., :dv], sol[..., dv:]
    qk = jnp.where(causal, jnp.einsum('bnhcd,bnhed->bnhce', qc, kc) * decay, 0.0)

    def step(S, inp):
        q_i, k_i, u_i, w_i, qk_i, g_i = inp
        v_new = u_i - jnp.einsum('bhcd,bhde->bhce', w_i, S)
        o = (jnp.einsum('bhcd,bhde->bhce', q_i * jnp.exp(g_i)[..., None], S)
             + jnp.einsum('bhce,bhef->bhcf', qk_i, v_new))
        g_last = g_i[..., -1]
        k_dec = k_i * jnp.exp(g_last[..., None] - g_i)[..., None]
        S = S * jnp.exp(g_last)[..., None, None] + jnp.einsum('bhcd,bhce->bhde', k_dec, v_new)
        return S, o

    xs = tuple(jnp.moveaxis(t, 1, 0) for t in (qc, kc, u, w, qk, gcum))
    S0 = jnp.zeros((B, H, dk, dv), jnp.float32)
    _, o = lax.scan(step, S0, xs)
    return o.transpose(1, 0, 3, 2, 4).reshape(B, T, H, dv)

def _gated_deltanet(xn, w_in, conv_w, A_log, dt_bias, norm_g, w_out):
    B, T, _ = xn.shape
    H, Dh, W = GDN_HEADS, GDN_HEAD_DIM, GDN_WIDTH
    proj = xn @ w_in
    qkv, z, b, a = jnp.split(proj, [3 * W, 4 * W, 4 * W + H], axis=-1)
    qkv = jax.nn.silu(_causal_dwconv(qkv, conv_w)).astype(jnp.float32)
    q, k, v = jnp.split(qkv, 3, axis=-1)
    q = _l2norm(q.reshape(B, T, H, Dh))
    k = _l2norm(k.reshape(B, T, H, Dh))
    v = v.reshape(B, T, H, Dh)
    beta = jax.nn.sigmoid(b.astype(jnp.float32))
    g = -jnp.exp(A_log.astype(jnp.float32)) * jax.nn.softplus(a.astype(jnp.float32) + dt_bias.astype(jnp.float32))
    o = _chunked_gated_delta_rule(q, k, v, g, beta)
    o = o * lax.rsqrt(jnp.mean(o * o, axis=-1, keepdims=True) + RMS_EPS) * norm_g.astype(jnp.float32)
    o = o.reshape(B, T, W) * jax.nn.silu(z.astype(jnp.float32))
    return o.astype(xn.dtype) @ w_out

def _conformer_conv(xn, w_in, dw_w, dw_b, ln_g, ln_b, w_out):
    val, gl, gate = jnp.split(xn @ w_in, 3, axis=-1)
    u = val * jax.nn.sigmoid(gl)
    u = (_causal_dwconv(u, dw_w) + dw_b).astype(jnp.float32)
    mu = jnp.mean(u, axis=-1, keepdims=True)
    var = jnp.mean(jnp.square(u - mu), axis=-1, keepdims=True)
    u = (u - mu) * lax.rsqrt(var + LN_EPS) * ln_g.astype(jnp.float32) + ln_b.astype(jnp.float32)
    u = jax.nn.silu(u) * jax.nn.silu(gate.astype(jnp.float32))
    return u.astype(xn.dtype) @ w_out

def _t5_causal_bucket(n):
    max_exact = REL_BUCKETS // 2
    large = max_exact + np.floor(
        np.log(np.maximum(n, max_exact) / max_exact) / np.log(REL_MAX_DIST / max_exact)
        * (REL_BUCKETS - max_exact)).astype(np.int32)
    large = np.minimum(large, REL_BUCKETS - 1)
    return np.where(n < max_exact, n, large).astype(np.int32)

def _swa_sink_attention(xn, w_in, q_norm_g, k_norm_g, sinks, rel_bias, w_out):
    B, T, _ = xn.shape
    H, KV, G, Dh = SWA_Q_HEADS, SWA_KV_HEADS, SWA_GROUP, SWA_HEAD_DIM
    Q = SWA_BLOCK
    NB = T // Q
    proj = xn @ w_in
    q, k, v, gate = jnp.split(proj, [SWA_WIDTH, SWA_WIDTH + SWA_KV_WIDTH, SWA_WIDTH + 2 * SWA_KV_WIDTH], axis=-1)
    q = _rmsnorm(q.reshape(B, T, H, Dh), q_norm_g).reshape(B, NB, Q, KV, G, Dh)
    k = _rmsnorm(k.reshape(B, T, KV, Dh), k_norm_g).reshape(B, NB, Q, KV, Dh)
    v = v.reshape(B, NB, Q, KV, Dh)

    def with_prev(t):
        prev = jnp.pad(t[:, :-1], ((0, 0), (1, 0), (0, 0), (0, 0), (0, 0)))
        return jnp.concatenate([prev, t], axis=2)

    kw, vw = with_prev(k), with_prev(v)
    logits = jnp.einsum('bnqkgd,bnckd->bnkgqc', q, kw, preferred_element_type=jnp.float32) * Dh ** -0.5
    qi = np.arange(Q)[:, None]
    cj = np.arange(2 * Q)[None, :]
    dist = qi + Q - cj
    in_window = jnp.asarray((dist >= 0) & (dist < SWA_WINDOW))
    bucket = _t5_causal_bucket(np.maximum(dist, 0))
    bias = rel_bias.astype(jnp.float32)[bucket].reshape(Q, 2 * Q, KV, G).transpose(2, 3, 0, 1)
    key_exists = (jnp.arange(NB)[:, None, None] > 0) | jnp.asarray(cj >= Q)[None]
    valid = in_window[None] & key_exists
    logits = jnp.where(valid[None, :, None, None], logits + bias[None, None], NEG_INF)
    sink = sinks.astype(jnp.float32).reshape(1, 1, KV, G, 1, 1)
    m = jnp.maximum(jnp.max(logits, axis=-1, keepdims=True), sink)
    e = jnp.exp(logits - m)
    probs = e / (jnp.sum(e, axis=-1, keepdims=True) + jnp.exp(sink - m))
    out = jnp.einsum('bnkgqc,bnckd->bnqkgd', probs.astype(vw.dtype), vw).reshape(B, T, SWA_WIDTH)
    out = out.astype(jnp.float32) * jax.nn.silu(gate.astype(jnp.float32))
    return out.astype(xn.dtype) @ w_out

def setup_inputs(seed: int = 0) -> dict:
    key = jax.random.key(seed)
    ks = jax.random.split(key, 24)

    def nrm(k, shape, scale):
        return jax.random.normal(k, shape, jnp.float32) * scale

    dt = jnp.exp(jax.random.uniform(ks[9], (N_GDN_LAYERS, GDN_HEADS), jnp.float32,
                                    minval=math.log(1e-3), maxval=math.log(1e-1)))
    return {
        'x': nrm(ks[0], (BATCH, SEQ, D_MODEL), 1.0),
        'p': nrm(ks[1], (DEPTH, BATCH, SEQ, D_PLE), 1.0),
        'norm_g': 1.0 + nrm(ks[2], (DEPTH, D_MODEL), 0.02),
        'ple_w_gate': nrm(ks[3], (DEPTH, D_MODEL, D_MODEL), D_MODEL ** -0.5),
        'ple_w_proj': nrm(ks[4], (DEPTH, D_PLE, D_MODEL), D_PLE ** -0.5),
        'rel_bias': nrm(ks[5], (REL_BUCKETS, SWA_Q_HEADS), 0.3),
        'gdn_w_in': nrm(ks[6], (N_GDN_LAYERS, D_MODEL, GDN_IN), D_MODEL ** -0.5),
        'gdn_conv_w': nrm(ks[7], (N_GDN_LAYERS, GDN_CONV, 3 * GDN_WIDTH), GDN_CONV ** -0.5),
        'gdn_A_log': jnp.log(jax.random.uniform(ks[8], (N_GDN_LAYERS, GDN_HEADS), jnp.float32, minval=1.0, maxval=16.0)),
        'gdn_dt_bias': dt + jnp.log(-jnp.expm1(-dt)),
        'gdn_norm_g': 1.0 + nrm(ks[10], (N_GDN_LAYERS, GDN_HEAD_DIM), 0.02),
        'gdn_w_out': nrm(ks[11], (N_GDN_LAYERS, GDN_WIDTH, D_MODEL), GDN_WIDTH ** -0.5),
        'cc_w_in': nrm(ks[12], (N_CC_LAYERS, D_MODEL, CC_IN), D_MODEL ** -0.5),
        'cc_dw_w': nrm(ks[13], (N_CC_LAYERS, CC_CONV, CC_WIDTH), CC_CONV ** -0.5),
        'cc_dw_b': nrm(ks[14], (N_CC_LAYERS, CC_WIDTH), 0.02),
        'cc_ln_g': 1.0 + nrm(ks[15], (N_CC_LAYERS, CC_WIDTH), 0.02),
        'cc_ln_b': nrm(ks[16], (N_CC_LAYERS, CC_WIDTH), 0.02),
        'cc_w_out': nrm(ks[17], (N_CC_LAYERS, CC_WIDTH, D_MODEL), CC_WIDTH ** -0.5),
        'swa_w_in': nrm(ks[18], (N_SWA_LAYERS, D_MODEL, SWA_IN), D_MODEL ** -0.5),
        'swa_q_norm_g': 1.0 + nrm(ks[19], (N_SWA_LAYERS, SWA_HEAD_DIM), 0.02),
        'swa_k_norm_g': 1.0 + nrm(ks[20], (N_SWA_LAYERS, SWA_HEAD_DIM), 0.02),
        'swa_sinks': nrm(ks[21], (N_SWA_LAYERS, SWA_Q_HEADS), 1.0),
        'swa_w_out': nrm(ks[22], (N_SWA_LAYERS, SWA_WIDTH, D_MODEL), SWA_WIDTH ** -0.5),
    }

def reference(x, p, norm_g, ple_w_gate, ple_w_proj, rel_bias,
              gdn_w_in, gdn_conv_w, gdn_A_log, gdn_dt_bias, gdn_norm_g, gdn_w_out,
              cc_w_in, cc_dw_w, cc_dw_b, cc_ln_g, cc_ln_b, cc_w_out,
              swa_w_in, swa_q_norm_g, swa_k_norm_g, swa_sinks, swa_w_out):
    for i in range(DEPTH):
        kind, slot = i % N_MIXERS, i // N_MIXERS
        h = _rmsnorm(x, norm_g[i])
        if kind == 0:
            y = _gated_deltanet(h, gdn_w_in[slot], gdn_conv_w[slot], gdn_A_log[slot],
                                gdn_dt_bias[slot], gdn_norm_g[slot], gdn_w_out[slot])
        elif kind == 1:
            y = _conformer_conv(h, cc_w_in[slot], cc_dw_w[slot], cc_dw_b[slot],
                                cc_ln_g[slot], cc_ln_b[slot], cc_w_out[slot])
        else:
            y = _swa_sink_attention(h, swa_w_in[slot], swa_q_norm_g[slot], swa_k_norm_g[slot],
                                    swa_sinks[slot], rel_bias, swa_w_out[slot])
        x = x + y
        x = x + jax.nn.sigmoid(x @ ple_w_gate[i]) * (p[i] @ ple_w_proj[i])
    return x


_drawn_inputs = setup_inputs


def setup_inputs(seed=0):
    import zlib

    import numpy as np

    out = dict(_drawn_inputs(seed))
    spreads = {}
    factors = {'rel_bias': 43.591,
     'gdn_norm_g': 4.72,
     'cc_dw_b': 5.64,
     'cc_ln_g': 8.0,
     'cc_ln_b': 8.0,
     'swa_q_norm_g': 23.937,
     'swa_k_norm_g': 23.488,
     'swa_sinks': 200.0}
    for name, (base, spread) in spreads.items():
        noise = np.random.default_rng([zlib.crc32(name.encode()), seed]).standard_normal(out[name].shape)
        drawn = base * np.exp(spread * noise) if base else spread * noise
        out[name] = __import__('jax').numpy.asarray(drawn.astype(out[name].dtype))
    for name, factor in factors.items():
        out[name] = (out[name] * factor).astype(out[name].dtype)
    return out
```

```python
from contextlib import ExitStack

import numpy as np

import concourse.bass as bass
from concourse import mybir

F32 = mybir.dt.float32
F32R = mybir.dt.float32r
BF16 = mybir.dt.bfloat16
ALU = mybir.AluOpType
ACT = mybir.ActivationFunctionType
AX_X = mybir.AxisListType.X

P = 128
D = 1024
T = 1024
KT = D // P
HALF = 512
DEPTH = 4
PLE_K = 2
RMS_EPS = 1e-6
LN_EPS = 1e-5
HEADS = 8
TAPS = 4
CHUNK = 128
NCHUNK = T // CHUNK
GROUP = 4
Z_EARLY = 32
LEVELS = 7
CC_TAPS = 31
WINDOW = 128
NB = T // WINDOW
QH = 16
HD = 64
BUCKETS = 32
BIAS_LEN = 3 * WINDOW - 1
NEG = -1e30

GDN_IN = 4 * HEADS
CC_IN = 3 * KT
SWA_IN = 2 + 2 * KT
OUT = KT
LAYER_IN = [GDN_IN, CC_IN, SWA_IN, GDN_IN]
TILE0 = [sum(LAYER_IN[:l]) + 2 * OUT * l for l in range(DEPTH + 1)]
TILES = TILE0[DEPTH]


class Chain:

    def __init__(self, eng, sem, base):
        self.eng, self.sem, self.base, self.n = eng, sem, base, 0

    def link(self, ins):
        ins.then_inc(self.sem, 1)
        self.n += 1
        self.eng.wait_ge(self.sem, self.base + self.n)

    def end(self, n):
        assert self.n == n, (self.sem, self.n, n)


def build(nc, d):
    ctx = ExitStack()
    with ctx:
        psum = [ctx.enter_context(nc.psum_tensor(f"bank{b}", [P, HALF], F32)) for b in range(8)]
        PB = [psum[0:2], psum[2:4]]
        DB = psum[4:8]

        def at(name, offset, shape, dt=F32):
            return nc.alloc_sbuf_tensor_at(name, [P] + shape, dt, offset=offset)

        S0 = 16512
        w_raw = [at(f"w_raw{j}", S0 + 4096 * j, [KT, P]) for j in range(2)]
        w_hi = [at(f"w_hi{j}", S0 + 8192 + 4096 * j, [KT, P], F32R) for j in range(2)]
        w_lo = [at(f"w_lo{j}", S0 + 16384 + 4096 * j, [KT, P], F32R) for j in range(2)]
        A0 = S0 + 24576
        a_hi = at("a_hi", A0, [KT, T], F32R)
        a_lo = at("a_lo", A0 + 32768, [KT, T], F32R)
        X0 = A0 + 65536
        x_sb = at("x_sb", X0, [KT, T])
        B0 = X0 + 32768
        b_hi = at("b_hi", B0, [KT, T], F32R)
        b_lo = at("b_lo", B0 + 32768, [KT, T], F32R)
        M0 = B0 + 65536
        C0 = 229344 - 11872
        cur = [C0]

        def const(name, shape, dt=F32):
            n = int(np.prod(shape)) * (2 if dt == BF16 else 4)
            t = at(name, cur[0], shape, dt)
            cur[0] += (n + 31) // 32 * 32
            assert cur[0] <= 229344, (name, cur[0])
            return t

        ident = const("ident", [P])
        ident_r = const("ident_r", [P], F32R)
        cum_u = const("cum_u", [P])
        mask_t = const("mask_t", [P])
        ones = const("ones", [P])
        level_mask = const("level_mask", [LEVELS, P], BF16)
        strict = const("strict", [P], BF16)
        norm_g = const("norm_g", [DEPTH, KT])
        conv_w = const("conv_w", [2, HEADS, 3, TAPS])
        a_log = const("a_log", [2, HEADS, NCHUNK])
        dt_b = const("dt_b", [2, HEADS, NCHUNK])
        gdn_g = const("gdn_g", [2, 1])
        gdn_gh = const("gdn_gh", [2, 1])
        KINDS = 7
        NGC, EG, NEG_EG, EDEC, EGL, BETA, GG = range(KINDS)
        tok = const("tok", [HEADS, KINDS, NCHUNK])
        hv = [const(f"hv{j}", [KINDS, NCHUNK]) for j in range(2)]
        cw = const("cw", [3, TAPS])
        ssk = const("ssk", [NCHUNK])
        ssq = const("ssq", [NCHUNK])
        c_tok = const("c_tok", [NCHUNK])
        sq_tk = const("sq_tk", [NCHUNK])
        half_e = const("half_e", [NCHUNK])
        mhalf_e = const("mhalf_e", [NCHUNK])
        tq = const("tq", [NCHUNK])
        oss = const("oss", [NCHUNK])
        om = const("om", [NCHUNK])
        osc = const("osc", [NCHUNK])
        blk = const("blk", [P])
        sinks = const("sinks", [QH])
        qk_g = const("qk_g", [2])
        cc_w = const("cc_w", [KT, CC_TAPS])
        cc_par = const("cc_par", [3, KT])
        CC_B, LN_G, LN_B = range(3)
        eps = const("eps", [1])
        ln_eps = const("ln_eps", [1])

        acc = at("acc", M0, [T])
        sqt = at("sqt", M0 + 4096, [T])
        rstd = at("rstd", B0 + 16384, [T])
        hf = [at(f"hf{j}", B0 + 20480 + 4096 * j, [T]) for j in range(2)]

        class Embedding:

            def __init__(self, name, base):
                self.p_raw = at(name + "p_raw", base, [PLE_K, T])
                self.pw_raw = at(name + "pw_raw", base + 8192, [KT, PLE_K, P])
                self.p_hi = at(name + "p_hi", base + 16384, [PLE_K, T], F32R)
                self.p_lo = at(name + "p_lo", base + 24576, [PLE_K, T], F32R)
                self.pw_hi = at(name + "pw_hi", base + 32768, [KT, PLE_K, P], F32R)
                self.pw_lo = at(name + "pw_lo", base + 40960, [KT, PLE_K, P], F32R)
                self.p_th = at(name + "p_th", base + 49152, [T])
                self.p_t = at(name + "p_t", base + 53248, [T])

        in_a, in_b = (a_hi, a_lo), (b_hi, b_lo)
        emb_a, emb_b = Embedding("a_", A0), Embedding("b_", B0)
        PLACES = {"gdn": (in_b, in_a, emb_b), "swa": (in_b, in_a, emb_b), "cc": (in_a, in_b, emb_a)}

        PAD = CC_TAPS - 1
        u_in = [at(f"u_in{j}", M0 + 4224 * j, [PAD + T]) for j in range(2)]
        cc_th = at("cc_th", M0 + 8448, [T])
        uc = at("uc", B0, [KT, T])
        cc_gate = at("cc_gate", B0 + 32768, [KT, T])
        mu = at("mu", M0, [T])
        cc_sq = at("cc_sq", M0 + 4096, [T])
        cc_rstd = at("cc_rstd", M0 + 8192, [T])

        bias = at("bias", X0, [2, 2, 2 * WINDOW])
        k_pad = [at("k_pad0", B0 + 6 * 4096, [2, T]), at("k_pad1", X0 + 4096, [2, T])]
        v_tok = at("v_tok", X0 + 12288, [NB, P])
        q_n = [at(f"q_n{j}", X0 + 16384 + 4096 * j, [T]) for j in range(2)]
        zs = [at(f"zs{j}", X0 + 24576 + 4096 * j, [T]) for j in range(2)]
        qs = at("qs", M0, [T])
        lg = [at(f"lg{j}", M0 + 4096 + 2048 * j, [2, 2 * WINDOW]) for j in range(2)]
        pr_t = [at(f"pr_t{j}", M0 + 8192 + 2048 * j, [2, 2, WINDOW]) for j in range(2)]
        sm = [at(f"sm{j}", M0 + 12288 + 64 * j, [8, 2]) for j in range(2)]
        MX, MM, NEG_M, SK, ES, ESK, DEN, RDEN = range(8)
        rel = nc.alloc_sbuf_tensor_at("rel", [BUCKETS, QH], F32, offset=A0)
        onehot = nc.alloc_sbuf_tensor_at("onehot", [BUCKETS, BIAS_LEN], F32, offset=A0 + 64)
        bias_mask = nc.alloc_sbuf_tensor_at("bias_mask", [QH, BIAS_LEN], F32, offset=A0 + 2048)
        bias_rows = nc.alloc_sbuf_tensor_at("bias_rows", [QH, BIAS_LEN], F32, offset=A0 + 4096)

        o_sb = at("o_sb", X0, [HEADS, T])
        kq = [at(f"kq{j}", B0 + 16384 * j, [NCHUNK, 2, P]) for j in range(2)]
        vb = [at(f"vb{j}", B0 + 16384 * j + 8192, [T]) for j in range(2)]
        zb = [at(f"zb{j}", B0 + 16384 * j + 12288, [T]) for j in range(2)]
        G0 = B0 + 32768

        def slot(name, g, s, dt=F32):
            return at(f"{name}{g}", G0 + (g * 8 + s) * 2048, [GROUP, P], dt)

        u_g = [slot("u_g", g, 0) for g in range(2)]
        p_m = [slot("p_m", g, 0, F32R) for g in range(2)]
        y_m = [slot("y_m", g, 0) for g in range(2)]
        arg = [slot("arg", g, 1) for g in range(2)]
        nt_r = [slot("nt_r", g, 1, F32R) for g in range(2)]
        tt = [slot("tt", g, 1) for g in range(2)]
        dt_m = [slot("dt_m", g, 2) for g in range(2)]
        m_m = [slot("m_m", g, 2, F32R) for g in range(2)]
        dts = [slot("dts", g, 3) for g in range(2)]
        mt_m = [slot("mt_m", g, 3, F32R) for g in range(2)]
        nt = [slot("nt", g, 4) for g in range(2)]
        o_g = [slot("o_g", g, 4) for g in range(2)]
        p_t_m = [slot("p_t_m", g, 5) for g in range(2)]
        k_dec = [slot("k_dec", g, 6) for g in range(2)]
        r_v = [slot("r_v", g, 7) for g in range(2)]
        kt_sq = at("kt_sq", G0 + 3 * 2048 + 512, [P])
        state = at("state", G0 + 2 * 2048, [P])
        r4 = at("r4", G0 + 2 * 2048 + 512, [P])
        u_sb = at("u_sb", G0 + 2 * 2048 + 1024, [P])
        qs_sb = at("qs_sb", G0 + 2 * 2048 + 1536, [P])
        sq_o = at("sq_o", G0 + 3 * 2048, [P])
        F0 = G0 + 32768
        c_in = at("c_in", F0, [TAPS - 1 + T])
        c_acc = at("c_acc", F0 + 4128, [T])
        th = at("th", F0 + 8224, [T])
        assert F0 + 12320 <= C0
        WB0 = G0 + 12 * 2048
        wb_raw = at("wb_raw", WB0, [KT, 2 * HEADS])
        wb_hi = at("wb_hi", WB0 + 512, [KT, 2 * HEADS], F32R)
        wb_lo = at("wb_lo", WB0 + 1024, [KT, 2 * HEADS], F32R)
        g_t = [at(f"g_t{j}", WB0 + 2048 + 256 * j, [HEADS, NCHUNK]) for j in range(6)]
        ba_rows = nc.alloc_sbuf_tensor_at("ba_rows", [2 * HEADS, T], F32, offset=G0 + 6 * 2048)
        mask_stage = at("mask_stage", B0, [LEVELS + 1, P])

        flat = lambda t: t[:, :, :].rearrange("p a b -> p (a b)")
        conv_flat = conv_w[:, :, :, :, :].rearrange("p s h r t -> p (s h r t)")
        tok_flat = tok[:, :, :, :].rearrange("p h k c -> p (h k c)")
        CONSTS = {
            "c_ident": ident[:, :], "c_cum_u": cum_u[:, :], "c_mask_t": mask_t[:, :], "c_ones": ones[:, :],
            "c_masks": mask_stage[:, :, :].rearrange("p a b -> p (a b)"),
            "c_norm_g": norm_g[:, :, :].rearrange("p a b -> p (a b)"), "c_conv_w": conv_flat,
            "c_a_log": a_log[:, :, :, :].rearrange("p s h c -> p (s h c)"),
            "c_dt_b": dt_b[:, :, :, :].rearrange("p s h c -> p (s h c)"),
            "c_gdn_g": gdn_g[:, :, 0], "c_blk": blk[:, :], "c_sinks": sinks[:, :], "c_qk_g": qk_g[:, :],
            "c_cc_w": cc_w[:, :, :].rearrange("p a b -> p (a b)"),
            "c_cc_par": cc_par[:, :, :].rearrange("p a b -> p (a b)"),
            "c_rel": rel[:, :], "c_onehot": onehot[:, :], "c_bias_mask": bias_mask[:, :],
        }

        def sem(name):
            return ctx.enter_context(nc.semaphore(name))

        const_loaded = sem("const_loaded")
        const_ready = sem("const_ready")
        w_loaded = [sem(f"w_loaded{j}") for j in range(2)]
        w_hi_done = sem("w_hi_done")
        w_split = sem("w_split")
        tile_done = sem("tile_done")
        pb_free = [sem(f"pb_free{j}") for j in range(2)]
        x_tile_loaded = [sem(f"x_tile_loaded{k}") for k in range(KT)]
        sq_done = sem("sq_done")
        acc_done = sem("acc_done")
        stat_done = sem("stat_done")
        rstd_step = sem("rstd_step")
        hf_done = sem("hf_done")
        split_hi = sem("split_hi")
        split_lo = sem("split_lo")
        x_mid = sem("x_mid")
        x_new = sem("x_new")
        x_reloaded = sem("x_reloaded")
        x_stored = sem("x_stored")
        p_loaded = sem("p_loaded")
        pw_loaded = sem("pw_loaded")
        p_hi_done = sem("p_hi_done")
        p_split = sem("p_split")
        pp_done = sem("pp_done")
        p_th_done = sem("p_th_done")
        p_t_done = sem("p_t_done")

        def split_at(l, which, k):
            return 24 * l + 8 * which + k

        def pairs(first, n):
            return first // 2, n // 2

        x_flat, o_flat = flat(x_sb), flat(o_sb)
        flat4 = lambda t: t[:, :, :, :].rearrange("p a b c -> p (a b c)")
        a_hi_flat, a_lo_flat, b_hi_flat, b_lo_flat = flat(a_hi), flat(a_lo), flat(b_hi), flat(b_lo)

        wb_loaded = sem("wb_loaded")
        wb_hi_done = sem("wb_hi_done")
        wb_split = sem("wb_split")
        ba_rows_done = sem("ba_rows_done")
        ba_rows_ready = sem("ba_rows_ready")
        ba_done = sem("ba_done")
        ba_step = sem("ba_step")
        ba_act = sem("ba_act")
        g_ready = sem("g_ready")
        gcum_done = sem("gcum_done")
        tok_done = sem("tok_done")
        pad_ready = sem("pad_ready")
        conv_step = sem("conv_step")
        conv_done = sem("conv_done")
        th_done = sem("th_done")
        silu_done = sem("silu_done")
        cw_ready = sem("cw_ready")
        kt_done = sem("kt_done")
        ss_read = sem("ss_read")
        dve_step = sem("dve_step")
        sqrt_done = sem("sqrt_done")
        hv_ready = sem("hv_ready")
        c_ready = sem("c_ready")
        ug_ready = sem("ug_ready")
        rowg_done = sem("rowg_done")
        arg_ready = sem("arg_ready")
        dt_ready = sem("dt_ready")
        dts_ready = sem("dts_ready")
        gram_done = sem("gram_done")
        nt_ready = sem("nt_ready")
        ntr_ready = sem("ntr_ready")
        tr_done = sem("tr_done")
        kdec_ready = sem("kdec_ready")
        ssk_done = sem("ssk_done")
        ssq_done = sem("ssq_done")
        rv_ready = sem("rv_ready")
        pm_done = sem("pm_done")
        p_ready = sem("p_ready")
        m_done = sem("m_done")
        m_ready = sem("m_ready")
        mt_ready = sem("mt_ready")
        y_done = sem("y_done")
        y_ready = sem("y_ready")
        t_done = sem("t_done")
        tt_ready = sem("tt_ready")
        ks_done = sem("ks_done")
        qs_done = sem("qs_done")
        qs_ready = sem("qs_ready")
        r4_ready = sem("r4_ready")
        u_done = sem("u_done")
        u_ready = sem("u_ready")
        ds_done = sem("ds_done")
        op_done = sem("op_done")
        s_ready = sem("s_ready")
        o_ready = sem("o_ready")
        oss_ready = sem("oss_ready")
        om_ready = sem("om_ready")
        tq_ready = sem("tq_ready")
        osc_ready = sem("osc_ready")
        on_ready = sem("on_ready")
        ot_done = sem("ot_done")
        o_written = sem("o_written")

        block = ctx.enter_context(nc.Block())

        cc_u_ready = sem("cc_u_ready")
        cc_pad = sem("cc_pad")
        tap = sem("tap")
        cc_done = sem("cc_done")
        mean_done = sem("mean_done")
        mu_ready = sem("mu_ready")
        centred = sem("centred")
        cc_sq_ready = sem("cc_sq_ready")
        var_done = sem("var_done")
        cc_rstd_step = sem("cc_rstd_step")
        scaled_u = sem("scaled_u")
        silu_u = sem("silu_u")
        gated_u = sem("gated_u")
        bias_psum = sem("bias_psum")
        bias_sum = sem("bias_sum")
        bias_stored = sem("bias_stored")
        bias_spread = sem("bias_spread")
        bias_loaded = [sem(f"bias_loaded{j}") for j in range(2)]
        nsq_ready = sem("nsq_ready")
        nms_done = sem("nms_done")
        nln_done = sem("nln_done")
        nrr_ready = sem("nrr_ready")
        qn_ready = sem("qn_ready")
        k_spread = sem("k_spread")
        k_zeros = sem("k_zeros")
        v_turned = sem("v_turned")
        v_ready = sem("v_ready")
        lmm_done = sem("lmm_done")
        lg_ready = sem("lg_ready")
        soft_step = sem("soft_step")
        mx_ready = sem("mx_ready")
        e_ready = sem("e_ready")
        esk_ready = sem("esk_ready")
        den_ready = sem("den_ready")
        r_ready = sem("r_ready")
        pr_ready = sem("pr_ready")
        trp_done = sem("trp_done")
        prt_ready = sem("prt_ready")
        pv_done = sem("pv_done")
        att_ready = sem("att_ready")
        gth_done = sem("gth_done")
        half_hi = sem("half_hi")
        half_lo = sem("half_lo")

        def gdn_slot(l):
            return l // 3

        @block.sync
        def _(sp):
            def section(source, base, n):
                first = 0
                if base == 0:
                    for j in range(2):
                        sp.dma_start(flat(w_raw[j]), source[j]).then_inc(w_loaded[j], 16)
                    first = 1
                with sp.Fori(first, n // 2) as i:
                    for j in range(2):
                        sp.wait_ge(w_split, base + 2 * i + j - 1)
                        sp.dma_start(flat(w_raw[j]), source[bass.ds(2 * i + j, 1)]
                                     .rearrange("a p n -> (a p) n")).then_inc(w_loaded[j], 16)

            for l in range(LAYERS):
                mixer = MIXER[l]
                section(d["w_" + mixer + "_in"][gdn_slot(l) if mixer == "gdn" else 0], TILE0[l], LAYER_IN[l])
                section(d["w_" + mixer + "_out"][gdn_slot(l) if mixer == "gdn" else 0], TILE0[l] + LAYER_IN[l], OUT)
                section(d["w_gate"][l], TILE0[l] + LAYER_IN[l] + OUT, OUT)

        @block.gpsimd
        def _(pool):
            def split_tile(pair, j):
                pool.wait_ge(w_loaded[j], 16 * (pair + 1))
                if not (isinstance(pair, int) and pair == 0):
                    pool.wait_ge(tile_done, 2 * pair + j - 1)
                nc.gpsimd.tensor_tensor(w_hi[j][:, :, :], w_raw[j][:, :, :],
                                        ones[:, :].unsqueeze(1).to_broadcast([P, KT, P]), ALU.mult)\
                    .then_inc(w_hi_done, 1)
                pool.wait_ge(w_hi_done, 2 * pair + j + 1)
                nc.gpsimd.tensor_tensor(flat(w_lo[j]), flat(w_raw[j]), flat(w_hi[j]).bitcast(F32),
                                        ALU.subtract).then_inc(w_split, 1)

            def section(base, n):
                if base + n + 2 > STREAM:
                    n -= 2
                with pool.Fori(0, n // 2) as i:
                    for j in range(2):
                        split_tile(base // 2 + i + 1, j)

            def gdn(l):
                pair0, h0 = TILE0[l] // 2, HEADS * gdn_slot(l)

                def prepare(h):
                    hh = h0 + h
                    for g in range(2):
                        pool.wait_ge(dt_ready, 2 * hh + g + 1)
                        nc.gpsimd.tensor_tensor(dts[g][:, :, :], dt_m[g][:, :, :],
                                                strict[:, :].unsqueeze(1).to_broadcast([P, GROUP, P]),
                                                ALU.mult).then_inc(dts_ready, 1)
                    pool.wait_ge(ss_read, hh + 1)
                    nc.gpsimd.tensor_tensor(sq_tk[:, :], ssk[:, :], half_e[:, :], ALU.pow)\
                        .then_inc(sqrt_done, 1)

                def output_scale(hh, g):
                    pool.wait_ge(om_ready, 2 * hh + g + 1)
                    nc.gpsimd.tensor_tensor(osc[:, 4 * g:4 * g + 4], om[:, 4 * g:4 * g + 4],
                                            mhalf_e[:, 4 * g:4 * g + 4], ALU.pow).then_inc(osc_ready, 1)

                def delta(h, j, last):
                    hh = h0 + h
                    pair = pair0 + 2 * (h + 1)
                    split_tile(pair, 1)
                    if not last:
                        split_tile(pair + 1, 0)
                        split_tile(pair + 1, 1)
                    output_scale(hh, 0)
                    if not last:
                        split_tile(pair + 2, 0)
                    output_scale(hh, 1)
                    if not last:
                        prepare(h + 1)

                for pair, r in ((1, 0), (1, 1), (2, 0)):
                    split_tile(pair0 + pair, r)
                prepare(0)
                with pool.Fori(0, (HEADS - 2) // 2) as i:
                    for j in range(2):
                        delta(2 * i + j, j, False)
                delta(HEADS - 2, 0, False)
                delta(HEADS - 1, 1, True)

            def swa(l):
                pair0 = TILE0[l] // 2

                def probabilities(n, b):
                    keys = slice(WINDOW if b == 0 else 0, 2 * WINDOW)
                    e = lg[b % 2][:, :, keys]
                    pool.wait_ge(r_ready, NB * n + b + 1)
                    nc.gpsimd.tensor_tensor(e, e, sm[b % 2][:, RDEN, :].unsqueeze(2).to_broadcast([P, 2, keys.stop - keys.start]),
                                            ALU.mult).then_inc(pr_ready, 1)

                def heads(n, last):
                    for b in range(4):
                        probabilities(n, b)
                    if not last:
                        split_tile(pair0 + n + 3, 0)
                    for b in range(4, NB):
                        probabilities(n, b)
                    if not last:
                        split_tile(pair0 + n + 3, 1)

                for n in range(2):
                    for j in range(2):
                        split_tile(pair0 + 1 + n, j)
                with pool.Fori(0, KT - 1) as n:
                    heads(n, False)
                heads(KT - 1, True)

            pool.wait_ge(const_ready, 1)
            split_tile(0, 0)
            split_tile(0, 1)
            for l in range(LAYERS):
                if MIXER[l] == "gdn":
                    gdn(l)
                elif MIXER[l] == "swa":
                    swa(l)
                else:
                    section(TILE0[l], LAYER_IN[l])
                section(TILE0[l] + LAYER_IN[l], OUT)
                section(TILE0[l] + LAYER_IN[l] + OUT, OUT)

        @block.tensor
        def _(pe):
            PASSES = ((0, 0), (0, 1), (1, 0))

            def product(out, j, k, half, act, last):
                for n, (wl, al) in enumerate(PASSES):
                    mm = pe.matmul(out[:, :], (w_lo if wl else w_hi)[j][:, k, :],
                                   act[al][:, k, half * HALF:(half + 1) * HALF],
                                   start=(k == 0 and n == 0), stop=(last and n == 2), skip_group_check=True)
                return mm

            def tile(pair, j, act, lo_waits=None):
                pe.wait_ge(w_split, 2 * pair + j + 1)
                if not (isinstance(pair, int) and pair == 0):
                    pe.wait_ge(pb_free[j], pair)
                for k in range(KT):
                    if lo_waits is not None:
                        pe.wait_ge(split_lo, lo_waits + k + 1)
                    for half in range(2):
                        mm = product(PB[j][half], j, k, half, act, k == KT - 1)
                mm.then_inc(tile_done, 1)

            def stats(value, weights):
                pe.wait_ge(acc_done, 7 * value)
                for half in range(2):
                    mm = pe.matmul(DB[half][:, :], weights[:, :], acc[:, half * HALF:(half + 1) * HALF],
                                   start=True, stop=True)
                mm.then_inc(stat_done, 1)

            def out_projection(l):
                pair0 = (TILE0[l] + LAYER_IN[l]) // 2
                for j in range(2):
                    tile(pair0, j, PLACES[MIXER[l]][0], split_at(l, 1, 0) if j == 0 else None)
                with pe.Fori(1, OUT // 2) as i:
                    for j in range(2):
                        tile(pair0 + i, j, PLACES[MIXER[l]][0])

            def embedding_product(l, n, j):
                em = PLACES[MIXER[l]][2]
                if not isinstance(n, int) or n >= 2:
                    pe.wait_ge(p_t_done, OUT * l + n - 1)
                for half in range(2):
                    for k in range(PLE_K):
                        for m, (wl, al) in enumerate(PASSES):
                            mm = pe.matmul(DB[2 * j + half][:, :],
                                           (em.pw_lo if wl else em.pw_hi)[:, n, k, :],
                                           (em.p_lo if al else em.p_hi)[:, k, half * HALF:(half + 1) * HALF],
                                           start=(k == 0 and m == 0), stop=(k == PLE_K - 1 and m == 2),
                                           skip_group_check=True)
                mm.then_inc(pp_done, 1)

            def embedding(l):
                pair0 = (TILE0[l] + LAYER_IN[l] + OUT) // 2
                for n in range(OUT):
                    tile(pair0 + n // 2, n % 2, PLACES[MIXER[l]][1], split_at(l, 2, 0) if n == 0 else None)
                    if n == 1:
                        pe.wait_ge(p_split, 2 * (l + 1))
                    if n > 0:
                        embedding_product(l, n - 1, (n - 1) % 2)
                embedding_product(l, OUT - 1, (OUT - 1) % 2)

            def gdn(l):
                pair0, h0 = TILE0[l] // 2, HEADS * gdn_slot(l)
                tile(pair0, 0, (a_hi, a_lo), split_at(l, 0, 0))
                pe.wait_ge(wb_split, gdn_slot(l) + 1)
                for half in range(2):
                    for k in range(KT):
                        for m, (wl, al) in enumerate(PASSES):
                            mm = pe.matmul(DB[half][0:2 * HEADS, :], (wb_lo if wl else wb_hi)[:, k, :],
                                           (a_lo if al else a_hi)[:, k, half * HALF:(half + 1) * HALF],
                                           start=(k == 0 and m == 0), stop=(k == KT - 1 and m == 2),
                                           skip_group_check=True)
                mm.then_inc(ba_rows_done, 1)
                tile(pair0, 1, (a_hi, a_lo))
                pe.wait_ge(ba_rows_ready, gdn_slot(l) + 1)
                for c in range(NCHUNK):
                    mm = pe.transpose(DB[2][:, c * 16:c * 16 + 16], ba_rows[:, c * CHUNK:(c + 1) * CHUNK],
                                      ident[0:2 * HEADS, 0:2 * HEADS])
                mm.then_inc(ba_done, 1)
                tile(pair0 + 1, 0, (a_hi, a_lo))
                pe.wait_ge(g_ready, gdn_slot(l) + 1)
                pe.matmul(DB[3][:, 0:64], cum_u[:, :], flat(g_t[5]), start=True, stop=True)
                pe.matmul(DB[3][:, 64:128], ones[:, :], flat(g_t[5]), start=True, stop=True)\
                    .then_inc(gcum_done, 1)

                def filler(h, first, end):
                    sent = [first]

                    def fill(n):
                        for _ in range(n):
                            s = sent[0]
                            if s == end:
                                return
                            r, half, k, m = s // 48, s % 48 // 24, s % 24 // 3, s % 3
                            j, pair = (r + 1) % 2, pair0 + 2 * h + 1 + r // 2 + r % 2
                            if s % 48 == 0:
                                pe.wait_ge(w_split, 2 * pair + j + 1)
                                pe.wait_ge(pb_free[j], pair)
                            wl, al = PASSES[m]
                            mm = pe.matmul(PB[j][half][:, :], (w_lo if wl else w_hi)[j][:, k, :],
                                           (a_lo if al else a_hi)[:, k, half * HALF:(half + 1) * HALF],
                                           start=(k == 0 and m == 0), stop=(k == KT - 1 and m == 2),
                                           skip_group_check=True)
                            if s % 48 == 47:
                                mm.then_inc(tile_done, 1)
                            sent[0] += 1

                    return fill

                def prepare(h, fill):
                    hh = h0 + h
                    for g in range(2):
                        pe.wait_ge(ug_ready, 2 * hh + g + 1)
                        pe.matmul(DB[g][:, :], ones[:, :], flat(u_g[g]), start=True, stop=True)\
                            .then_inc(rowg_done, 1)
                    fill(10)

                def turn_k(h, p, n, out):
                    if n == 0:
                        pe.wait_ge(silu_done, 4 * (h0 + h) + 1)
                    pe.transpose(out, kq[p][:, n, 0, :], ident[:, :]).then_inc(kt_done, 1)

                def delta(h, j, last):
                    hh = h0 + h
                    fill = filler(h, Z_EARLY, 48 if last else 192 + Z_EARLY)
                    k_q = kq[j]
                    for g in range(2):
                        pe.wait_ge(arg_ready, 2 * hh + 2)
                        for c in range(GROUP):
                            kc = k_q[:, GROUP * g + c, 0, :]
                            mm = pe.matmul(DB[2 * g + c // 2][:, (c % 2) * 256:(c % 2) * 256 + 256], kc,
                                           k_q[:, GROUP * g + c, :, :].rearrange("p a b -> p (a b)"),
                                           start=True, stop=True)
                        mm.then_inc(gram_done, 1)
                        fill(5)
                    pe.wait_ge(silu_done, 4 * hh + 3)
                    for g in range(2):
                        pe.wait_ge(nt_ready, 2 * hh + g + 1)
                        for c in range(GROUP):
                            n = GROUP * g + c
                            pe.transpose(DB[2 * g][:, c * P:(c + 1) * P], k_q[:, n, 1, :], ident[:, :])
                            mm = pe.transpose(DB[2 * g + 1][:, c * P:(c + 1) * P],
                                              vb[j][:, n * P:(n + 1) * P], ident[:, :])
                        mm.then_inc(tr_done, 1)
                        fill(5)
                    for lv in range(LEVELS):
                        for g in range(2):
                            e = 2 * (LEVELS * hh + lv) + g
                            if lv == 0:
                                pe.wait_ge(ntr_ready, 2 * hh + g + 1)
                                pe.wait_ge(ssq_done, NCHUNK * hh + GROUP * (g + 1))
                            else:
                                pe.wait_ge(m_ready, e - 1)
                            for c in range(GROUP):
                                mm = pe.matmul(DB[2 * g][:, c * P:(c + 1) * P], nt_r[g][:, c, :],
                                               m_m[g][:, c, :] if lv else ident_r[:, :], start=True, stop=True)
                            mm.then_inc(pm_done, 1)
                            fill(4)
                        for g in range(2):
                            e = 2 * (LEVELS * hh + lv) + g
                            pe.wait_ge(p_ready, e + 1)
                            if lv:
                                pe.wait_ge(mt_ready, e - 1)
                                for c in range(GROUP):
                                    pe.matmul(DB[2 * g][:, c * P:(c + 1) * P], mt_m[g][:, c, :],
                                              p_m[g][:, c, :], start=True, stop=True)
                                pe.matmul(DB[2 * g + 1][:, :], ident_r[:, :], flat(mt_m[g]),
                                          start=True, stop=False, skip_group_check=True)
                            else:
                                pe.wait_ge(rv_ready, 2 * hh + g + 1)
                                for c in range(GROUP):
                                    pe.matmul(DB[2 * g + 1][:, c * P:(c + 1) * P], ident_r[:, :],
                                              ident_r[:, :], start=(c == 0), stop=False, skip_group_check=True)
                            for c in range(GROUP):
                                mm = pe.matmul(DB[2 * g + 1][:, c * P:(c + 1) * P], p_m[g][:, c, :],
                                               mt_m[g][:, c, :] if lv else ident_r[:, :],
                                               start=False, stop=(c == GROUP - 1), skip_group_check=True)
                            mm.then_inc(m_done, 1)
                            fill(3)
                    for g in range(2):
                        pe.wait_ge(m_ready, 2 * (LEVELS * hh + LEVELS - 1) + g + 1)
                        for c in range(GROUP):
                            mm = pe.matmul(DB[2 * g][:, c * P:(c + 1) * P], nt[g][:, c, :],
                                           m_m[g][:, c, :].bitcast(F32), start=True, stop=True)
                        mm.then_inc(y_done, 1)
                        fill(3)
                    for g in range(2):
                        pe.wait_ge(y_ready, 2 * hh + g + 1)
                        pe.wait_ge(mt_ready, 2 * (LEVELS * hh + LEVELS - 1) + g + 1)
                        for c in range(GROUP):
                            mm = pe.matmul(DB[2 * g + 1][:, c * P:(c + 1) * P], y_m[g][:, c, :],
                                           mt_m[g][:, c, :].bitcast(F32), start=True, stop=True)
                        mm.then_inc(t_done, 1)
                        fill(3)
                    for n in range(NCHUNK):
                        g, c, e = n // GROUP, n % GROUP, NCHUNK * hh + n
                        if n == 0:
                            pe.wait_ge(tt_ready, 2 * hh + 2)
                        pe.wait_ge(s_ready, NCHUNK * hh + n + 1)
                        pe.matmul(DB[0][:, 0:P], k_q[:, n, 0, :], state[:, :], start=True, stop=True)\
                            .then_inc(ks_done, 1)
                        if n:
                            pe.wait_ge(o_ready, e)
                        pe.matmul(DB[1][:, 0:P], k_q[:, n, 1, :], state[:, :], start=True, stop=True)\
                            .then_inc(qs_done, 1)
                        fill(2)
                        pe.wait_ge(r4_ready, e + 1)
                        if n and not last:
                            pe.wait_ge(kdec_ready, e + NCHUNK)
                        pe.matmul(DB[2][:, 0:P], tt[g][:, c, :], r4[:, :], start=True, stop=True)\
                            .then_inc(u_done, 1)
                        fill(2)
                        pe.wait_ge(u_ready, e + 1)
                        if n < NCHUNK - 1:
                            pe.matmul(DB[3][:, 0:P], k_dec[g][:, c, :], u_sb[:, :], start=True, stop=True)\
                                .then_inc(ds_done, 1)
                        pe.wait_ge(qs_ready, e + 1)
                        pe.matmul(DB[1][:, 0:P], p_t_m[g][:, c, :], u_sb[:, :], start=True, stop=True)\
                            .then_inc(op_done, 1)
                        if not last:
                            turn_k(h + 1, 1 - j, n, DB[2][:, P:2 * P])
                        fill(2)
                    if not last:
                        pe.wait_ge(o_ready, NCHUNK * (hh + 1))
                        prepare(h + 1, fill)
                        pe.wait_ge(kdec_ready, NCHUNK * (hh + 2))
                    for g in range(2):
                        pe.wait_ge(on_ready, 2 * hh + g + 1)
                        for c in range(GROUP):
                            mm = pe.transpose(DB[2 + g][:, c * P:(c + 1) * P], o_g[g][:, c, :], ident[:, :])
                        mm.then_inc(ot_done, 1)
                    fill(192)
                    pe.wait_ge(o_written, 2 * hh + 2)

                fill = filler(-1, 192, 192 + Z_EARLY)
                pe.wait_ge(tok_done, gdn_slot(l) + 1)
                pe.wait_ge(ba_step, 5 * (gdn_slot(l) + 1))
                prepare(0, fill)
                for n in range(NCHUNK):
                    turn_k(0, 0, n, DB[2 + n // GROUP][:, n % GROUP * P:(n % GROUP + 1) * P])
                fill(192)
                pe.wait_ge(kdec_ready, NCHUNK * (h0 + 1))
                with pe.Fori(0, (HEADS - 2) // 2) as i:
                    for j in range(2):
                        delta(2 * i + j, j, False)
                delta(HEADS - 2, 0, False)
                delta(HEADS - 1, 1, True)

            def cc(l):
                pair0 = TILE0[l] // 2

                def mean(n):
                    pe.wait_ge(cc_done, n + 1)
                    for half in range(2):
                        mm = pe.matmul(DB[half][:, :], ones[:, :], uc[:, n, half * HALF:(half + 1) * HALF],
                                       start=(n == 0), stop=(n == KT - 1), skip_group_check=True)
                    mm.then_inc(mean_done, 1)

                def variance(n):
                    pe.wait_ge(cc_sq_ready, n + 1)
                    for half in range(2):
                        mm = pe.matmul(DB[2 + half][:, :], ones[:, :], cc_sq[:, half * HALF:(half + 1) * HALF],
                                       start=(n == 0), stop=(n == KT - 1), skip_group_check=True)
                    mm.then_inc(var_done, 1)

                for n in range(KT):
                    for j in range(2):
                        tile(pair0 + n, j, in_a, split_at(l, 0, 0) if n + j == 0 else None)
                    if n:
                        mean(n - 1)
                for n in range(KT):
                    tile(pair0 + KT + n // 2, n % 2, in_a)
                    if n == 1:
                        mean(KT - 1)
                    if n > 2:
                        variance(n - 3)
                for n in range(KT - 3, KT):
                    variance(n)

            def swa(l):
                pair0 = TILE0[l] // 2

                def mean_square(e, half):
                    pe.wait_ge(nsq_ready, e + 1)
                    if half or not isinstance(e, int) or e:
                        pe.wait_ge(nln_done, 2 * e + half)
                    pe.matmul(DB[1][:, :], blk[:, :], qs[:, half * HALF:(half + 1) * HALF], start=True, stop=True)\
                        .then_inc(nms_done, 1)

                def heads(n, j, kv, last):
                    sent = [0]

                    def fill(count):
                        if last:
                            return
                        for _ in range(count):
                            s = sent[0]
                            if s == 96:
                                return
                            r, half, k, m = s // 48, s % 48 // 24, s % 24 // 3, s % 3
                            if s % 48 == 0:
                                pe.wait_ge(w_split, 2 * (pair0 + n + 2) + r + 1)
                                pe.wait_ge(pb_free[r], pair0 + n + 2)
                            wl, al = PASSES[m]
                            mm = pe.matmul(PB[r][half][:, :], (w_lo if wl else w_hi)[r][:, k, :],
                                           (a_lo if al else a_hi)[:, k, half * HALF:(half + 1) * HALF],
                                           start=(k == 0 and m == 0), stop=(k == KT - 1 and m == 2),
                                           skip_group_check=True)
                            if s % 48 == 47:
                                mm.then_inc(tile_done, 1)
                            sent[0] += 1

                    def logits(b):
                        e = NB * n + b
                        if b == 0:
                            pe.wait_ge(qn_ready, n + 2)
                        else:
                            pe.wait_ge(lg_ready, e)
                        first = max(b - 1, 0)
                        bank = DB[0][:, :].rearrange("p (h c) -> p h c", h=2)
                        pe.matmul(bank[:, :, WINDOW if b == 0 else 0:2 * WINDOW], q_n[j][:, b * WINDOW:(b + 1) * WINDOW],
                                  k_pad[kv][:, :, first * WINDOW:(b + 1) * WINDOW], start=True, stop=True)\
                            .then_inc(lmm_done, 1)

                    def turn(b):
                        e = NB * n + b
                        pe.wait_ge(pr_ready, e + 1)
                        if b:
                            pe.wait_ge(prt_ready, e)
                        for hh in range(2):
                            for part in range(1 if b == 0 else 0, 2):
                                mm = pe.transpose(DB[2][:, (2 * hh + part) * P:(2 * hh + part + 1) * P],
                                                  lg[b % 2][:, hh, part * WINDOW:(part + 1) * WINDOW], ident[:, :])
                        mm.then_inc(trp_done, 1)

                    def values(b):
                        e = NB * n + b
                        pe.wait_ge(prt_ready, e + 1)
                        if b == 4:
                            pe.wait_ge(att_ready, 2 * n + 1)
                        for hh in range(2):
                            for part in range(1 if b == 0 else 0, 2):
                                mm = pe.matmul(DB[3][HD * hh:HD * hh + HD, (b % 4) * P:(b % 4 + 1) * P],
                                               v_tok[:, b - 1 + part, HD * kv:HD * kv + HD],
                                               pr_t[b % 2][:, hh, part, :], start=(part == 0 or b == 0), stop=(part == 1),
                                               skip_group_check=True)
                        mm.then_inc(pv_done, 1)

                    for b in range(NB + 2):
                        if b < NB:
                            logits(b)
                            fill(4)
                        if 0 < b <= NB:
                            turn(b - 1)
                            fill(4)
                        if b > 1:
                            values(b - 2)
                            fill(4)
                        if not last and b == 6:
                            mean_square(n + 2, 0)
                        if not last and b == 7:
                            mean_square(n + 2, 1)
                    fill(96)

                pe.wait_ge(split_lo, split_at(l, 0, KT))
                for n in range(2):
                    for j in range(2):
                        tile(pair0 + n, j, in_a)
                    if n == 0:
                        for half in range(2):
                            mean_square(0, half)
                for half in range(2):
                    mean_square(1, half)
                pe.wait_ge(pb_free[1], pair0 + 1)
                for b in range(NB):
                    mm = pe.transpose(DB[2 + b // 4][:, (b % 4) * P:(b % 4 + 1) * P], zs[1][:, b * P:(b + 1) * P],
                                      ident[:, :])
                mm.then_inc(v_turned, 1)
                pe.wait_ge(k_spread, 64)
                pe.wait_ge(k_zeros, 1)
                pe.wait_ge(v_ready, 1)
                with pe.Fori(0, 2) as i:
                    for j in range(2):
                        heads(2 * i + j, j, 0, False)
                for n in range(4, KT):
                    heads(n, n % 2, 1, n == KT - 1)

            pe.wait_ge(const_ready, 1)
            pe.matmul(DB[3][0:QH, 0:BIAS_LEN], rel[:, :], onehot[:, :], start=True, stop=True).then_inc(bias_psum, 1)
            for l in range(LAYERS):
                stats(l + 1, ones)
                if MIXER[l] == "gdn":
                    gdn(l)
                elif MIXER[l] == "cc":
                    cc(l)
                else:
                    swa(l)
                out_projection(l)
                embedding(l)

        @block.scalar
        def _(act):
            def halves(t, off=0):
                return [t[:, off + half * HALF:off + (half + 1) * HALF] for half in range(2)]

            def copy_hi(dst, src):
                return nc.scalar.copy(dst, src)

            for name, t in CONSTS.items():
                act.dma_start(t, d[name]).then_inc(const_loaded, 16)
            for k in range(KT):
                act.dma_start(x_sb[:, k, :], d["x_t"][:, k * T:(k + 1) * T]).then_inc(x_tile_loaded[k], 16)

            def squares(l, k):
                if l == 0:
                    act.wait_ge(x_tile_loaded[k], 16)
                else:
                    act.wait_ge(x_new, OUT * (l - 1) + k + 1)
                if k > 1:
                    act.wait_ge(acc_done, 7 * l + k - 1)
                nc.scalar.activation((sqt if k else acc)[:, :], x_sb[:, k, :], ACT.Square).then_inc(sq_done, 1)

            def norm(l):
                act.wait_ge(stat_done, l + 1)
                for half in range(2):
                    nc.scalar.activation(halves(sqt)[half], DB[half][:, :], ACT.Ln,
                                         scale=1.0 / D, bias=eps[:, 0:1]).then_inc(rstd_step, 1)
                act.wait_ge(rstd_step, 3 * l + 2)
                nc.scalar.activation(rstd[:, :], sqt[:, :], ACT.Exp, scale=-0.5).then_inc(rstd_step, 1)
                for k in range(KT):
                    act.wait_ge(hf_done, KT * l + k + 1)
                    copy_hi(a_hi[:, k, :], hf[k % 2][:, :]).then_inc(split_hi, 1)

            def out_projection(l):
                if MIXER[l] == "gdn":
                    for k in range(KT):
                        if k == 0:
                            act.wait_ge(o_written, 2 * HEADS * (gdn_slot(l) + 1))
                        copy_hi(b_hi[:, k, :], o_sb[:, k, :]).then_inc(split_hi, 1)
                if MIXER[l] != "cc":
                    act.wait_ge(split_lo, split_at(l, 1, KT))
                    act.dma_start(flat(x_sb), d["x_t"] if l == 0 else d["x_save"][l - 1]).then_inc(x_reloaded, 16)
                pair0 = (TILE0[l] + LAYER_IN[l]) // 2
                with act.Fori(0, OUT // 2) as i:
                    for j in range(2):
                        act.wait_ge(pb_free[j], pair0 + i + 1)
                        tile_cols = bass.ds((2 * i + j) * T, T)
                        copy_hi(flat(PLACES[MIXER[l]][1][0])[:, tile_cols], x_flat[:, tile_cols]).then_inc(split_hi, 1)

            def embedding(l):
                act.wait_ge(tile_done, TILE0[l] + LAYER_IN[l] + OUT)
                em = PLACES[MIXER[l]][2]
                p_th = em.p_th
                act.dma_start(flat(em.p_raw), d["p_t"][l]).then_inc(p_loaded, 16)
                act.dma_start(em.pw_raw[:, :, :, :].rearrange("p a b c -> p (a b c)"), d["w_embed"][l])\
                    .then_inc(pw_loaded, 16)
                act.wait_ge(p_loaded, 16 * (l + 1))
                copy_hi(flat(em.p_hi), flat(em.p_raw)).then_inc(p_hi_done, 1)
                act.wait_ge(pw_loaded, 16 * (l + 1))
                copy_hi(em.pw_hi[:, :, :, :], em.pw_raw[:, :, :, :]).then_inc(p_hi_done, 1)
                base = TILE0[l] + LAYER_IN[l] + OUT
                for n in range(OUT):
                    act.wait_ge(tile_done, base + n + 1)
                    if n:
                        act.wait_ge(p_t_done, OUT * l + n)
                    for half in range(2):
                        ins = nc.scalar.activation(halves(p_th)[half], PB[n % 2][half][:, :], ACT.Tanh, scale=0.5)
                        if half:
                            ins.then_inc(pb_free[n % 2], 1)
                    if n and l + 1 < LAYERS:
                        squares(l + 1, n - 1)
                    if n and (SPILL[l] or l + 1 == LAYERS):
                        store(l, n - 1)
                if l + 1 < LAYERS:
                    squares(l + 1, OUT - 1)
                if SPILL[l] or l + 1 == LAYERS:
                    store(l, OUT - 1)
                    act.wait_ge(x_stored, 16 * OUT * (1 + sum(SPILL[:l])))

            def store(l, n):
                act.wait_ge(x_new, OUT * l + n + 1)
                to = d["out"] if l + 1 == LAYERS else d["x_save"][l]
                act.dma_start(to[:, n * T:(n + 1) * T], x_sb[:, n, :]).then_inc(x_stored, 16)

            def gdn(l):
                s = gdn_slot(l)
                base, pair0, h0 = TILE0[l], TILE0[l] // 2, HEADS * s
                act.dma_start(flat(wb_raw), d["w_gdn_ba"][s]).then_inc(wb_loaded, 16)
                act.wait_ge(wb_loaded, 16 * (s + 1))
                copy_hi(flat(wb_hi), flat(wb_raw)).then_inc(wb_hi_done, 1)
                def evacuate(h, r, p=0):
                    w = base + 4 * h + r
                    act.wait_ge(tile_done, w + 1)
                    t0 = 3 * (h0 + h) + r
                    if r < 3:
                        if not isinstance(h, int) or t0 > 0:
                            act.wait_ge(conv_done, t0)
                        for half in range(2):
                            ins = copy_hi(halves(c_in, TAPS - 1)[half], PB[r % 2][half][:, :])
                        ins.then_inc(pb_free[r % 2], 1)
                    else:
                        tanh(h, 3)
                        for half in range(2):
                            ins = copy_hi(halves(zb[p])[half], PB[1][half][:, :])
                        ins.then_inc(pb_free[1], 1)

                def tanh(h, r):
                    e = 4 * (h0 + h) + r
                    if not isinstance(h, int) or e:
                        act.wait_ge(silu_done, e)
                    if r < 3:
                        act.wait_ge(conv_done, 3 * (h0 + h) + r + 1)
                        nc.scalar.activation(th[:, :], c_acc[:, :], ACT.Tanh, scale=0.5).then_inc(th_done, 1)
                    else:
                        for half in range(2):
                            ins = nc.scalar.activation(halves(th)[half], PB[1][half][:, :], ACT.Tanh, scale=0.5)
                        ins.then_inc(th_done, 1)

                def k_chunk(h, p, n, kt, turned):
                    e = NCHUNK * (h0 + h) + n
                    if n == 0:
                        act.wait_ge(hv_ready, h0 + h + 1)
                    act.wait_ge(kt_done, e + turned)
                    nc.scalar.activation(kt_sq[:, :], kt, ACT.Square, accum_out=ssk[:, n:n + 1]).then_inc(ssk_done, 1)
                    nc.scalar.activation(k_dec[n // GROUP][:, n % GROUP, :], kt, ACT.Copy,
                                         scale=hv[p][:, EDEC, n:n + 1]).then_inc(kdec_ready, 1)
                    act.wait_ge(kdec_ready, e + 1)

                def decay(h, j):
                    for g in range(2):
                        act.wait_ge(arg_ready, 2 * (h0 + h) + g + 1)
                        for c in range(GROUP):
                            n = GROUP * g + c
                            ins = nc.scalar.activation(dt_m[g][:, c, :], arg[g][:, c, :], ACT.Exp,
                                                       bias=hv[j][:, NGC, n:n + 1])
                        ins.then_inc(dt_ready, 1)

                def delta(h, j, last):
                    hh = h0 + h
                    v = hv[j]
                    for g in range(2):
                        act.wait_ge(nt_ready, 2 * hh + g + 1)
                        copy_hi(flat(nt_r[g]), flat(nt[g])).then_inc(ntr_ready, 1)
                    for g in range(2):
                        act.wait_ge(tr_done, 2 * hh + g + 1)
                        for c in range(GROUP):
                            n = GROUP * g + c
                            nc.scalar.activation(kt_sq[:, :], DB[2 * g][:, c * P:(c + 1) * P], ACT.Square,
                                                 accum_out=ssq[:, n:n + 1]).then_inc(ssq_done, 1)
                            act.wait_ge(ssq_done, NCHUNK * hh + n + 1)
                    evacuate(h, 3, j)
                    for lv in range(LEVELS):
                        for g in range(2):
                            act.wait_ge(m_done, 2 * (LEVELS * hh + lv) + g + 1)
                            copy_hi(flat(mt_m[g]), DB[2 * g + 1][:, :]).then_inc(mt_ready, 1)
                        if not last:
                            if lv == 3:
                                evacuate(h + 1, 0)
                            if lv == 5:
                                tanh(h + 1, 0)
                    if not last:
                        evacuate(h + 1, 1)
                    for n in range(NCHUNK):
                        e = NCHUNK * hh + n
                        act.wait_ge(qs_done, e + 1)
                        if n:
                            act.wait_ge(o_ready, e)
                        nc.scalar.activation(qs_sb[:, :], DB[1][:, 0:P], ACT.Copy, scale=v[:, EG, n:n + 1])\
                            .then_inc(qs_ready, 1)
                        act.wait_ge(u_done, e + 1)
                        if n:
                            act.wait_ge(op_done, e)
                        nc.scalar.activation(u_sb[:, :], DB[2][:, 0:P], ACT.Copy, scale=c_tok[:, n:n + 1])\
                            .then_inc(u_ready, 1)
                        if not last:
                            if n == 2:
                                tanh(h + 1, 1)
                            if n == 5:
                                evacuate(h + 1, 2)
                            k_chunk(h + 1, 1 - j, n, DB[2][:, P:2 * P], 1)
                        if n % GROUP == GROUP - 1:
                            g = n // GROUP
                            act.wait_ge(o_ready, e + 1)
                            for c in range(GROUP):
                                nc.scalar.activation(sq_o[:, :], o_g[g][:, c, :], ACT.Square,
                                                     accum_out=oss[:, GROUP * g + c:GROUP * g + c + 1])\
                                    .then_inc(oss_ready, 1)
                                act.wait_ge(oss_ready, NCHUNK * hh + GROUP * g + c + 1)
                    if not last:
                        decay(h + 1, 1 - j)
                        tanh(h + 1, 2)

                evacuate(0, 0)
                act.wait_ge(ba_rows_done, s + 1)
                for half in range(2):
                    ins = copy_hi(ba_rows[:, half * HALF:(half + 1) * HALF], DB[half][0:2 * HEADS, :])
                ins.then_inc(ba_rows_ready, 1)
                tanh(0, 0)
                evacuate(0, 1)
                bb = DB[2][:, 0:2 * 64].rearrange("p (c k) -> p k c", k=16)
                ch = Chain(act, ba_act, 5 * s)
                act.wait_ge(ba_done, s + 1)
                ch.link(nc.scalar.activation(g_t[0][:, :, :], bb[:, 0:HEADS, :], ACT.Tanh, scale=0.5))
                act.wait_ge(ba_step, 5 * s + 2)
                ch.link(nc.scalar.activation(flat(g_t[2]), flat(g_t[1]), ACT.Exp, scale=-1.0))
                ch.link(nc.scalar.activation(flat(g_t[3]), flat(g_t[2]), ACT.Ln, bias=1.0))
                ch.link(nc.scalar.activation(flat(g_t[4]), a_log[:, s, :, :].rearrange("p a b -> p (a b)"), ACT.Exp))
                tanh(0, 1)
                evacuate(0, 2)
                act.wait_ge(gcum_done, s + 1)
                gc = DB[3][:, 0:64].rearrange("p (h c) -> p h c", h=HEADS)
                gl = DB[3][:, 64:128].rearrange("p (h c) -> p h c", h=HEADS)
                nc.scalar.activation(tok[:, :, NGC, :], gc, ACT.Copy, scale=-1.0)
                nc.scalar.activation(tok[:, :, EG, :], gc, ACT.Exp)
                nc.scalar.activation(tok[:, :, EGL, :], gl, ACT.Exp)
                ch.link(nc.scalar.activation(g_t[1][:, :, :], gl, ACT.Copy))
                ch.end(5)
                act.wait_ge(ba_step, 5 * s + 4)
                nc.scalar.activation(tok[:, :, EDEC, :], g_t[2][:, :, :], ACT.Exp).then_inc(tok_done, 1)
                for n in range(NCHUNK):
                    c = n % GROUP
                    k_chunk(0, 0, n, DB[2 + n // GROUP][:, c * P:(c + 1) * P], GROUP - c)
                decay(0, 0)
                tanh(0, 2)
                with act.Fori(0, (HEADS - 2) // 2) as i:
                    for j in range(2):
                        delta(2 * i + j, j, False)
                delta(HEADS - 2, 0, False)
                delta(HEADS - 1, 1, True)

            def cc(l):
                base = TILE0[l]
                for n in range(KT):
                    act.wait_ge(tile_done, base + 2 * n + 2)
                    if n:
                        act.wait_ge(cc_u_ready, n)
                    for half in range(2):
                        ins = nc.scalar.activation(halves(cc_th)[half], PB[1][half][:, :], ACT.Tanh, scale=0.5)
                    ins.then_inc(pb_free[1], 1)

                def gate(n):
                    act.wait_ge(tile_done, base + 2 * KT + n + 1)
                    for half in range(2):
                        ins = nc.scalar.activation(cc_gate[:, n, half * HALF:(half + 1) * HALF], PB[n % 2][half][:, :],
                                                   ACT.Silu)
                    ins.then_inc(pb_free[n % 2], 1)

                def square(n):
                    act.wait_ge(centred, n + 1)
                    if n:
                        act.wait_ge(var_done, n)
                    nc.scalar.activation(cc_sq[:, :], uc[:, n, :], ACT.Square).then_inc(cc_sq_ready, 1)

                for n in range(2):
                    gate(n)
                act.wait_ge(mean_done, KT)
                for half in range(2):
                    ins = nc.scalar.activation(halves(mu)[half], DB[half][:, :], ACT.Copy, scale=1.0 / D)
                ins.then_inc(mu_ready, 1)
                for n in range(2, KT):
                    square(n - 2)
                    gate(n)
                square(KT - 2)
                square(KT - 1)
                act.wait_ge(var_done, KT)
                for half in range(2):
                    nc.scalar.activation(halves(cc_sq)[half], DB[2 + half][:, :], ACT.Ln, scale=1.0 / D,
                                         bias=ln_eps[:, 0:1]).then_inc(cc_rstd_step, 1)
                act.wait_ge(cc_rstd_step, 2)
                nc.scalar.activation(cc_rstd[:, :], cc_sq[:, :], ACT.Exp, scale=-0.5).then_inc(cc_rstd_step, 1)

                def high(k):
                    act.wait_ge(gated_u, k + 1)
                    copy_hi(a_hi[:, k, :], uc[:, k, :]).then_inc(split_hi, 1)

                for k in range(KT):
                    act.wait_ge(scaled_u, k + 1)
                    nc.scalar.activation(uc[:, k, :], uc[:, k, :], ACT.Silu, bias=cc_par[:, LN_B, k:k + 1],
                                         scale=cc_par[:, LN_G, k:k + 1]).then_inc(silu_u, 1)
                    if k:
                        high(k - 1)
                high(KT - 1)

            def swa(l):
                base = TILE0[l]

                def raw_and_square(e, w, dst):
                    act.wait_ge(tile_done, w + 1)
                    if not isinstance(e, int) or e:
                        act.wait_ge(qn_ready, e)
                    for half in range(2):
                        ins = copy_hi(halves(dst)[half], PB[0][half][:, :])
                    ins.then_inc(pb_free[0], 1)
                    for half in range(2):
                        ins = nc.scalar.activation(halves(qs)[half], PB[0][half][:, :], ACT.Square)
                    ins.then_inc(nsq_ready, 1)

                def log_mean(e, half):
                    act.wait_ge(nms_done, 2 * e + half + 1)
                    nc.scalar.activation(halves(qs)[half], DB[1][:, :], ACT.Ln, bias=eps[:, 0:1]).then_inc(nln_done, 1)
                    if half:
                        act.wait_ge(nln_done, 2 * e + 2)
                        nc.scalar.activation(qs[:, :], qs[:, :], ACT.Exp, scale=-0.5).then_inc(nrr_ready, 1)

                def gate_tanh(n, w, p):
                    act.wait_ge(tile_done, w + 1)
                    for half in range(2):
                        ins = nc.scalar.activation(halves(zs[p])[half], PB[1][half][:, :], ACT.Tanh, scale=0.5)
                    ins.then_inc(gth_done, 1)

                def load_bias(n, p):
                    act.dma_start(bias[:, p, :, :],
                                  bias_window(n)).then_inc(bias_loaded[p], 16)

                def exps(n, b):
                    e, s = NB * n + b, sm[b % 2]
                    keys = slice(WINDOW if b == 0 else 0, 2 * WINDOW)
                    act.wait_ge(mx_ready, e + 1)
                    nc.scalar.activation(s[:, ESK, :], s[:, SK, :], ACT.Exp).then_inc(esk_ready, 1)
                    for hh in range(2):
                        ins = nc.scalar.activation(lg[b % 2][:, hh, keys], lg[b % 2][:, hh, keys], ACT.Exp,
                                                   bias=s[:, NEG_M, hh:hh + 1], accum_out=s[:, ES, hh:hh + 1])
                        ins.then_inc(e_ready, 1)

                def turned(n, b):
                    act.wait_ge(trp_done, NB * n + b + 1)
                    if b > 1:
                        act.wait_ge(pv_done, NB * n + b - 1)
                    bank = DB[2][:, :].rearrange("p (h a i) -> p h a i", h=2, a=2)
                    part = slice(1 if b == 0 else 0, 2)
                    copy_hi(pr_t[b % 2][:, :, part, :], bank[:, :, part, :]).then_inc(prt_ready, 1)

                def high(n, m, p):
                    act.wait_ge(att_ready, 2 * n + m + 1)
                    cols = bass.ds(n * T + m * HALF, HALF)
                    copy_hi(b_hi_flat[:, cols], halves(zs[p])[m]).then_inc(split_hi if m else half_hi, 1)

                def heads(n, j, last):
                    for b in range(NB):
                        exps(n, b)
                        if b:
                            turned(n, b - 1)
                        if b == 6:
                            high(n, 0, j)
                        if not last:
                            if b == 5:
                                raw_and_square(n + 2, base + 2 * (n + 2), q_n[1 - j])
                            if b == 6:
                                log_mean(n + 2, 0)
                            if b == 7:
                                log_mean(n + 2, 1)
                    turned(n, NB - 1)
                    high(n, 1, j)
                    if not last:
                        gate_tanh(n + 1, base + 2 * (n + 2) + 1, 1 - j)

                act.wait_ge(bias_spread, 16)
                act.wait_ge(split_lo, split_at(l, 0, KT))
                load_bias(0, 0)
                load_bias(1, 1)
                raw_and_square(0, base, q_n[1])
                act.wait_ge(tile_done, base + 2)
                for half in range(2):
                    ins = copy_hi(halves(zs[1])[half], PB[1][half][:, :])
                ins.then_inc(pb_free[1], 1)
                for half in range(2):
                    log_mean(0, half)
                act.wait_ge(qn_ready, 1)
                for kv in range(2):
                    for hh in range(2):
                        act.dma_start(k_pad[kv][HD * hh:HD * hh + HD, hh, :], q_n[1][HD * kv:HD * kv + HD, :])\
                            .then_inc(k_spread, 16)
                raw_and_square(1, base + 2, q_n[0])
                for half in range(2):
                    log_mean(1, half)
                act.wait_ge(v_turned, 1)
                for m in range(2):
                    ins = copy_hi(v_tok[:, 4 * m:4 * m + 4, :], DB[2 + m][:, :].rearrange("p (b i) -> p b i", b=4))
                ins.then_inc(v_ready, 1)
                gate_tanh(0, base + 3, 0)
                act.wait_ge(k_spread, 64)
                with act.Fori(0, 3) as i:
                    for j in range(2):
                        heads(2 * i + j, j, False)
                        act.wait_ge(lg_ready, NB * (2 * i + j + 1))
                        load_bias(2 * i + j + 2, j)
                heads(KT - 2, 0, False)
                heads(KT - 1, 1, True)

            def bias_window(n):
                return d["bias_window"][:, bass.ds(2 * n, 2), :]

            act.wait_ge(bias_sum, 1)
            act.dma_start(d["bias_rows"], bias_rows[:, :]).then_inc(bias_stored, 16)
            act.wait_ge(bias_stored, 16)
            act.dma_start(d["bias_copies"], d["bias_rows"].unsqueeze(1).to_broadcast([QH, P, BIAS_LEN]))\
                .then_inc(bias_spread, 16)
            for k in range(KT):
                squares(0, k)
            for l in range(LAYERS):
                norm(l)
                if MIXER[l] == "gdn":
                    gdn(l)
                elif MIXER[l] == "cc":
                    cc(l)
                else:
                    swa(l)
                out_projection(l)
                embedding(l)

        @block.vector
        def _(dve):
            def halves(t, off=0):
                return [t[:, off + half * HALF:off + (half + 1) * HALF] for half in range(2)]

            dve.wait_ge(const_loaded, 16 * len(CONSTS))
            nc.vector.memset(half_e[:, :], 0.5)
            nc.vector.memset(mhalf_e[:, :], -0.5)
            nc.vector.memset(eps[:, :], RMS_EPS)
            nc.vector.memset(ln_eps[:, :], LN_EPS)
            nc.vector.tensor_copy(level_mask[:, :, :], mask_stage[:, 0:LEVELS, :])
            nc.vector.tensor_copy(strict[:, :], mask_stage[:, LEVELS, :])
            nc.vector.tensor_scalar(cc_w[:, :, :], cc_w[:, :, :], 0.5, None, ALU.mult)
            nc.vector.tensor_scalar(gdn_gh[:, :, :], gdn_g[:, :, :], 0.5, None, ALU.mult)
            nc.vector.tensor_copy(ident_r[:, :], ident[:, :]).then_inc(const_ready, 1)

            def accumulate(l, k):
                if k == 0:
                    return
                dve.wait_ge(sq_done, KT * l + k + 1)
                if k > 1:
                    dve.wait_ge(acc_done, 7 * l + k - 1)
                nc.vector.tensor_tensor(acc[:, :], acc[:, :], sqt[:, :], ALU.add).then_inc(acc_done, 1)

            def norm(l):
                def scaled(k):
                    if k > 1:
                        dve.wait_ge(split_lo, split_at(l, 0, k - 1))
                    nc.vector.scalar_tensor_tensor(hf[k % 2][:, :], x_sb[:, k, :], norm_g[:, l, k:k + 1],
                                                   rstd[:, :], ALU.mult, ALU.mult).then_inc(hf_done, 1)

                dve.wait_ge(rstd_step, 3 * (l + 1))
                scaled(0)
                for k in range(KT):
                    if k + 1 < KT:
                        scaled(k + 1)
                    dve.wait_ge(hf_done, KT * l + k + 1)
                    dve.wait_ge(split_hi, split_at(l, 0, k) + 1)
                    nc.vector.tensor_tensor(a_lo[:, k, :], hf[k % 2][:, :], a_hi[:, k, :].bitcast(F32),
                                            ALU.subtract).then_inc(split_lo, 1)

            def out_projection(l):
                pair0 = (TILE0[l] + LAYER_IN[l]) // 2
                if MIXER[l] == "gdn":
                    for k in range(KT):
                        dve.wait_ge(split_hi, split_at(l, 1, k) + 1)
                        nc.vector.tensor_tensor(b_lo[:, k, :], o_sb[:, k, :], b_hi[:, k, :].bitcast(F32),
                                                ALU.subtract).then_inc(split_lo, 1)
                if MIXER[l] != "cc":
                    dve.wait_ge(x_reloaded, 16 * sum(m != "cc" for m in MIXER[:l + 1]))
                with dve.Fori(0, OUT // 2) as i:
                    for j in range(2):
                        dve.wait_ge(tile_done, 2 * (pair0 + i) + j + 1)
                        for half in range(2):
                            cols = bass.ds((2 * i + j) * T + half * HALF, HALF)
                            ins = nc.vector.tensor_tensor(x_flat[:, cols], x_flat[:, cols], PB[j][half][:, :],
                                                          ALU.add)
                        ins.then_inc(pb_free[j], 1)
                        dve.wait_ge(split_hi, split_at(l, 2, 2 * i + j) + 1)
                        cols = bass.ds((2 * i + j) * T, T)
                        hi, lo = (flat(t) for t in PLACES[MIXER[l]][1])
                        nc.vector.tensor_tensor(lo[:, cols], x_flat[:, cols], hi[:, cols].bitcast(F32),
                                                ALU.subtract).then_inc(split_lo, 1)

            def embedding(l):
                dve.wait_ge(p_hi_done, 2 * l + 1)
                em = PLACES[MIXER[l]][2]
                p_th, p_t = em.p_th, em.p_t
                nc.vector.tensor_tensor(flat(em.p_lo), flat(em.p_raw), flat(em.p_hi).bitcast(F32),
                                        ALU.subtract).then_inc(p_split, 1)
                dve.wait_ge(p_hi_done, 2 * l + 2)
                nc.vector.tensor_tensor(flat4(em.pw_lo), flat4(em.pw_raw), flat4(em.pw_hi).bitcast(F32),
                                        ALU.subtract).then_inc(p_split, 1)
                pair0 = (TILE0[l] + LAYER_IN[l] + OUT) // 2
                for n in range(OUT):
                    dve.wait_ge(pb_free[n % 2], pair0 + n // 2 + 1)
                    dve.wait_ge(pp_done, OUT * l + n + 1)
                    if n:
                        dve.wait_ge(x_new, OUT * l + n)
                    for half in range(2):
                        cols = slice(half * HALF, (half + 1) * HALF)
                        ins = nc.vector.scalar_tensor_tensor(p_t[:, cols], p_th[:, cols], 1.0,
                                                             DB[2 * (n % 2) + half][:, :], ALU.add, ALU.mult)
                    ins.then_inc(p_t_done, 1)
                    dve.wait_ge(p_t_done, OUT * l + n + 1)
                    nc.vector.scalar_tensor_tensor(x_sb[:, n, :], p_t[:, :], 0.5, x_sb[:, n, :], ALU.mult,
                                                   ALU.add).then_inc(x_new, 1)
                    if n and l + 1 < LAYERS:
                        accumulate(l + 1, n - 1)
                if l + 1 < LAYERS:
                    accumulate(l + 1, OUT - 1)

            def gdn(l):
                s = gdn_slot(l)
                pair0, h0 = TILE0[l] // 2, HEADS * s
                dve.wait_ge(wb_hi_done, s + 1)
                nc.vector.tensor_tensor(flat(wb_lo), flat(wb_raw), flat(wb_hi).bitcast(F32),
                                        ALU.subtract).then_inc(wb_split, 1)
                def conv(h, r, q, p):
                    hh = h0 + h
                    out = [kq[p][:, :, 0, :], kq[p][:, :, 1, :], vb[p][:, :], zb[p][:, :]][r]
                    if q == 4:
                        dve.wait_ge(th_done, 4 * hh + r + 1)
                        if r == 3:
                            dve.wait_ge(pb_free[1], pair0 + 2 * h + 2)
                            nc.vector.scalar_tensor_tensor(out, th[:, :], 1.0, zb[p][:, :], ALU.add,
                                                           ALU.mult).then_inc(silu_done, 1)
                            return
                        a, b = th[:, :], c_acc[:, :]
                        if r < 2:
                            a, b = (t.rearrange("p (n c) -> p n c", c=CHUNK) for t in (a, b))
                        nc.vector.scalar_tensor_tensor(out, a, 1.0, b, ALU.add, ALU.mult).then_inc(silu_done, 1)
                        return
                    if q == 0:
                        if r == 0:
                            nc.vector.tensor_copy(cw[:, :, :].rearrange("p a b -> p (a b)"),
                                                  conv_flat[:, bass.ds((h0 + h) * 3 * TAPS, 3 * TAPS)])\
                                .then_inc(cw_ready, 1)
                            dve.wait_ge(cw_ready, hh + 1)
                        dve.wait_ge(pb_free[r % 2], pair0 + 2 * h + r // 2 + 1)
                        if r or not isinstance(hh, int) or hh:
                            dve.wait_ge(silu_done, 4 * hh + r)
                        nc.vector.tensor_scalar(c_acc[:, :], c_in[:, TAPS - 1:TAPS - 1 + T],
                                                cw[:, r, TAPS - 1:TAPS], None, ALU.mult).then_inc(conv_step, 1)
                        return
                    t = TAPS - 1 - q
                    dve.wait_ge(conv_step, 9 * hh + 3 * r + q)
                    nc.vector.scalar_tensor_tensor(c_acc[:, :], c_in[:, t:t + T], cw[:, r, t:t + 1], c_acc[:, :],
                                                   ALU.mult, ALU.add)\
                        .then_inc(conv_done if q == TAPS - 1 else conv_step, 1)

                def token_values(h, p):
                    nc.vector.tensor_copy(flat(hv[p]), tok_flat[:, bass.ds(h * KINDS * NCHUNK, KINDS * NCHUNK)])\
                        .then_inc(hv_ready, 1)

                def log_decays(h, p):
                    hh, v = h0 + h, hv[p]
                    dve.wait_ge(hv_ready, hh + 1)
                    for g in range(2):
                        nc.vector.tensor_tensor(u_g[g][:, :, :], cum_u[:, :].unsqueeze(1).to_broadcast([P, GROUP, P]),
                                                v[:, GG, GROUP * g:GROUP * g + GROUP].unsqueeze(2)
                                                .to_broadcast([P, GROUP, P]), ALU.mult).then_inc(ug_ready, 1)

                def rows(h, g):
                    dve.wait_ge(rowg_done, 2 * (h0 + h) + g + 1)
                    nc.vector.tensor_tensor(arg[g][:, :, :], DB[g][:, :].rearrange("p (c i) -> p c i", c=GROUP),
                                            mask_t[:, :].unsqueeze(1).to_broadcast([P, GROUP, P]), ALU.add)\
                        .then_inc(arg_ready, 1)

                def norms(h, p):
                    hh = h0 + h
                    dve.wait_ge(ssk_done, NCHUNK * (hh + 1))
                    nc.vector.tensor_scalar(ssk[:, :], ssk[:, :], 4 * RMS_EPS, None, ALU.add).then_inc(ss_read, 1)
                    dve.wait_ge(ss_read, hh + 1)
                    ch = Chain(dve, dve_step, 2 * hh)
                    ch.link(nc.vector.reciprocal(c_tok[:, :], ssk[:, :]))
                    ch.link(nc.vector.tensor_tensor(c_tok[:, :], c_tok[:, :], hv[p][:, BETA, :], ALU.mult))
                    ch.end(2)

                def delta(h, j, last):
                    hh, v, nj = h0 + h, hv[j], 1 - j

                    def conv_next(*steps):
                        if not last:
                            for r, q in steps:
                                conv(h + 1, r, q, nj)

                    for g in range(2):
                        dve.wait_ge(gram_done, 2 * hh + g + 1)
                        dve.wait_ge(dt_ready, 2 * hh + g + 1)
                        for b in range(2):
                            qk = DB[2 * g + b][:, :].rearrange("p (c m i) -> p c m i", c=2, m=2)[:, :, 1, :]
                            nc.vector.tensor_tensor(p_t_m[g][:, 2 * b:2 * b + 2, :], qk, dt_m[g][:, 2 * b:2 * b + 2, :],
                                                    ALU.mult)
                        dve.wait_ge(dts_ready, 2 * hh + g + 1)
                        for c in range(GROUP):
                            ins = nc.vector.scalar_tensor_tensor(
                                nt[g][:, c, :], DB[2 * g + c // 2][:, (c % 2) * 256:(c % 2) * 256 + P],
                                c_tok[:, GROUP * g + c:GROUP * g + c + 1], dts[g][:, c, :], ALU.mult, ALU.mult)
                        ins.then_inc(nt_ready, 1)
                    dve.wait_ge(sqrt_done, hh + 1)
                    for g in range(2):
                        dve.wait_ge(tr_done, 2 * hh + g + 1)
                        nc.vector.scalar_tensor_tensor(
                            r_v[g][:, :, :], DB[2 * g + 1][:, :].rearrange("p (c i) -> p c i", c=GROUP), 0.5,
                            sq_tk[:, GROUP * g:GROUP * g + GROUP].unsqueeze(2).to_broadcast([P, GROUP, P]),
                            ALU.mult, ALU.mult).then_inc(rv_ready, 1)
                    for lv in range(LEVELS):
                        fillers = {4: [(0, 0), (0, 1)], 5: [(0, 2), (0, 3)], 6: [(0, 4)]}.get(lv, [])
                        for g in range(2):
                            e = 2 * (LEVELS * hh + lv) + g
                            dve.wait_ge(pm_done, e + 1)
                            nc.vector.tensor_tensor(p_m[g][:, :, :], DB[2 * g][:, :].rearrange("p (c i) -> p c i", c=GROUP),
                                                    level_mask[:, lv, :].unsqueeze(1).to_broadcast([P, GROUP, P]),
                                                    ALU.mult).then_inc(p_ready, 1)
                        conv_next(*fillers)
                        if lv == 1:
                            conv(h, 3, 4, j)
                            dve.wait_ge(ssq_done, NCHUNK * (hh + 1))
                            nc.vector.tensor_scalar(tq[:, :], ssq[:, :], RMS_EPS * CHUNK, 4 * RMS_EPS * RMS_EPS * CHUNK,
                                                    ALU.mult, ALU.add).then_inc(tq_ready, 1)
                            dve.wait_ge(tq_ready, hh + 1)
                        if lv == LEVELS - 1 and not last:
                            token_values(h + 1, nj)
                        for g in range(2):
                            e = 2 * (LEVELS * hh + lv) + g
                            if lv == 0:
                                dve.wait_ge(p_ready, e + 1)
                                nc.vector.tensor_tensor(m_m[g][:, :, :], p_m[g][:, :, :].bitcast(F32),
                                                        ident[:, :].unsqueeze(1).to_broadcast([P, GROUP, P]),
                                                        ALU.add).then_inc(m_ready, 1)
                            else:
                                dve.wait_ge(m_done, e + 1)
                                nc.vector.tensor_tensor(flat(m_m[g]), flat(m_m[g]).bitcast(F32), DB[2 * g][:, :],
                                                        ALU.add).then_inc(m_ready, 1)
                    conv_next((1, 0), (1, 1))
                    for g in range(2):
                        dve.wait_ge(m_ready, 2 * (LEVELS * hh + LEVELS - 1) + g + 1)
                        dve.wait_ge(y_done, 2 * hh + g + 1)
                        nc.vector.scalar_tensor_tensor(flat(y_m[g]), DB[2 * g][:, :], -1.0, flat(m_m[g]).bitcast(F32),
                                                       ALU.mult, ALU.subtract).then_inc(y_ready, 1)
                    for g in range(2):
                        dve.wait_ge(t_done, 2 * hh + g + 1)
                        nc.vector.scalar_tensor_tensor(flat(tt[g]), flat(mt_m[g]).bitcast(F32), 2.0, DB[2 * g + 1][:, :],
                                                       ALU.mult, ALU.add).then_inc(tt_ready, 1)
                    nc.vector.memset(state[:, :], 0.0).then_inc(s_ready, 1)
                    for n in range(NCHUNK):
                        g, c, e = n // GROUP, n % GROUP, NCHUNK * hh + n
                        dve.wait_ge(ks_done, e + 1)
                        nc.vector.scalar_tensor_tensor(r4[:, :], DB[0][:, 0:P], v[:, NEG_EG, n:n + 1], r_v[g][:, c, :],
                                                       ALU.mult, ALU.add).then_inc(r4_ready, 1)
                        conv_next(*{0: [(1, 2)], 1: [(1, 3)], 3: [(1, 4)], 6: [(2, 0)], 7: [(2, 1)]}.get(n, []))
                        if n == 2 and not last:
                            log_decays(h + 1, nj)
                        if n < NCHUNK - 1:
                            dve.wait_ge(ds_done, (NCHUNK - 1) * hh + n + 1)
                            dve.wait_ge(s_ready, e + 1)
                            nc.vector.scalar_tensor_tensor(state[:, :], state[:, :], v[:, EGL, n:n + 1], DB[3][:, 0:P],
                                                           ALU.mult, ALU.add).then_inc(s_ready, 1)
                        dve.wait_ge(op_done, e + 1)
                        nc.vector.tensor_tensor(o_g[g][:, c, :], DB[1][:, 0:P], qs_sb[:, :], ALU.add)\
                            .then_inc(o_ready, 1)
                        if n == 7 and not last:
                            rows(h + 1, 0)
                        if n == 4 or n == 7:
                            m = slice(4 * (n // 4 if n == 7 else 0), 4 * (n // 4 if n == 7 else 0) + 4)
                            dve.wait_ge(oss_ready, NCHUNK * hh + m.stop)
                            nc.vector.scalar_tensor_tensor(om[:, m], oss[:, m], 1.0 / P, tq[:, m], ALU.mult,
                                                           ALU.add).then_inc(om_ready, 1)
                    if not last:
                        rows(h + 1, 1)
                        norms(h + 1, nj)
                    conv_next((2, 2))
                    for g in range(2):
                        dve.wait_ge(osc_ready, 2 * hh + g + 1)
                        dve.wait_ge(o_ready, NCHUNK * hh + GROUP * (g + 1))
                        nc.vector.tensor_tensor(o_g[g][:, :, :], o_g[g][:, :, :],
                                                osc[:, GROUP * g:GROUP * g + GROUP].unsqueeze(2)
                                                .to_broadcast([P, GROUP, P]), ALU.mult).then_inc(on_ready, 1)
                    conv_next((2, 3))
                    for g in range(2):
                        dve.wait_ge(ot_done, 2 * hh + g + 1)
                        nc.vector.scalar_tensor_tensor(o_flat[:, bass.ds(h * T + g * HALF, HALF)], DB[2 + g][:, :],
                                                       gdn_gh[:, s, :], zb[j][:, g * HALF:(g + 1) * HALF],
                                                       ALU.mult, ALU.mult).then_inc(o_written, 1)
                    conv_next((2, 4))

                nc.vector.memset(c_in[:, 0:TAPS - 1], 0.0).then_inc(pad_ready, 1)
                dve.wait_ge(pad_ready, s + 1)
                for q in range(5):
                    conv(0, 0, q, 0)
                for q in range(4):
                    conv(0, 1, q, 0)
                aa = DB[2][:, 0:2 * 64].rearrange("p (c k) -> p k c", k=16)[:, HEADS:2 * HEADS, :]
                ch = Chain(dve, ba_step, 5 * s)
                dve.wait_ge(ba_act, 5 * s + 1)
                ch.link(nc.vector.tensor_tensor(g_t[5][:, :, :], aa, dt_b[:, s, :, :], ALU.add))
                ch.link(nc.vector.scalar_tensor_tensor(flat(g_t[1]), flat(g_t[5]), -1.0, flat(g_t[5]), ALU.mult,
                                                       ALU.max))
                dve.wait_ge(ba_act, 5 * s + 4)
                ch.link(nc.vector.scalar_tensor_tensor(flat(g_t[1]), flat(g_t[5]), 0.0, flat(g_t[3]), ALU.max,
                                                       ALU.add))
                nc.vector.scalar_tensor_tensor(flat(g_t[5]), flat(g_t[1]), -1.0, flat(g_t[4]), ALU.mult,
                                               ALU.mult).then_inc(g_ready, 1)
                nc.vector.tensor_scalar(tok[:, :, BETA, :], g_t[0][:, :, :], 0.5, 0.5, ALU.mult, ALU.add)
                dve.wait_ge(g_ready, s + 1)
                nc.vector.tensor_copy(tok[:, :, GG, :], g_t[5][:, :, :])
                conv(0, 1, 4, 0)
                for q in range(4):
                    conv(0, 2, q, 0)
                dve.wait_ge(ba_act, 5 * s + 5)
                gc = DB[3][:, 0:64].rearrange("p (h c) -> p h c", h=HEADS)
                ch.link(nc.vector.tensor_tensor(g_t[2][:, :, :], g_t[1][:, :, :], gc, ALU.subtract))
                ch.link(nc.vector.tensor_scalar(tok[:, :, NEG_EG, :], tok[:, :, EG, :], -1.0, None, ALU.mult))
                ch.end(5)
                dve.wait_ge(tok_done, s + 1)
                token_values(0, 0)
                log_decays(0, 0)
                rows(0, 0)
                rows(0, 1)
                norms(0, 0)
                conv(0, 2, 4, 0)
                with dve.Fori(0, (HEADS - 2) // 2) as i:
                    for j in range(2):
                        delta(2 * i + j, j, False)
                delta(HEADS - 2, 0, False)
                delta(HEADS - 1, 1, True)

            def cc(l):
                pair0 = TILE0[l] // 2
                for j in range(2):
                    ins = nc.vector.memset(u_in[j][:, 0:PAD], 0.0)
                ins.then_inc(cc_pad, 1)
                dve.wait_ge(cc_pad, 1)
                for n in range(KT):
                    u = u_in[n % 2]
                    dve.wait_ge(tile_done, 2 * (pair0 + n) + 1)
                    dve.wait_ge(pb_free[1], pair0 + n + 1)
                    if n > 1:
                        dve.wait_ge(cc_done, n - 1)
                    for half in range(2):
                        cols = slice(half * HALF, (half + 1) * HALF)
                        ins = nc.vector.scalar_tensor_tensor(u[:, PAD + half * HALF:PAD + (half + 1) * HALF],
                                                             cc_th[:, cols], 1.0, PB[0][half][:, :], ALU.add, ALU.mult)
                    ins.then_inc(pb_free[0], 1)
                    dve.wait_ge(pb_free[0], pair0 + n + 1)
                    t = CC_TAPS - 1
                    nc.vector.tensor_scalar(uc[:, n, :], u[:, t:t + T], cc_w[:, n, t:t + 1],
                                            cc_par[:, CC_B, n:n + 1], ALU.mult, ALU.add).then_inc(cc_u_ready, 1)
                    dve.wait_ge(cc_u_ready, n + 1)
                    for t in range(CC_TAPS - 2, -1, -1):
                        ins = nc.vector.scalar_tensor_tensor(uc[:, n, :], u[:, t:t + T], cc_w[:, n, t:t + 1],
                                                             uc[:, n, :], ALU.mult, ALU.add)
                        if t:
                            ins.then_inc(tap, 1)
                            dve.wait_ge(tap, (CC_TAPS - 2) * n + CC_TAPS - 1 - t)
                        else:
                            ins.then_inc(cc_done, 1)
                dve.wait_ge(mu_ready, 1)
                for n in range(KT):
                    nc.vector.tensor_tensor(uc[:, n, :], uc[:, n, :], mu[:, :], ALU.subtract).then_inc(centred, 1)
                dve.wait_ge(cc_rstd_step, 3)
                dve.wait_ge(tile_done, TILE0[l] + LAYER_IN[l])

                def scale(k):
                    dve.wait_ge(centred, k + 1)
                    nc.vector.tensor_tensor(uc[:, k, :], uc[:, k, :], cc_rstd[:, :], ALU.mult).then_inc(scaled_u, 1)

                def low(k):
                    dve.wait_ge(split_hi, split_at(l, 1, k) + 1)
                    nc.vector.tensor_tensor(a_lo[:, k, :], uc[:, k, :], a_hi[:, k, :].bitcast(F32), ALU.subtract)\
                        .then_inc(split_lo, 1)

                scale(0)
                for k in range(KT):
                    if k + 1 < KT:
                        scale(k + 1)
                    dve.wait_ge(silu_u, k + 1)
                    dve.wait_ge(pb_free[k % 2], pair0 + KT + k // 2 + 1)
                    nc.vector.tensor_tensor(uc[:, k, :], uc[:, k, :], cc_gate[:, k, :], ALU.mult).then_inc(gated_u, 1)
                    if k:
                        low(k - 1)
                low(KT - 1)

            def swa(l):
                pair0 = TILE0[l] // 2

                def normed(e, dst, g):
                    dve.wait_ge(nrr_ready, e + 1)
                    nc.vector.scalar_tensor_tensor(dst[:, :], dst[:, :], qk_g[:, g:g + 1], qs[:, :], ALU.mult, ALU.mult)\
                        .then_inc(qn_ready, 1)

                def gate(n, p):
                    dve.wait_ge(gth_done, n + 1)
                    for half in range(2):
                        z = halves(zs[p])[half]
                        ins = nc.vector.scalar_tensor_tensor(z, z, 1.0, PB[1][half][:, :], ALU.add, ALU.mult)
                    ins.then_inc(pb_free[1], 1)

                def soft(n, b, j):
                    e, s = NB * n + b, sm[b % 2]
                    keys = slice(WINDOW if b == 0 else 0, 2 * WINDOW)
                    dve.wait_ge(lmm_done, e + 1)
                    if b == 0:
                        dve.wait_ge(bias_loaded[j], 8 * (n - j) + 16)
                    if b > 1:
                        dve.wait_ge(trp_done, e - 1)
                    nc.vector.scalar_tensor_tensor(
                        lg[b % 2][:, :, keys], DB[0][:, :].rearrange("p (h c) -> p h c", h=2)[:, :, keys], HD ** -0.5,
                        bias[:, j, :, keys], ALU.mult, ALU.add).then_inc(lg_ready, 1)
                    dve.wait_ge(lg_ready, e + 1)
                    ch = Chain(dve, soft_step, 3 * e)
                    ch.link(nc.vector.tensor_reduce(s[:, MX, :], lg[b % 2][:, :, keys], AX_X, ALU.max))
                    sink = sinks[:, bass.ds(2 * n, 2)]
                    ch.link(nc.vector.tensor_tensor(s[:, MM, :], s[:, MX, :], sink, ALU.max))
                    ch.link(nc.vector.tensor_scalar(s[:, NEG_M, :], s[:, MM, :], -1.0, None, ALU.mult))
                    nc.vector.tensor_tensor(s[:, SK, :], s[:, NEG_M, :], sink, ALU.add).then_inc(mx_ready, 1)

                def inverse(n, b):
                    e, s = NB * n + b, sm[b % 2]
                    dve.wait_ge(e_ready, 2 * e + 2)
                    dve.wait_ge(esk_ready, e + 1)
                    nc.vector.tensor_tensor(s[:, DEN, :], s[:, ES, :], s[:, ESK, :], ALU.add).then_inc(den_ready, 1)
                    dve.wait_ge(den_ready, e + 1)
                    nc.vector.reciprocal(s[:, RDEN, :], s[:, DEN, :]).then_inc(r_ready, 1)

                def gated(n, m, p):
                    dve.wait_ge(pv_done, NB * n + 4 * m + 4)
                    z = halves(zs[p])[m]
                    nc.vector.scalar_tensor_tensor(z, DB[3][:, :], 0.5, z, ALU.mult, ALU.mult).then_inc(att_ready, 1)

                def low(n, m, p):
                    if m:
                        dve.wait_ge(split_hi, split_at(l, 1, n) + 1)
                    else:
                        dve.wait_ge(half_hi, n + 1)
                    cols = bass.ds(n * T + m * HALF, HALF)
                    nc.vector.tensor_tensor(b_lo_flat[:, cols], halves(zs[p])[m], b_hi_flat[:, cols].bitcast(F32),
                                            ALU.subtract).then_inc(split_lo if m else half_lo, 1)

                def heads(n, j, last):
                    for b in range(NB):
                        soft(n, b, j)
                        if b:
                            inverse(n, b - 1)
                        if b == 6:
                            gated(n, 0, j)
                        if b == 7:
                            low(n, 0, j)
                    inverse(n, NB - 1)
                    if not last:
                        normed(n + 2, q_n[1 - j], 0)
                    gated(n, 1, j)
                    low(n, 1, j)
                    if not last:
                        gate(n + 1, 1 - j)

                dve.wait_ge(split_lo, split_at(l, 0, KT))
                for kv in range(2):
                    for hh in range(2):
                        ins = nc.vector.memset(k_pad[kv][HD * (1 - hh):HD * (1 - hh) + HD, hh, :], 0.0)
                ins.then_inc(k_zeros, 1)
                normed(0, q_n[1], 1)
                normed(1, q_n[0], 0)
                gate(0, 0)
                with dve.Fori(0, 3) as i:
                    for j in range(2):
                        heads(2 * i + j, j, False)
                heads(KT - 2, 0, False)
                heads(KT - 1, 1, True)

            dve.wait_ge(bias_psum, 1)
            nc.vector.tensor_tensor(bias_rows[:, :], DB[3][0:QH, 0:BIAS_LEN], bias_mask[:, :], ALU.add)\
                .then_inc(bias_sum, 1)
            for k in range(KT):
                accumulate(0, k)
            for l in range(LAYERS):
                norm(l)
                if MIXER[l] == "gdn":
                    gdn(l)
                elif MIXER[l] == "cc":
                    cc(l)
                else:
                    swa(l)
                out_projection(l)
                embedding(l)


def _tiles(w, order=None):
    *lead, k, n = w.shape
    w = w.reshape(*lead, k // P, P, n // P, P)
    m = len(lead)
    w = w.transpose(*range(m), m + 2, m + 1, m, m + 3)
    if order is not None:
        w = w[(slice(None),) * m + (order,)]
    return w.reshape(*lead, n // P, P, k)


def _arrays(a):
    a = {k: np.asarray(v) for k, v in a.items()}
    x_t = a["x"][0].T.reshape(KT, P, T).transpose(1, 0, 2).reshape(P, KT * T)
    p_t = a["p"][:, 0].transpose(0, 2, 1).reshape(DEPTH, PLE_K, P, T).transpose(0, 2, 1, 3).reshape(DEPTH, P, PLE_K * T)
    gdn_order = [t * HEADS + h for h in range(HEADS) for t in (1, 0, 2, 3)]
    w_ba = a["gdn_w_in"][:, :, 4 * D:].reshape(2, KT, P, 16).transpose(0, 2, 1, 3).reshape(2, P, KT * 16)
    wp = a["ple_w_proj"].reshape(DEPTH, PLE_K, P, KT, P).transpose(0, 2, 3, 1, 4).reshape(DEPTH, P, KT * PLE_K * P)
    cw = a["gdn_conv_w"].reshape(2, TAPS, 3, HEADS, P)[:, :, [1, 0, 2]].transpose(4, 0, 3, 2, 1).reshape(P, -1)
    per_head = lambda v: np.broadcast_to(v[None, :, :, None], (P, 2, HEADS, NCHUNK)).reshape(P, -1)
    i, j = np.arange(P)[:, None], np.arange(P)[None, :]
    levels = [-((i // (2 << b) == j // (2 << b)) & (i >> b & 1 == 1) & (j >> b & 1 == 0)).astype(np.float32)
              for b in range(LEVELS)]
    f = np.float32
    dist = 2 * P - 1 - np.arange(BIAS_LEN)
    valid = (dist >= 0) & (dist < WINDOW)
    half_b = BUCKETS // 2
    n = np.maximum(dist, half_b)
    bucket = np.where(dist < half_b, np.maximum(dist, 0), np.minimum(
        half_b + np.floor(np.log(n / half_b) / np.log(WINDOW / half_b) * half_b).astype(np.int32), BUCKETS - 1))
    swa_order = [QH // 2, QH // 2 + 1] + [t for n in range(KT) for t in (n, KT + 2 + n)]
    cc_order = [t for n in range(KT) for t in (n, KT + n)] + list(range(2 * KT, 3 * KT))
    per_tile = lambda v: v.reshape(KT, P).T
    out = {
        "w_cc_in": _tiles(a["cc_w_in"], cc_order), "w_cc_out": _tiles(a["cc_w_out"]),
        "w_swa_in": _tiles(a["swa_w_in"], swa_order), "w_swa_out": _tiles(a["swa_w_out"]),
        "c_blk": ((i // HD == j // HD) / HD).astype(f),
        "c_sinks": np.broadcast_to(a["swa_sinks"], (P, QH)),
        "c_qk_g": np.stack([np.tile(a["swa_q_norm_g"][0], 2), np.tile(a["swa_k_norm_g"][0], 2)], 1),
        "c_cc_w": a["cc_dw_w"][0].reshape(CC_TAPS, KT, P).transpose(2, 1, 0).reshape(P, -1),
        "c_cc_par": np.concatenate([per_tile(a["cc_dw_b"][0]), per_tile(a["cc_ln_g"][0]), per_tile(a["cc_ln_b"][0])], 1),
        "c_rel": a["rel_bias"],
        "c_onehot": (valid & (bucket == np.arange(BUCKETS)[:, None])).astype(f),
        "c_bias_mask": np.broadcast_to(np.where(valid, 0, NEG).astype(f), (QH, BIAS_LEN)),
        "x_t": x_t, "p_t": p_t, "w_gdn_in": _tiles(a["gdn_w_in"][:, :, :4 * D], gdn_order),
        "w_gdn_ba": w_ba, "w_gdn_out": _tiles(a["gdn_w_out"]), "w_gate": _tiles(a["ple_w_gate"]), "w_embed": wp,
        "c_ident": np.eye(P, dtype=f), "c_cum_u": (i <= j).astype(f), "c_mask_t": np.where(j >= i, 0, NEG).astype(f),
        "c_ones": np.ones((P, P), f),
        "c_masks": np.concatenate([*levels, (j > i).astype(f)], 1),
        "c_norm_g": a["norm_g"].reshape(DEPTH, KT, P).transpose(2, 0, 1).reshape(P, -1),
        "c_conv_w": cw, "c_a_log": per_head(a["gdn_A_log"]), "c_dt_b": per_head(a["gdn_dt_bias"]),
        "c_gdn_g": a["gdn_norm_g"].T,
    }
    return {k: np.ascontiguousarray(v) for k, v in out.items()}


LAYERS = DEPTH
MIXER = ["gdn", "cc", "swa", "gdn"]
SPILL = [False, True, True, False]
STREAM = TILE0[LAYERS]


def kernel(**inputs):
    import concourse.bacc as bacc
    from concourse.bass_utils import run_bass_kernel_spmd

    nc = bacc.Bacc("TRN2", target_bir_lowering=False, num_devices=1)
    arrays = _arrays(inputs)
    d = {n: nc.dram_tensor("in_" + n, a.shape, mybir.dt.from_np(a.dtype), kind="ExternalInput").ap()
         for n, a in arrays.items()}
    d["out"] = nc.dram_tensor("out_x_t", (P, KT * T), F32, kind="ExternalOutput").ap()
    save = nc.dram_tensor("x_save", (DEPTH, P, KT * T), F32, kind="Internal").ap()
    d["x_save"] = [save[l] for l in range(DEPTH)]
    d["bias_rows"] = nc.dram_tensor("bias_rows_dram", (QH, BIAS_LEN), F32, kind="Internal").ap()
    copies = nc.dram_tensor("bias_copies", (QH, P * BIAS_LEN), F32, kind="Internal").ap()
    d["bias_copies"] = copies.rearrange("h (q m) -> h q m", q=P)
    d["bias_window"] = copies[:, WINDOW - 1:WINDOW - 1 + P * (BIAS_LEN - 1)]\
        .rearrange("h (q m) -> q h m", q=P)[:, :, 0:2 * WINDOW]
    build(nc, d)
    r = run_bass_kernel_spmd(nc, [{"in_" + n: a for n, a in arrays.items()}], core_ids=[0])
    out = r.results[0]["out_x_t"].reshape(P, KT, T)
    return np.ascontiguousarray(out.transpose(2, 1, 0)).reshape(1, T, D)
```

```python
from contextlib import ExitStack

import numpy as np

import concourse.bass as bass
from concourse import mybir

F32 = mybir.dt.float32
F32R = mybir.dt.float32r
BF16 = mybir.dt.bfloat16
ALU = mybir.AluOpType
ACT = mybir.ActivationFunctionType
AX_X = mybir.AxisListType.X

P = 128
D = 1024
T = 1024
KT = D // P
HALF = 512
DEPTH = 4
PLE_K = 2
RMS_EPS = 1e-6
LN_EPS = 1e-5
HEADS = 8
TAPS = 4
CHUNK = 128
NCHUNK = T // CHUNK
GROUP = 4
Z_EARLY = 32
LEVELS = 7
CC_TAPS = 31
CC_SHARED = 9
WINDOW = 128
NB = T // WINDOW
QH = 16
HD = 64
BUCKETS = 32
BIAS_LEN = 3 * WINDOW - 1
NEG = -1e30

GDN_IN = 4 * HEADS
CC_IN = 3 * KT
SWA_IN = 2 + 2 * KT
OUT = KT
LAYER_IN = [GDN_IN, CC_IN, SWA_IN, GDN_IN]
TILE0 = [sum(LAYER_IN[:l]) + 2 * OUT * l for l in range(DEPTH + 1)]
TILES = TILE0[DEPTH]


class Chain:

    def __init__(self, eng, sem, base):
        self.eng, self.sem, self.base, self.n = eng, sem, base, 0

    def link(self, ins):
        ins.then_inc(self.sem, 1)
        self.n += 1
        self.eng.wait_ge(self.sem, self.base + self.n)

    def end(self, n):
        assert self.n == n, (self.sem, self.n, n)


def build(nc, d):
    ctx = ExitStack()
    with ctx:
        psum = [ctx.enter_context(nc.psum_tensor(f"bank{b}", [P, HALF], F32)) for b in range(8)]
        PB = [psum[0:2], psum[2:4]]
        DB = psum[4:8]

        def at(name, offset, shape, dt=F32):
            return nc.alloc_sbuf_tensor_at(name, [P] + shape, dt, offset=offset)

        S0 = 16512
        w_raw = [at(f"w_raw{j}", S0 + 4096 * j, [KT, P]) for j in range(2)]
        w_hi = [at(f"w_hi{j}", S0 + 8192 + 4096 * j, [KT, P], F32R) for j in range(2)]
        w_lo = [at(f"w_lo{j}", S0 + 16384 + 4096 * j, [KT, P], F32R) for j in range(2)]
        A0 = S0 + 24576
        a_hi = at("a_hi", A0, [KT, T], F32R)
        a_lo = at("a_lo", A0 + 32768, [KT, T], F32R)
        X0 = A0 + 65536
        x_sb = at("x_sb", X0, [KT, T])
        B0 = X0 + 32768
        b_hi = at("b_hi", B0, [KT, T], F32R)
        b_lo = at("b_lo", B0 + 32768, [KT, T], F32R)
        M0 = B0 + 65536
        C0 = 229344 - 11872
        cur = [C0]

        def const(name, shape, dt=F32):
            n = int(np.prod(shape)) * (2 if dt == BF16 else 4)
            t = at(name, cur[0], shape, dt)
            cur[0] += (n + 31) // 32 * 32
            assert cur[0] <= 229344, (name, cur[0])
            return t

        ident = const("ident", [P])
        ident_r = const("ident_r", [P], F32R)
        cum_u = const("cum_u", [P])
        mask_t = const("mask_t", [P])
        ones = const("ones", [P])
        level_mask = const("level_mask", [LEVELS, P], BF16)
        strict = const("strict", [P], BF16)
        norm_g = const("norm_g", [DEPTH, KT])
        conv_w = const("conv_w", [2, HEADS, 3, TAPS])
        a_log = const("a_log", [2, HEADS, NCHUNK])
        dt_b = const("dt_b", [2, HEADS, NCHUNK])
        gdn_g = const("gdn_g", [2, 1])
        gdn_gh = const("gdn_gh", [2, 1])
        KINDS = 7
        NGC, EG, NEG_EG, EDEC, EGL, BETA, GG = range(KINDS)
        tok = const("tok", [HEADS, KINDS, NCHUNK])
        hv = [const(f"hv{j}", [KINDS, NCHUNK]) for j in range(2)]
        cw = const("cw", [3, TAPS])
        ssk = const("ssk", [NCHUNK])
        ssq = const("ssq", [NCHUNK])
        gg_hi = const("gg_hi", [NCHUNK], F32R)
        gg_lo = const("gg_lo", [NCHUNK])
        ones_r = const("ones_r", [P], F32R)
        c_tok = const("c_tok", [NCHUNK])
        sq_tk = const("sq_tk", [NCHUNK])
        half_e = const("half_e", [NCHUNK])
        mhalf_e = const("mhalf_e", [NCHUNK])
        tq = const("tq", [NCHUNK])
        oss = const("oss", [NCHUNK])
        om = const("om", [NCHUNK])
        osc = const("osc", [NCHUNK])
        blk = const("blk", [P])
        sinks = const("sinks", [QH])
        qk_g = const("qk_g", [2])
        cc_w = const("cc_w", [KT, CC_TAPS])
        cc_par = const("cc_par", [3, KT])
        CC_B, LN_G, LN_B = range(3)
        eps = const("eps", [1])
        ln_eps = const("ln_eps", [1])

        acc = at("acc", M0, [T])
        sqt = at("sqt", M0 + 4096, [T])
        sqt2 = at("sqt2", M0 + 8192, [T])
        rstd = at("rstd", B0 + 16384, [T])
        hf = [at(f"hf{j}", B0 + 20480 + 4096 * j, [T]) for j in range(KT)]

        class Embedding:

            def __init__(self, name, base):
                self.p_raw = at(name + "p_raw", base, [PLE_K, T])
                self.pw_raw = at(name + "pw_raw", base + 8192, [KT, PLE_K, P])
                self.p_hi = at(name + "p_hi", base + 16384, [PLE_K, T], F32R)
                self.p_lo = at(name + "p_lo", base + 24576, [PLE_K, T], F32R)
                self.pw_hi = at(name + "pw_hi", base + 32768, [KT, PLE_K, P], F32R)
                self.pw_lo = at(name + "pw_lo", base + 40960, [KT, PLE_K, P], F32R)
                self.p_th = at(name + "p_th", base + 49152, [T])
                self.p_t = at(name + "p_t", base + 53248, [T])

        in_a, in_b = (a_hi, a_lo), (b_hi, b_lo)
        emb_a, emb_b = Embedding("a_", A0), Embedding("b_", B0)
        PLACES = {"gdn": (in_b, in_a, emb_b), "swa": (in_b, in_a, emb_b), "cc": (in_a, in_b, emb_a)}

        PAD = CC_TAPS - 1
        u_in = [at(f"u_in{j}", M0 + 4224 * j, [PAD + T]) for j in range(2)]
        cc_th = at("cc_th", M0 + 8448, [T])
        uc = at("uc", B0, [KT, T])
        cc_gate = at("cc_gate", B0 + 32768, [KT, T])
        shared = [at(f"shared{j}", X0 + 4096 * j, [T]) for j in range(2)]
        scaled_tap = [at(f"scaled_tap{j}", X0 + 8192 + 4096 * j, [T]) for j in range(2)]
        sq_sum = [at(f"sq_sum{j}", X0 + 16384 + 4096 * j, [T]) for j in range(2)]
        u_sq = [at(f"u_sq{j}", X0 + 24576 + 4096 * j, [T]) for j in range(2)]
        mu = at("mu", M0, [T])
        cc_sq = at("cc_sq", M0 + 4096, [T])
        cc_rstd = at("cc_rstd", M0 + 8192, [T])

        bias = at("bias", X0, [2, 2, 2 * WINDOW])
        k_pad = [at("k_pad0", B0 + 6 * 4096, [2, T]), at("k_pad1", X0 + 4096, [2, T])]
        v_tok = at("v_tok", X0 + 12288, [NB, P])
        q_n = [at(f"q_n{j}", X0 + 16384 + 4096 * j, [T]) for j in range(2)]
        zs = [at(f"zs{j}", X0 + 24576 + 4096 * j, [T]) for j in range(2)]
        qs = at("qs", M0, [T])
        lg = [at(f"lg{j}", M0 + 4096 + 2048 * j, [2, 2 * WINDOW]) for j in range(2)]
        pr_t = [at(f"pr_t{j}", M0 + 8192 + 2048 * j, [2, 2, WINDOW]) for j in range(2)]
        sm = [at(f"sm{j}", M0 + 12288 + 64 * j, [8, 2]) for j in range(2)]
        MX, MM, NEG_M, SK, ES, ESK, DEN, RDEN = range(8)
        rel = nc.alloc_sbuf_tensor_at("rel", [BUCKETS, QH], F32, offset=A0)
        onehot = nc.alloc_sbuf_tensor_at("onehot", [BUCKETS, BIAS_LEN], F32, offset=A0 + 64)
        bias_mask = nc.alloc_sbuf_tensor_at("bias_mask", [QH, BIAS_LEN], F32, offset=A0 + 2048)
        bias_rows = nc.alloc_sbuf_tensor_at("bias_rows", [QH, BIAS_LEN], F32, offset=A0 + 4096)

        o_sb = at("o_sb", X0, [HEADS, T])
        kq = [at(f"kq{j}", B0 + 16384 * j, [NCHUNK, 2, P]) for j in range(2)]
        vb = [at(f"vb{j}", B0 + 16384 * j + 8192, [T]) for j in range(2)]
        zb = [at(f"zb{j}", B0 + 16384 * j + 12288, [T]) for j in range(2)]
        G0 = B0 + 32768

        def slot(name, g, s, dt=F32):
            return at(f"{name}{g}", G0 + (g * 8 + s) * 2048, [GROUP, P], dt)

        u_hi = [slot("u_hi", g, 0, F32R) for g in range(2)]
        u_lo = [slot("u_lo", 1, 2 + g, F32R) for g in range(2)]
        p_m = [slot("p_m", g, 0, F32R) for g in range(2)]
        y_m = [slot("y_m", g, 0, F32R) for g in range(2)]
        arg = [slot("arg", g, 1) for g in range(2)]
        nt_r = [slot("nt_r", g, 1, F32R) for g in range(2)]
        tt = [slot("tt", g, 1) for g in range(2)]
        dt_m = [slot("dt_m", g, 2) for g in range(2)]
        m_m = [slot("m_m", g, 2, F32R) for g in range(2)]
        dts = [slot("dts", g, 3) for g in range(2)]
        mt_m = [slot("mt_m", g, 3, F32R) for g in range(2)]
        nt = [slot("nt", g, 4) for g in range(2)]
        nt_lo = [slot("nt_lo", g, 4, F32R) for g in range(2)]
        o_g = [slot("o_g", g, 4) for g in range(2)]
        p_t_m = [slot("p_t_m", g, 5) for g in range(2)]
        k_dec = [slot("k_dec", g, 6) for g in range(2)]
        r_v = [slot("r_v", g, 7) for g in range(2)]
        kt_sq = at("kt_sq", G0 + 3 * 2048 + 512, [P])
        state = at("state", G0 + 2 * 2048, [P])
        r4 = at("r4", G0 + 2 * 2048 + 512, [P])
        u_sb = at("u_sb", G0 + 2 * 2048 + 1024, [P])
        qs_sb = at("qs_sb", G0 + 2 * 2048 + 1536, [P])
        sq_o = at("sq_o", G0 + 3 * 2048, [P])
        F0 = G0 + 32768
        c_in = at("c_in", F0, [TAPS - 1 + T])
        c_acc = at("c_acc", F0 + 4128, [T])
        th = at("th", F0 + 8224, [T])
        assert F0 + 12320 <= C0
        WB0 = G0 + 12 * 2048
        wb_raw = at("wb_raw", WB0, [KT, 2 * HEADS])
        wb_hi = at("wb_hi", WB0 + 512, [KT, 2 * HEADS], F32R)
        wb_lo = at("wb_lo", WB0 + 1024, [KT, 2 * HEADS], F32R)
        g_t = [at(f"g_t{j}", WB0 + 2048 + 256 * j, [HEADS, NCHUNK]) for j in range(6)]
        ba_rows = nc.alloc_sbuf_tensor_at("ba_rows", [2 * HEADS, T], F32, offset=G0 + 6 * 2048)
        mask_stage = at("mask_stage", B0, [LEVELS + 1, P])

        flat = lambda t: t[:, :, :].rearrange("p a b -> p (a b)")
        conv_flat = conv_w[:, :, :, :, :].rearrange("p s h r t -> p (s h r t)")
        tok_flat = tok[:, :, :, :].rearrange("p h k c -> p (h k c)")
        CONSTS = {
            "c_ident": ident[:, :], "c_cum_u": cum_u[:, :], "c_mask_t": mask_t[:, :], "c_ones": ones[:, :],
            "c_masks": mask_stage[:, :, :].rearrange("p a b -> p (a b)"),
            "c_norm_g": norm_g[:, :, :].rearrange("p a b -> p (a b)"), "c_conv_w": conv_flat,
            "c_a_log": a_log[:, :, :, :].rearrange("p s h c -> p (s h c)"),
            "c_dt_b": dt_b[:, :, :, :].rearrange("p s h c -> p (s h c)"),
            "c_gdn_g": gdn_g[:, :, 0], "c_blk": blk[:, :], "c_sinks": sinks[:, :], "c_qk_g": qk_g[:, :],
            "c_cc_w": cc_w[:, :, :].rearrange("p a b -> p (a b)"),
            "c_cc_par": cc_par[:, :, :].rearrange("p a b -> p (a b)"),
            "c_rel": rel[:, :], "c_onehot": onehot[:, :], "c_bias_mask": bias_mask[:, :],
        }

        def sem(name):
            return ctx.enter_context(nc.semaphore(name))

        const_loaded = sem("const_loaded")
        const_ready = sem("const_ready")
        w_loaded = [sem(f"w_loaded{j}") for j in range(2)]
        w_hi_done = sem("w_hi_done")
        w_split = sem("w_split")
        tile_done = sem("tile_done")
        pb_free = [sem(f"pb_free{j}") for j in range(2)]
        x_tile_loaded = [sem(f"x_tile_loaded{k}") for k in range(KT)]
        sq_done = sem("sq_done")
        acc_done = sem("acc_done")
        stat_done = sem("stat_done")
        rstd_step = sem("rstd_step")
        hf_done = sem("hf_done")
        split_hi = sem("split_hi")
        split_lo = sem("split_lo")
        x_mid = sem("x_mid")
        x_new = sem("x_new")
        x_reloaded = sem("x_reloaded")
        x_stored = sem("x_stored")
        p_loaded = sem("p_loaded")
        pw_loaded = sem("pw_loaded")
        p_hi_done = sem("p_hi_done")
        p_split = sem("p_split")
        pp_done = sem("pp_done")
        p_t_done = sem("p_t_done")

        def split_at(l, which, k):
            return 24 * l + 8 * which + k

        x_flat, o_flat = flat(x_sb), flat(o_sb)
        flat4 = lambda t: t[:, :, :, :].rearrange("p a b c -> p (a b c)")
        a_hi_flat, a_lo_flat, b_hi_flat, b_lo_flat = flat(a_hi), flat(a_lo), flat(b_hi), flat(b_lo)

        wb_loaded = sem("wb_loaded")
        wb_hi_done = sem("wb_hi_done")
        wb_split = sem("wb_split")
        ba_rows_done = sem("ba_rows_done")
        ba_rows_ready = sem("ba_rows_ready")
        ba_done = sem("ba_done")
        ba_step = sem("ba_step")
        ba_act = sem("ba_act")
        g_ready = sem("g_ready")
        gcum_done = sem("gcum_done")
        tok_done = sem("tok_done")
        pad_ready = sem("pad_ready")
        conv_step = sem("conv_step")
        conv_done = sem("conv_done")
        th_done = sem("th_done")
        silu_done = sem("silu_done")
        cw_ready = sem("cw_ready")
        kt_done = sem("kt_done")
        ss_read = sem("ss_read")
        dve_step = sem("dve_step")
        sqrt_done = sem("sqrt_done")
        hv_ready = sem("hv_ready")
        ug_ready = sem("ug_ready")
        gg_step = sem("gg_step")
        rowg_done = sem("rowg_done")
        arg_ready = sem("arg_ready")
        dt_ready = sem("dt_ready")
        dts_ready = sem("dts_ready")
        gram_done = sem("gram_done")
        nt_ready = sem("nt_ready")
        ntr_ready = sem("ntr_ready")
        tr_done = sem("tr_done")
        kdec_ready = sem("kdec_ready")
        ssk_done = sem("ssk_done")
        ssq_done = sem("ssq_done")
        rv_ready = sem("rv_ready")
        pm_done = sem("pm_done")
        p_ready = sem("p_ready")
        m_done = sem("m_done")
        m_ready = sem("m_ready")
        mt_ready = sem("mt_ready")
        y_done = sem("y_done")
        ntlo_ready = sem("ntlo_ready")
        y_ready = sem("y_ready")
        t_done = sem("t_done")
        tt_ready = sem("tt_ready")
        ks_done = sem("ks_done")
        qs_done = sem("qs_done")
        qs_ready = sem("qs_ready")
        r4_ready = sem("r4_ready")
        u_done = sem("u_done")
        u_ready = sem("u_ready")
        ds_done = sem("ds_done")
        op_done = sem("op_done")
        s_ready = sem("s_ready")
        o_ready = sem("o_ready")
        oss_ready = sem("oss_ready")
        om_ready = sem("om_ready")
        tq_ready = sem("tq_ready")
        osc_ready = sem("osc_ready")
        on_ready = sem("on_ready")
        ot_done = sem("ot_done")
        o_written = sem("o_written")

        block = ctx.enter_context(nc.Block())

        cc_u_ready = sem("cc_u_ready")
        cc_pad = sem("cc_pad")
        tap = sem("tap")
        cc_done = sem("cc_done")
        cc_product = sem("cc_product")
        cc_added = sem("cc_added")
        mean_done = sem("mean_done")
        mu_ready = sem("mu_ready")
        centred = sem("centred")
        cc_sq_ready = sem("cc_sq_ready")
        var_done = sem("var_done")
        sq_added = [sem(f"sq_added{j}") for j in range(2)]
        cc_rstd_step = sem("cc_rstd_step")
        scaled_u = sem("scaled_u")
        silu_u = sem("silu_u")
        gated_u = sem("gated_u")
        bias_psum = sem("bias_psum")
        bias_sum = sem("bias_sum")
        bias_stored = sem("bias_stored")
        bias_spread = sem("bias_spread")
        bias_loaded = [sem(f"bias_loaded{j}") for j in range(2)]
        nsq_ready = sem("nsq_ready")
        nms_done = sem("nms_done")
        nln_done = sem("nln_done")
        nrr_ready = sem("nrr_ready")
        qn_ready = sem("qn_ready")
        k_spread = sem("k_spread")
        k_zeros = sem("k_zeros")
        v_turned = sem("v_turned")
        v_ready = sem("v_ready")
        lmm_done = sem("lmm_done")
        lg_ready = sem("lg_ready")
        soft_step = sem("soft_step")
        mx_ready = sem("mx_ready")
        e_ready = sem("e_ready")
        esk_ready = sem("esk_ready")
        den_ready = sem("den_ready")
        r_ready = sem("r_ready")
        pr_ready = sem("pr_ready")
        trp_done = sem("trp_done")
        prt_ready = sem("prt_ready")
        pv_done = sem("pv_done")
        att_ready = sem("att_ready")
        gth_done = sem("gth_done")
        half_hi = sem("half_hi")
        half_lo = sem("half_lo")

        def gdn_slot(l):
            return l // 3

        @block.sync
        def _(sp):
            def section(source, base, n):
                first = 0
                if base == 0:
                    for j in range(2):
                        sp.dma_start(flat(w_raw[j]), source[j]).then_inc(w_loaded[j], 16)
                    first = 1
                with sp.Fori(first, n // 2) as i:
                    for j in range(2):
                        sp.wait_ge(w_split, base + 2 * i + j - 1)
                        sp.dma_start(flat(w_raw[j]), source[bass.ds(2 * i + j, 1)]
                                     .rearrange("a p n -> (a p) n")).then_inc(w_loaded[j], 16)

            for name, t in CONSTS.items():
                sp.dma_start(t, d[name]).then_inc(const_loaded, 16)
            for l in range(LAYERS):
                mixer = MIXER[l]
                section(d["w_" + mixer + "_in"][gdn_slot(l) if mixer == "gdn" else 0], TILE0[l], LAYER_IN[l])
                section(d["w_" + mixer + "_out"][gdn_slot(l) if mixer == "gdn" else 0], TILE0[l] + LAYER_IN[l], OUT)
                section(d["w_gate"][l], TILE0[l] + LAYER_IN[l] + OUT, OUT)

        @block.gpsimd
        def _(pool):
            def split_tile(pair, j):
                pool.wait_ge(w_loaded[j], 16 * (pair + 1))
                if not (isinstance(pair, int) and pair == 0):
                    pool.wait_ge(tile_done, 2 * pair + j - 1)
                nc.gpsimd.tensor_tensor(w_hi[j][:, :, :], w_raw[j][:, :, :],
                                        ones[:, :].unsqueeze(1).to_broadcast([P, KT, P]), ALU.mult)\
                    .then_inc(w_hi_done, 1)
                pool.wait_ge(w_hi_done, 2 * pair + j + 1)
                nc.gpsimd.tensor_tensor(flat(w_lo[j]), flat(w_raw[j]), flat(w_hi[j]).bitcast(F32),
                                        ALU.subtract).then_inc(w_split, 1)

            def section(base, n):
                if base + n + 2 > STREAM:
                    n -= 2
                with pool.Fori(0, n // 2) as i:
                    for j in range(2):
                        split_tile(base // 2 + i + 1, j)

            def gdn(l):
                pair0, h0 = TILE0[l] // 2, HEADS * gdn_slot(l)

                def prepare(h):
                    hh = h0 + h
                    for g in range(2):
                        pool.wait_ge(dt_ready, 2 * hh + g + 1)
                        nc.gpsimd.tensor_tensor(dts[g][:, :, :], dt_m[g][:, :, :],
                                                strict[:, :].unsqueeze(1).to_broadcast([P, GROUP, P]),
                                                ALU.mult).then_inc(dts_ready, 1)
                    pool.wait_ge(ss_read, hh + 1)
                    nc.gpsimd.tensor_tensor(sq_tk[:, :], ssk[:, :], half_e[:, :], ALU.pow)\
                        .then_inc(sqrt_done, 1)

                def output_scale(hh, g):
                    pool.wait_ge(om_ready, 2 * hh + g + 1)
                    nc.gpsimd.tensor_tensor(osc[:, 4 * g:4 * g + 4], om[:, 4 * g:4 * g + 4],
                                            mhalf_e[:, 4 * g:4 * g + 4], ALU.pow).then_inc(osc_ready, 1)

                def delta(h, j, last):
                    hh = h0 + h
                    pair = pair0 + 2 * (h + 1)
                    split_tile(pair, 1)
                    if not last:
                        split_tile(pair + 1, 0)
                        split_tile(pair + 1, 1)
                    output_scale(hh, 0)
                    if not last:
                        split_tile(pair + 2, 0)
                    output_scale(hh, 1)
                    if not last:
                        prepare(h + 1)

                for pair, r in ((1, 0), (1, 1), (2, 0)):
                    split_tile(pair0 + pair, r)
                prepare(0)
                with pool.Fori(0, (HEADS - 2) // 2) as i:
                    for j in range(2):
                        delta(2 * i + j, j, False)
                delta(HEADS - 2, 0, False)
                delta(HEADS - 1, 1, True)

            def swa(l):
                pair0 = TILE0[l] // 2

                def probabilities(n, b):
                    keys = slice(WINDOW if b == 0 else 0, 2 * WINDOW)
                    e = lg[b % 2][:, :, keys]
                    pool.wait_ge(r_ready, NB * n + b + 1)
                    nc.gpsimd.tensor_tensor(e, e, sm[b % 2][:, RDEN, :].unsqueeze(2).to_broadcast([P, 2, keys.stop - keys.start]),
                                            ALU.mult).then_inc(pr_ready, 1)

                def heads(n, last):
                    for b in range(NB):
                        probabilities(n, b)
                    if not last:
                        split_tile(pair0 + n + 3, 0)
                        split_tile(pair0 + n + 3, 1)

                for n in range(2):
                    for j in range(2):
                        split_tile(pair0 + 1 + n, j)
                with pool.Fori(0, KT - 1) as n:
                    heads(n, False)
                heads(KT - 1, True)

            def cc(l):
                base, pair0 = TILE0[l], TILE0[l] // 2

                def ahead(t):
                    split_tile(pair0 + t // 2, t % 2)

                def add(n, i):
                    pool.wait_ge(cc_product, CC_SHARED * n + i + 1)
                    if n or i > 1:
                        pool.wait_ge(cc_added, (CC_SHARED - 1) * n + i - 1)
                    nc.gpsimd.tensor_tensor(shared[n % 2][:, :], shared[n % 2][:, :],
                                            scaled_tap[i % 2][:, :], ALU.add).then_inc(cc_added, 1)

                ahead(2)
                ahead(3)
                for n in range(KT):
                    for i in range(1, 3):
                        add(n, i)
                    ahead(3 * n + 4)
                    for i in range(3, 6):
                        add(n, i)
                    if n < KT - 1:
                        ahead(3 * n + 5)
                    for i in range(6, CC_SHARED):
                        add(n, i)
                    if n < KT - 1:
                        ahead(3 * n + 6)
                for k in range(2, KT, 2):
                    pool.wait_ge(cc_sq_ready, k + 1)
                    if k > 2:
                        pool.wait_ge(sq_added[0], k // 2 - 1)
                    nc.gpsimd.tensor_tensor(sq_sum[0][:, :], sq_sum[0][:, :], u_sq[0][:, :], ALU.add)\
                        .then_inc(sq_added[0], 1)
                for k in range(KT):
                    pool.wait_ge(silu_u, k + 1)
                    nc.gpsimd.tensor_tensor(uc[:, k, :], uc[:, k, :], cc_gate[:, k, :], ALU.mult)\
                        .then_inc(gated_u, 1)

            pool.wait_ge(const_ready, 1)
            split_tile(0, 0)
            split_tile(0, 1)
            for l in range(LAYERS):
                if MIXER[l] == "gdn":
                    gdn(l)
                elif MIXER[l] == "swa":
                    swa(l)
                else:
                    cc(l)
                section(TILE0[l] + LAYER_IN[l], OUT)
                section(TILE0[l] + LAYER_IN[l] + OUT, OUT)

        @block.tensor
        def _(pe):
            PASSES = ((0, 0), (0, 1), (1, 0))

            def product(out, j, k, half, act, last):
                for n, (wl, al) in enumerate(PASSES):
                    mm = pe.matmul(out[:, :], (w_lo if wl else w_hi)[j][:, k, :],
                                   act[al][:, k, half * HALF:(half + 1) * HALF],
                                   start=(k == 0 and n == 0), stop=(last and n == 2), skip_group_check=True)
                return mm

            def first_pair(pair, act, l, which):
                for j in range(2):
                    pe.wait_ge(w_split, 2 * pair + j + 1)
                    if pair:
                        pe.wait_ge(pb_free[j], pair)
                for k in range(KT):
                    pe.wait_ge(split_hi, split_at(l, which, k) + 1)
                    for j in range(2):
                        for half in range(2):
                            for w in (w_hi, w_lo):
                                pe.matmul(PB[j][half][:, :], w[j][:, k, :], act[0][:, k, half * HALF:(half + 1) * HALF],
                                          start=(k == 0 and w is w_hi), stop=False, skip_group_check=True)
                for j in range(2):
                    for k in range(KT):
                        if j == 0:
                            pe.wait_ge(split_lo, split_at(l, which, k) + 1)
                        for half in range(2):
                            mm = pe.matmul(PB[j][half][:, :], w_hi[j][:, k, :],
                                           act[1][:, k, half * HALF:(half + 1) * HALF],
                                           start=False, stop=(k == KT - 1), skip_group_check=True)
                    mm.then_inc(tile_done, 1)

            def tile(pair, j, act, lo_waits=None):
                pe.wait_ge(w_split, 2 * pair + j + 1)
                if not (isinstance(pair, int) and pair == 0):
                    pe.wait_ge(pb_free[j], pair)
                for k in range(KT):
                    if lo_waits is not None:
                        pe.wait_ge(split_lo, lo_waits + k + 1)
                    for half in range(2):
                        mm = product(PB[j][half], j, k, half, act, k == KT - 1)
                mm.then_inc(tile_done, 1)

            def stats(value):
                pe.wait_ge(acc_done, 6 * value)
                for squares in (acc, sqt):
                    if squares is sqt:
                        pe.wait_ge(sq_done, KT * value)
                    for half in range(2):
                        mm = pe.matmul(DB[half][:, :], ones[:, :], squares[:, half * HALF:(half + 1) * HALF],
                                       start=(squares is acc), stop=(squares is sqt), skip_group_check=True)
                mm.then_inc(stat_done, 1)

            def out_projection(l):
                pair0 = (TILE0[l] + LAYER_IN[l]) // 2
                first_pair(pair0, PLACES[MIXER[l]][0], l, 1)
                with pe.Fori(1, OUT // 2) as i:
                    for j in range(2):
                        tile(pair0 + i, j, PLACES[MIXER[l]][0])

            def embedding_product(l, n, j):
                em = PLACES[MIXER[l]][2]
                if not isinstance(n, int) or n >= 2:
                    pe.wait_ge(p_t_done, OUT * l + n - 1)
                for half in range(2):
                    for k in range(PLE_K):
                        for m, (wl, al) in enumerate(PASSES):
                            mm = pe.matmul(DB[2 * j + half][:, :],
                                           (em.pw_lo if wl else em.pw_hi)[:, n, k, :],
                                           (em.p_lo if al else em.p_hi)[:, k, half * HALF:(half + 1) * HALF],
                                           start=(k == 0 and m == 0), stop=(k == PLE_K - 1 and m == 2),
                                           skip_group_check=True)
                mm.then_inc(pp_done, 1)

            def embedding(l):
                pair0 = (TILE0[l] + LAYER_IN[l] + OUT) // 2
                for n in range(OUT):
                    tile(pair0 + n // 2, n % 2, PLACES[MIXER[l]][1], split_at(l, 2, 0) if n == 0 else None)
                    if n == 1:
                        pe.wait_ge(p_split, 2 * (l + 1))
                    if n > 0:
                        embedding_product(l, n - 1, (n - 1) % 2)
                embedding_product(l, OUT - 1, (OUT - 1) % 2)

            def gdn(l):
                pair0, h0 = TILE0[l] // 2, HEADS * gdn_slot(l)
                first_pair(pair0, (a_hi, a_lo), l, 0)
                pe.wait_ge(wb_split, gdn_slot(l) + 1)
                for half in range(2):
                    for k in range(KT):
                        for m, (wl, al) in enumerate(PASSES):
                            mm = pe.matmul(DB[half][0:2 * HEADS, :], (wb_lo if wl else wb_hi)[:, k, :],
                                           (a_lo if al else a_hi)[:, k, half * HALF:(half + 1) * HALF],
                                           start=(k == 0 and m == 0), stop=(k == KT - 1 and m == 2),
                                           skip_group_check=True)
                mm.then_inc(ba_rows_done, 1)
                pe.wait_ge(ba_rows_ready, gdn_slot(l) + 1)
                for c in range(NCHUNK):
                    mm = pe.transpose(DB[2][:, c * 16:c * 16 + 16], ba_rows[:, c * CHUNK:(c + 1) * CHUNK],
                                      ident[0:2 * HEADS, 0:2 * HEADS])
                mm.then_inc(ba_done, 1)
                tile(pair0 + 1, 0, (a_hi, a_lo))
                pe.wait_ge(g_ready, gdn_slot(l) + 1)
                pe.matmul(DB[3][:, 0:64], cum_u[:, :], flat(g_t[5]), start=True, stop=True)
                pe.matmul(DB[3][:, 64:128], ones[:, :], flat(g_t[5]), start=True, stop=True)\
                    .then_inc(gcum_done, 1)

                def filler(h, first, end):
                    sent = [first]

                    def fill(n):
                        for _ in range(n):
                            s = sent[0]
                            if s == end:
                                return
                            r, half, k, m = s // 48, s % 48 // 24, s % 24 // 3, s % 3
                            j, pair = (r + 1) % 2, pair0 + 2 * h + 1 + r // 2 + r % 2
                            if s % 48 == 0:
                                pe.wait_ge(w_split, 2 * pair + j + 1)
                                pe.wait_ge(pb_free[j], pair)
                            wl, al = PASSES[m]
                            mm = pe.matmul(PB[j][half][:, :], (w_lo if wl else w_hi)[j][:, k, :],
                                           (a_lo if al else a_hi)[:, k, half * HALF:(half + 1) * HALF],
                                           start=(k == 0 and m == 0), stop=(k == KT - 1 and m == 2),
                                           skip_group_check=True)
                            if s % 48 == 47:
                                mm.then_inc(tile_done, 1)
                            sent[0] += 1

                    return fill

                def prepare(h, fill):
                    hh = h0 + h
                    for g in range(2):
                        pe.wait_ge(ug_ready, 2 * hh + g + 1)
                        for part in (u_hi, u_lo):
                            mm = pe.matmul(DB[g][:, :], ones_r[:, :], flat(part[g]), start=(part is u_hi),
                                           stop=(part is u_lo), skip_group_check=True)
                        mm.then_inc(rowg_done, 1)
                    fill(12)

                def turn_k(h, p, n, out):
                    if n == 0:
                        pe.wait_ge(silu_done, 4 * (h0 + h) + 1)
                    pe.transpose(out, kq[p][:, n, 0, :], ident[:, :]).then_inc(kt_done, 1)

                def delta(h, j, last):
                    hh = h0 + h
                    fill = filler(h, Z_EARLY, 48 if last else 192 + Z_EARLY)
                    k_q = kq[j]
                    for g in range(2):
                        pe.wait_ge(arg_ready, 2 * hh + 2)
                        for c in range(GROUP):
                            kc = k_q[:, GROUP * g + c, 0, :]
                            mm = pe.matmul(DB[2 * g + c // 2][:, (c % 2) * 256:(c % 2) * 256 + 256], kc,
                                           k_q[:, GROUP * g + c, :, :].rearrange("p a b -> p (a b)"),
                                           start=True, stop=True)
                        mm.then_inc(gram_done, 1)
                        fill(5)
                    pe.wait_ge(silu_done, 4 * hh + 3)
                    for g in range(2):
                        pe.wait_ge(nt_ready, 2 * hh + g + 1)
                        for c in range(GROUP):
                            n = GROUP * g + c
                            pe.transpose(DB[2 * g][:, c * P:(c + 1) * P], k_q[:, n, 1, :], ident[:, :])
                            mm = pe.transpose(DB[2 * g + 1][:, c * P:(c + 1) * P],
                                              vb[j][:, n * P:(n + 1) * P], ident[:, :])
                        mm.then_inc(tr_done, 1)
                        fill(5)
                    for lv in range(LEVELS):
                        for g in range(2):
                            e = 2 * (LEVELS * hh + lv) + g
                            if lv == 0:
                                pe.wait_ge(ntr_ready, 2 * hh + g + 1)
                                pe.wait_ge(ssq_done, NCHUNK * hh + GROUP * (g + 1))
                            else:
                                pe.wait_ge(m_ready, e - 1)
                            for c in range(GROUP):
                                mm = pe.matmul(DB[2 * g][:, c * P:(c + 1) * P], nt_r[g][:, c, :],
                                               m_m[g][:, c, :] if lv else ident_r[:, :], start=True, stop=True)
                            mm.then_inc(pm_done, 1)
                            fill(4)
                        for g in range(2):
                            e = 2 * (LEVELS * hh + lv) + g
                            pe.wait_ge(p_ready, e + 1)
                            if lv:
                                pe.wait_ge(mt_ready, e - 1)
                                for c in range(GROUP):
                                    pe.matmul(DB[2 * g][:, c * P:(c + 1) * P], mt_m[g][:, c, :],
                                              p_m[g][:, c, :], start=True, stop=True)
                                pe.matmul(DB[2 * g + 1][:, :], ident_r[:, :], flat(mt_m[g]),
                                          start=True, stop=False, skip_group_check=True)
                            else:
                                pe.wait_ge(rv_ready, 2 * hh + g + 1)
                                for c in range(GROUP):
                                    pe.matmul(DB[2 * g + 1][:, c * P:(c + 1) * P], ident_r[:, :],
                                              ident_r[:, :], start=(c == 0), stop=False, skip_group_check=True)
                            for c in range(GROUP):
                                mm = pe.matmul(DB[2 * g + 1][:, c * P:(c + 1) * P], p_m[g][:, c, :],
                                               mt_m[g][:, c, :] if lv else ident_r[:, :],
                                               start=False, stop=(c == GROUP - 1), skip_group_check=True)
                            mm.then_inc(m_done, 1)
                            fill(3 if lv < LEVELS - 2 else 2)
                    for g in range(2):
                        pe.wait_ge(m_ready, 2 * (LEVELS * hh + LEVELS - 1) + g + 1)
                        pe.wait_ge(ntlo_ready, 2 * hh + g + 1)
                        pe.matmul(DB[2 * g][:, :], ident_r[:, :], flat(m_m[g]), start=True, stop=False,
                                  skip_group_check=True)
                        for c in range(GROUP):
                            for part in (nt_r, nt_lo):
                                mm = pe.matmul(DB[2 * g][:, c * P:(c + 1) * P], part[g][:, c, :], m_m[g][:, c, :],
                                               start=False, stop=(c == GROUP - 1 and part is nt_lo),
                                               skip_group_check=True)
                        mm.then_inc(y_done, 1)
                        fill(3)
                    for g in range(2):
                        pe.wait_ge(y_ready, 2 * hh + g + 1)
                        pe.wait_ge(mt_ready, 2 * (LEVELS * hh + LEVELS - 1) + g + 1)
                        for c in range(GROUP):
                            mm = pe.matmul(DB[2 * g + 1][:, c * P:(c + 1) * P], y_m[g][:, c, :],
                                           mt_m[g][:, c, :], start=True, stop=True)
                        mm.then_inc(t_done, 1)
                        fill(3)
                    for n in range(NCHUNK):
                        g, c, e = n // GROUP, n % GROUP, NCHUNK * hh + n
                        if n == 0:
                            pe.wait_ge(tt_ready, 2 * hh + 2)
                        pe.wait_ge(s_ready, NCHUNK * hh + n + 1)
                        pe.matmul(DB[0][:, 0:P], k_q[:, n, 0, :], state[:, :], start=True, stop=True)\
                            .then_inc(ks_done, 1)
                        if n:
                            pe.wait_ge(o_ready, e)
                        pe.matmul(DB[1][:, 0:P], k_q[:, n, 1, :], state[:, :], start=True, stop=True)\
                            .then_inc(qs_done, 1)
                        fill(2)
                        pe.wait_ge(r4_ready, e + 1)
                        if n and not last:
                            pe.wait_ge(kdec_ready, e + NCHUNK)
                        pe.matmul(DB[2][:, 0:P], tt[g][:, c, :], r4[:, :], start=True, stop=True)\
                            .then_inc(u_done, 1)
                        fill(2)
                        pe.wait_ge(u_ready, e + 1)
                        if n < NCHUNK - 1:
                            pe.matmul(DB[3][:, 0:P], k_dec[g][:, c, :], u_sb[:, :], start=True, stop=True)\
                                .then_inc(ds_done, 1)
                        pe.wait_ge(qs_ready, e + 1)
                        pe.matmul(DB[1][:, 0:P], p_t_m[g][:, c, :], u_sb[:, :], start=True, stop=True)\
                            .then_inc(op_done, 1)
                        if not last:
                            turn_k(h + 1, 1 - j, n, DB[2][:, P:2 * P])
                        fill(2)
                    if not last:
                        pe.wait_ge(o_ready, NCHUNK * (hh + 1))
                        prepare(h + 1, fill)
                        pe.wait_ge(kdec_ready, NCHUNK * (hh + 2))
                    for g in range(2):
                        pe.wait_ge(on_ready, 2 * hh + g + 1)
                        for c in range(GROUP):
                            mm = pe.transpose(DB[2 + g][:, c * P:(c + 1) * P], o_g[g][:, c, :], ident[:, :])
                        mm.then_inc(ot_done, 1)
                    fill(192)
                    pe.wait_ge(o_written, 2 * hh + 2)

                fill = filler(-1, 192, 192 + Z_EARLY)
                pe.wait_ge(tok_done, gdn_slot(l) + 1)
                pe.wait_ge(ba_step, 5 * (gdn_slot(l) + 1))
                prepare(0, fill)
                for n in range(NCHUNK):
                    turn_k(0, 0, n, DB[2 + n // GROUP][:, n % GROUP * P:(n % GROUP + 1) * P])
                fill(192)
                pe.wait_ge(kdec_ready, NCHUNK * (h0 + 1))
                with pe.Fori(0, (HEADS - 2) // 2) as i:
                    for j in range(2):
                        delta(2 * i + j, j, False)
                delta(HEADS - 2, 0, False)
                delta(HEADS - 1, 1, True)

            def cc(l):
                pair0 = TILE0[l] // 2

                def mean(n):
                    pe.wait_ge(cc_done, n + 1)
                    for half in range(2):
                        mm = pe.matmul(DB[half][:, :], ones[:, :], uc[:, n, half * HALF:(half + 1) * HALF],
                                       start=(n == 0), stop=(n == KT - 1), skip_group_check=True)
                    mm.then_inc(mean_done, 1)

                first_pair(pair0, in_a, l, 0)
                for t in range(2, 3 * KT):
                    tile(pair0 + t // 2, t % 2, in_a)
                    if t % 3 == 1 and t > 6:
                        mean(t // 3 - 2)
                mean(KT - 2)
                mean(KT - 1)
                pe.wait_ge(sq_added[1], KT // 2)
                for half in range(2):
                    mm = pe.matmul(DB[2 + half][:, :], ones[:, :], sq_sum[1][:, half * HALF:(half + 1) * HALF],
                                   start=True, stop=True)
                mm.then_inc(var_done, 1)

            def swa(l):
                pair0 = TILE0[l] // 2

                def mean_square(e, half, banks):
                    pe.wait_ge(nsq_ready, e + 1)
                    if isinstance(e, int) and e == 1:
                        pe.wait_ge(nln_done, half + 1)
                    pe.matmul(banks[half][:, :], blk[:, :], qs[:, half * HALF:(half + 1) * HALF], start=True, stop=True)\
                        .then_inc(nms_done, 1)

                def heads(n, j, kv, last):
                    sent = [0]

                    def fill(count):
                        if last:
                            return
                        for _ in range(count):
                            s = sent[0]
                            if s == 96:
                                return
                            r, half, k, m = s // 48, s % 48 // 24, s % 24 // 3, s % 3
                            if s % 48 == 0:
                                pe.wait_ge(w_split, 2 * (pair0 + n + 2) + r + 1)
                                pe.wait_ge(pb_free[r], pair0 + n + 2)
                                if r == 0:
                                    pe.wait_ge(nln_done, 2 * n + 4)
                            wl, al = PASSES[m]
                            mm = pe.matmul(PB[r][half][:, :], (w_lo if wl else w_hi)[r][:, k, :],
                                           (a_lo if al else a_hi)[:, k, half * HALF:(half + 1) * HALF],
                                           start=(k == 0 and m == 0), stop=(k == KT - 1 and m == 2),
                                           skip_group_check=True)
                            if s % 48 == 47:
                                mm.then_inc(tile_done, 1)
                            sent[0] += 1

                    def logits(b):
                        e = NB * n + b
                        if b == 0:
                            pe.wait_ge(qn_ready, n + 2)
                        elif b > 1:
                            pe.wait_ge(lg_ready, e - 1)
                        first = max(b - 1, 0)
                        bank = DB[b % 2][:, :].rearrange("p (h c) -> p h c", h=2)
                        pe.matmul(bank[:, :, WINDOW if b == 0 else 0:2 * WINDOW], q_n[j][:, b * WINDOW:(b + 1) * WINDOW],
                                  k_pad[kv][:, :, first * WINDOW:(b + 1) * WINDOW], start=True, stop=True)\
                            .then_inc(lmm_done, 1)

                    def turn(b):
                        e = NB * n + b
                        pe.wait_ge(pr_ready, e + 1)
                        if b:
                            pe.wait_ge(prt_ready, e)
                        for hh in range(2):
                            for part in range(1 if b == 0 else 0, 2):
                                mm = pe.transpose(DB[2][:, (2 * hh + part) * P:(2 * hh + part + 1) * P],
                                                  lg[b % 2][:, hh, part * WINDOW:(part + 1) * WINDOW], ident[:, :])
                        mm.then_inc(trp_done, 1)

                    def values(b):
                        e = NB * n + b
                        pe.wait_ge(prt_ready, e + 1)
                        if b == 4:
                            pe.wait_ge(att_ready, 2 * n + 1)
                        for hh in range(2):
                            for part in range(1 if b == 0 else 0, 2):
                                mm = pe.matmul(DB[3][HD * hh:HD * hh + HD, (b % 4) * P:(b % 4 + 1) * P],
                                               v_tok[:, b - 1 + part, HD * kv:HD * kv + HD],
                                               pr_t[b % 2][:, hh, part, :], start=(part == 0 or b == 0), stop=(part == 1),
                                               skip_group_check=True)
                        mm.then_inc(pv_done, 1)

                    for b in range(NB + 3):
                        if b < NB:
                            logits(b)
                        fill(3)
                        if 2 <= b < NB + 2:
                            turn(b - 2)
                        fill(3)
                        if b > 2:
                            values(b - 3)
                        fill(3 if b < NB else 2)
                        if not last and b == NB - 1:
                            for half in range(2):
                                mean_square(n + 2, half, PB[0])
                    fill(96)

                for n in range(2):
                    if n == 0:
                        first_pair(pair0, in_a, l, 0)
                    else:
                        for j in range(2):
                            tile(pair0 + n, j, in_a)
                    if n == 0:
                        for half in range(2):
                            mean_square(0, half, DB)
                for half in range(2):
                    mean_square(1, half, DB)
                pe.wait_ge(pb_free[1], pair0 + 1)
                for b in range(NB):
                    mm = pe.transpose(DB[2 + b // 4][:, (b % 4) * P:(b % 4 + 1) * P], zs[1][:, b * P:(b + 1) * P],
                                      ident[:, :])
                mm.then_inc(v_turned, 1)
                pe.wait_ge(k_spread, 64)
                pe.wait_ge(k_zeros, 1)
                pe.wait_ge(v_ready, 1)
                with pe.Fori(0, 2) as i:
                    for j in range(2):
                        heads(2 * i + j, j, 0, False)
                for n in range(4, KT):
                    heads(n, n % 2, 1, n == KT - 1)

            pe.wait_ge(const_ready, 1)
            pe.matmul(DB[3][0:QH, 0:BIAS_LEN], rel[:, :], onehot[:, :], start=True, stop=True).then_inc(bias_psum, 1)
            for l in range(LAYERS):
                stats(l + 1)
                if MIXER[l] == "gdn":
                    gdn(l)
                elif MIXER[l] == "cc":
                    cc(l)
                else:
                    swa(l)
                out_projection(l)
                embedding(l)

        @block.scalar
        def _(act):
            def halves(t, off=0):
                return [t[:, off + half * HALF:off + (half + 1) * HALF] for half in range(2)]

            def copy_hi(dst, src):
                return nc.scalar.copy(dst, src)

            for k in range(KT):
                act.dma_start(x_sb[:, k, :], d["x_t"][:, k * T:(k + 1) * T]).then_inc(x_tile_loaded[k], 16)

            def squares(l, k):
                if l == 0:
                    act.wait_ge(x_tile_loaded[k], 16)
                else:
                    act.wait_ge(x_new, OUT * (l - 1) + k + 1)
                if k > 2:
                    act.wait_ge(acc_done, 6 * l + k - 2)
                nc.scalar.activation(((sqt2, sqt)[k % 2] if k else acc)[:, :], x_sb[:, k, :], ACT.Square).then_inc(sq_done, 1)

            def norm(l):
                act.wait_ge(stat_done, l + 1)
                for half in range(2):
                    nc.scalar.activation(halves(sqt)[half], DB[half][:, :], ACT.Ln,
                                         scale=1.0 / D, bias=eps[:, 0:1]).then_inc(rstd_step, 1)
                act.wait_ge(rstd_step, 3 * l + 2)
                nc.scalar.activation(rstd[:, :], sqt[:, :], ACT.Exp, scale=-0.5).then_inc(rstd_step, 1)
                for k in range(KT):
                    act.wait_ge(hf_done, KT * l + k + 1)
                    copy_hi(a_hi[:, k, :], hf[k][:, :]).then_inc(split_hi, 1)

            def reload_x(l):
                act.dma_start(flat(x_sb), d["x_t"] if l == 0 else d["x_save"][l - 1]).then_inc(x_reloaded, 16)

            def out_projection(l):
                if MIXER[l] == "gdn":
                    for k in range(KT):
                        act.wait_ge(o_written, 2 * HEADS * (gdn_slot(l) + 1))
                        copy_hi(b_hi[:, k, :], o_sb[:, k, :]).then_inc(split_hi, 1)
                if MIXER[l] != "cc":
                    act.wait_ge(split_lo, split_at(l, 1, KT))
                    reload_x(l)
                pair0 = (TILE0[l] + LAYER_IN[l]) // 2
                with act.Fori(0, OUT // 2) as i:
                    for j in range(2):
                        act.wait_ge(pb_free[j], pair0 + i + 1)
                        tile_cols = bass.ds((2 * i + j) * T, T)
                        copy_hi(flat(PLACES[MIXER[l]][1][0])[:, tile_cols], x_flat[:, tile_cols]).then_inc(split_hi, 1)

            def embedding(l):
                act.wait_ge(tile_done, TILE0[l] + LAYER_IN[l] + OUT)
                em = PLACES[MIXER[l]][2]
                p_th = em.p_th
                act.dma_start(flat(em.p_raw), d["p_t"][l]).then_inc(p_loaded, 16)
                act.dma_start(em.pw_raw[:, :, :, :].rearrange("p a b c -> p (a b c)"), d["w_embed"][l])\
                    .then_inc(pw_loaded, 16)
                act.wait_ge(p_loaded, 16 * (l + 1))
                copy_hi(flat(em.p_hi), flat(em.p_raw)).then_inc(p_hi_done, 1)
                act.wait_ge(pw_loaded, 16 * (l + 1))
                copy_hi(em.pw_hi[:, :, :, :], em.pw_raw[:, :, :, :]).then_inc(p_hi_done, 1)
                base = TILE0[l] + LAYER_IN[l] + OUT
                for n in range(OUT):
                    act.wait_ge(tile_done, base + n + 1)
                    if n:
                        act.wait_ge(p_t_done, OUT * l + n)
                    for half in range(2):
                        ins = nc.scalar.activation(halves(p_th)[half], PB[n % 2][half][:, :], ACT.Tanh, scale=0.5)
                        if half:
                            ins.then_inc(pb_free[n % 2], 1)
                    if n and l + 1 < LAYERS:
                        squares(l + 1, n - 1)
                    if n and (SPILL[l] or l + 1 == LAYERS):
                        store(l, n - 1)
                if l + 1 < LAYERS:
                    squares(l + 1, OUT - 1)
                if SPILL[l] or l + 1 == LAYERS:
                    store(l, OUT - 1)
                if l + 1 == LAYERS:
                    act.wait_ge(x_stored, 16 * OUT * (1 + sum(SPILL[:l])))

            def store(l, n):
                act.wait_ge(x_new, OUT * l + n + 1)
                to = d["out"] if l + 1 == LAYERS else d["x_save"][l]
                act.dma_start(to[:, n * T:(n + 1) * T], x_sb[:, n, :]).then_inc(x_stored, 16)

            def gdn(l):
                s = gdn_slot(l)
                base, pair0, h0 = TILE0[l], TILE0[l] // 2, HEADS * s
                act.dma_start(flat(wb_raw), d["w_gdn_ba"][s]).then_inc(wb_loaded, 16)
                act.wait_ge(wb_loaded, 16 * (s + 1))
                copy_hi(flat(wb_hi), flat(wb_raw)).then_inc(wb_hi_done, 1)
                def evacuate(h, r, p=0):
                    w = base + 4 * h + r
                    act.wait_ge(tile_done, w + 1)
                    t0 = 3 * (h0 + h) + r
                    if r < 3:
                        if not isinstance(h, int) or t0 > 0:
                            act.wait_ge(conv_done, t0)
                        for half in range(2):
                            ins = copy_hi(halves(c_in, TAPS - 1)[half], PB[r % 2][half][:, :])
                        ins.then_inc(pb_free[r % 2], 1)
                    else:
                        tanh(h, 3)
                        for half in range(2):
                            ins = copy_hi(halves(zb[p])[half], PB[1][half][:, :])
                        ins.then_inc(pb_free[1], 1)

                def tanh(h, r):
                    e = 4 * (h0 + h) + r
                    if not isinstance(h, int) or e:
                        act.wait_ge(silu_done, e)
                    if r < 3:
                        act.wait_ge(conv_done, 3 * (h0 + h) + r + 1)
                        nc.scalar.activation(th[:, :], c_acc[:, :], ACT.Tanh, scale=0.5).then_inc(th_done, 1)
                    else:
                        for half in range(2):
                            ins = nc.scalar.activation(halves(th)[half], PB[1][half][:, :], ACT.Tanh, scale=0.5)
                        ins.then_inc(th_done, 1)

                def k_chunk(h, p, n, kt, turned):
                    e = NCHUNK * (h0 + h) + n
                    if n == 0:
                        act.wait_ge(hv_ready, h0 + h + 1)
                    act.wait_ge(kt_done, e + turned)
                    nc.scalar.activation(kt_sq[:, :], kt, ACT.Square, accum_out=ssk[:, n:n + 1]).then_inc(ssk_done, 1)
                    nc.scalar.activation(k_dec[n // GROUP][:, n % GROUP, :], kt, ACT.Copy,
                                         scale=hv[p][:, EDEC, n:n + 1]).then_inc(kdec_ready, 1)
                    act.wait_ge(kdec_ready, e + 1)

                def decay(h, j):
                    for g in range(2):
                        act.wait_ge(arg_ready, 2 * (h0 + h) + g + 1)
                        for c in range(GROUP):
                            n = GROUP * g + c
                            ins = nc.scalar.activation(dt_m[g][:, c, :], arg[g][:, c, :], ACT.Exp,
                                                       bias=hv[j][:, NGC, n:n + 1])
                        ins.then_inc(dt_ready, 1)

                def output_square(hh, n):
                    e = NCHUNK * hh + n
                    act.wait_ge(o_ready, e + 1)
                    nc.scalar.activation(sq_o[:, :], o_g[n // GROUP][:, n % GROUP, :], ACT.Square,
                                         accum_out=oss[:, n:n + 1]).then_inc(oss_ready, 1)
                    act.wait_ge(oss_ready, e + 1)

                def delta(h, j, last):
                    hh = h0 + h
                    v = hv[j]
                    for g in range(2):
                        act.wait_ge(nt_ready, 2 * hh + g + 1)
                        copy_hi(flat(nt_r[g]), flat(nt[g])).then_inc(ntr_ready, 1)
                    for g in range(2):
                        act.wait_ge(tr_done, 2 * hh + g + 1)
                        for c in range(GROUP):
                            n = GROUP * g + c
                            nc.scalar.activation(kt_sq[:, :], DB[2 * g][:, c * P:(c + 1) * P], ACT.Square,
                                                 accum_out=ssq[:, n:n + 1]).then_inc(ssq_done, 1)
                            act.wait_ge(ssq_done, NCHUNK * hh + n + 1)
                    evacuate(h, 3, j)
                    for lv in range(LEVELS):
                        for g in range(2):
                            act.wait_ge(m_done, 2 * (LEVELS * hh + lv) + g + 1)
                            copy_hi(flat(mt_m[g]), DB[2 * g + 1][:, :]).then_inc(mt_ready, 1)
                        if not last:
                            if lv == 3:
                                evacuate(h + 1, 0)
                            if lv == 5:
                                tanh(h + 1, 0)
                    if not last:
                        evacuate(h + 1, 1)
                    for n in range(NCHUNK):
                        e = NCHUNK * hh + n
                        act.wait_ge(qs_done, e + 1)
                        if n:
                            act.wait_ge(o_ready, e)
                        nc.scalar.activation(qs_sb[:, :], DB[1][:, 0:P], ACT.Copy, scale=v[:, EG, n:n + 1])\
                            .then_inc(qs_ready, 1)
                        act.wait_ge(u_done, e + 1)
                        if n:
                            act.wait_ge(op_done, e)
                        nc.scalar.activation(u_sb[:, :], DB[2][:, 0:P], ACT.Copy, scale=c_tok[:, n:n + 1])\
                            .then_inc(u_ready, 1)
                        if not last:
                            if n == 2:
                                tanh(h + 1, 1)
                            if n == 5:
                                evacuate(h + 1, 2)
                            k_chunk(h + 1, 1 - j, n, DB[2][:, P:2 * P], 1)
                        if n:
                            output_square(hh, n - 1)
                    output_square(hh, NCHUNK - 1)
                    if not last:
                        decay(h + 1, 1 - j)
                        tanh(h + 1, 2)

                evacuate(0, 0)
                act.wait_ge(ba_rows_done, s + 1)
                for half in range(2):
                    ins = copy_hi(ba_rows[:, half * HALF:(half + 1) * HALF], DB[half][0:2 * HEADS, :])
                ins.then_inc(ba_rows_ready, 1)
                tanh(0, 0)
                evacuate(0, 1)
                bb = DB[2][:, 0:2 * 64].rearrange("p (c k) -> p k c", k=16)
                ch = Chain(act, ba_act, 5 * s)
                act.wait_ge(ba_done, s + 1)
                ch.link(nc.scalar.activation(g_t[0][:, :, :], bb[:, 0:HEADS, :], ACT.Tanh, scale=0.5))
                act.wait_ge(ba_step, 5 * s + 2)
                ch.link(nc.scalar.activation(flat(g_t[2]), flat(g_t[1]), ACT.Exp, scale=-1.0))
                ch.link(nc.scalar.activation(flat(g_t[3]), flat(g_t[2]), ACT.Ln, bias=1.0))
                ch.link(nc.scalar.activation(flat(g_t[4]), a_log[:, s, :, :].rearrange("p a b -> p (a b)"), ACT.Exp))
                tanh(0, 1)
                evacuate(0, 2)
                act.wait_ge(gcum_done, s + 1)
                gc = DB[3][:, 0:64].rearrange("p (h c) -> p h c", h=HEADS)
                gl = DB[3][:, 64:128].rearrange("p (h c) -> p h c", h=HEADS)
                nc.scalar.activation(tok[:, :, NGC, :], gc, ACT.Copy, scale=-1.0)
                nc.scalar.activation(tok[:, :, EG, :], gc, ACT.Exp)
                nc.scalar.activation(tok[:, :, EGL, :], gl, ACT.Exp)
                ch.link(nc.scalar.activation(g_t[1][:, :, :], gl, ACT.Copy))
                ch.end(5)
                act.wait_ge(ba_step, 5 * s + 4)
                nc.scalar.activation(tok[:, :, EDEC, :], g_t[2][:, :, :], ACT.Exp).then_inc(tok_done, 1)
                for n in range(NCHUNK):
                    c = n % GROUP
                    k_chunk(0, 0, n, DB[2 + n // GROUP][:, c * P:(c + 1) * P], GROUP - c)
                decay(0, 0)
                tanh(0, 2)
                with act.Fori(0, (HEADS - 2) // 2) as i:
                    for j in range(2):
                        delta(2 * i + j, j, False)
                delta(HEADS - 2, 0, False)
                delta(HEADS - 1, 1, True)

            def cc(l):
                base, pair0 = TILE0[l], TILE0[l] // 2

                def gate_tanh(n):
                    t = 3 * n + 1
                    act.wait_ge(tile_done, base + t + 1)
                    if n:
                        act.wait_ge(pb_free[(t - 4) % 2], pair0 + (t - 4) // 2 + 1)
                    for half in range(2):
                        ins = nc.scalar.activation(halves(cc_th)[half], PB[t % 2][half][:, :], ACT.Tanh, scale=0.5)
                    ins.then_inc(pb_free[t % 2], 1)

                def gate(n):
                    t = 3 * n + 2
                    act.wait_ge(tile_done, base + t + 1)
                    for half in range(2):
                        ins = nc.scalar.activation(cc_gate[:, n, half * HALF:(half + 1) * HALF], PB[t % 2][half][:, :],
                                                   ACT.Silu)
                    ins.then_inc(pb_free[t % 2], 1)

                gate_tanh(0)
                act.wait_ge(x_stored, 16 * OUT * sum(SPILL[:l]))
                for n in range(KT):
                    act.wait_ge(pb_free[3 * n % 2], pair0 + 3 * n // 2 + 1)
                    if n > 1:
                        act.wait_ge(cc_done, n - 1)
                    for i in range(CC_SHARED):
                        if i == 4:
                            gate(n)
                        if i > 2:
                            act.wait_ge(cc_added, (CC_SHARED - 1) * n + i - 2)
                        elif i and n:
                            act.wait_ge(cc_added, (CC_SHARED - 1) * n)
                        nc.scalar.activation((scaled_tap[i % 2] if i else shared[n % 2])[:, :],
                                             u_in[n % 2][:, i:i + T], ACT.Copy, scale=cc_w[:, n, i:i + 1])\
                            .then_inc(cc_product, 1)
                    if n + 1 < KT:
                        gate_tanh(n + 1)
                act.wait_ge(mean_done, KT)
                for half in range(2):
                    ins = nc.scalar.activation(halves(mu)[half], DB[half][:, :], ACT.Copy, scale=1.0 / D)
                ins.then_inc(mu_ready, 1)
                for n in range(KT):
                    act.wait_ge(centred, n + 1)
                    if n > 3:
                        act.wait_ge(sq_added[n % 2], n // 2 - 1)
                    nc.scalar.activation((u_sq if n > 1 else sq_sum)[n % 2][:, :], uc[:, n, :], ACT.Square)\
                        .then_inc(cc_sq_ready, 1)
                act.wait_ge(var_done, 1)
                reload_x(l)
                for half in range(2):
                    nc.scalar.activation(halves(cc_sq)[half], DB[2 + half][:, :], ACT.Ln, scale=1.0 / D,
                                         bias=ln_eps[:, 0:1]).then_inc(cc_rstd_step, 1)
                act.wait_ge(cc_rstd_step, 2)
                nc.scalar.activation(cc_rstd[:, :], cc_sq[:, :], ACT.Exp, scale=-0.5).then_inc(cc_rstd_step, 1)

                def high(k):
                    act.wait_ge(gated_u, k + 1)
                    copy_hi(a_hi[:, k, :], uc[:, k, :]).then_inc(split_hi, 1)

                for k in range(KT):
                    act.wait_ge(scaled_u, k + 1)
                    nc.scalar.activation(uc[:, k, :], uc[:, k, :], ACT.Silu, bias=cc_par[:, LN_B, k:k + 1],
                                         scale=cc_par[:, LN_G, k:k + 1]).then_inc(silu_u, 1)
                    if k:
                        high(k - 1)
                high(KT - 1)

            def swa(l):
                base = TILE0[l]

                def raw_and_square(e, w, dst):
                    act.wait_ge(tile_done, w + 1)
                    if not isinstance(e, int) or e:
                        act.wait_ge(qn_ready, e)
                    for half in range(2):
                        ins = copy_hi(halves(dst)[half], PB[0][half][:, :])
                    ins.then_inc(pb_free[0], 1)
                    for half in range(2):
                        ins = nc.scalar.activation(halves(qs)[half], PB[0][half][:, :], ACT.Square)
                    ins.then_inc(nsq_ready, 1)

                def log_mean(e, half, banks):
                    act.wait_ge(nms_done, 2 * e + half + 1)
                    nc.scalar.activation(halves(qs)[half], banks[half][:, :], ACT.Ln, bias=eps[:, 0:1]).then_inc(nln_done, 1)
                    if half:
                        act.wait_ge(nln_done, 2 * e + 2)
                        nc.scalar.activation(qs[:, :], qs[:, :], ACT.Exp, scale=-0.5).then_inc(nrr_ready, 1)

                def gate_tanh(n, w, p):
                    act.wait_ge(tile_done, w + 1)
                    for half in range(2):
                        ins = nc.scalar.activation(halves(zs[p])[half], PB[1][half][:, :], ACT.Tanh, scale=0.5)
                    ins.then_inc(gth_done, 1)

                def load_bias(n, p):
                    act.dma_start(bias[:, p, :, :],
                                  bias_window(n)).then_inc(bias_loaded[p], 16)

                def exps(n, b):
                    e, s = NB * n + b, sm[b % 2]
                    keys = slice(WINDOW if b == 0 else 0, 2 * WINDOW)
                    act.wait_ge(mx_ready, e + 1)
                    nc.scalar.activation(s[:, ESK, :], s[:, SK, :], ACT.Exp).then_inc(esk_ready, 1)
                    for hh in range(2):
                        ins = nc.scalar.activation(lg[b % 2][:, hh, keys], lg[b % 2][:, hh, keys], ACT.Exp,
                                                   bias=s[:, NEG_M, hh:hh + 1], accum_out=s[:, ES, hh:hh + 1])
                        ins.then_inc(e_ready, 1)

                def turned(n, b):
                    act.wait_ge(trp_done, NB * n + b + 1)
                    if b > 1:
                        act.wait_ge(pv_done, NB * n + b - 1)
                    bank = DB[2][:, :].rearrange("p (h a i) -> p h a i", h=2, a=2)
                    part = slice(1 if b == 0 else 0, 2)
                    copy_hi(pr_t[b % 2][:, :, part, :], bank[:, :, part, :]).then_inc(prt_ready, 1)

                def high(n, m, p):
                    act.wait_ge(att_ready, 2 * n + m + 1)
                    cols = bass.ds(n * T + m * HALF, HALF)
                    copy_hi(b_hi_flat[:, cols], halves(zs[p])[m]).then_inc(split_hi if m else half_hi, 1)

                def heads(n, j, last):
                    for b in range(NB):
                        exps(n, b)
                        if b > 1:
                            turned(n, b - 2)
                        if b == 6 and not last:
                            raw_and_square(n + 2, base + 2 * (n + 2), q_n[1 - j])
                        if b == 7:
                            high(n, 0, j)
                    turned(n, NB - 2)
                    if not last:
                        for half in range(2):
                            log_mean(n + 2, half, PB[0])
                    turned(n, NB - 1)
                    high(n, 1, j)
                    if not last:
                        gate_tanh(n + 1, base + 2 * (n + 2) + 1, 1 - j)

                act.wait_ge(bias_spread, 16)
                act.wait_ge(split_lo, split_at(l, 0, KT))
                act.wait_ge(x_stored, 16 * OUT * sum(SPILL[:l]))
                load_bias(0, 0)
                load_bias(1, 1)
                raw_and_square(0, base, q_n[1])
                act.wait_ge(tile_done, base + 2)
                for half in range(2):
                    ins = copy_hi(halves(zs[1])[half], PB[1][half][:, :])
                ins.then_inc(pb_free[1], 1)
                for half in range(2):
                    log_mean(0, half, DB)
                act.wait_ge(qn_ready, 1)
                for kv in range(2):
                    for hh in range(2):
                        act.dma_start(k_pad[kv][HD * hh:HD * hh + HD, hh, :], q_n[1][HD * kv:HD * kv + HD, :])\
                            .then_inc(k_spread, 16)
                raw_and_square(1, base + 2, q_n[0])
                for half in range(2):
                    log_mean(1, half, DB)
                act.wait_ge(v_turned, 1)
                for m in range(2):
                    ins = copy_hi(v_tok[:, 4 * m:4 * m + 4, :], DB[2 + m][:, :].rearrange("p (b i) -> p b i", b=4))
                ins.then_inc(v_ready, 1)
                gate_tanh(0, base + 3, 0)
                act.wait_ge(k_spread, 64)
                with act.Fori(0, 3) as i:
                    for j in range(2):
                        heads(2 * i + j, j, False)
                        act.wait_ge(lg_ready, NB * (2 * i + j + 1))
                        load_bias(2 * i + j + 2, j)
                heads(KT - 2, 0, False)
                heads(KT - 1, 1, True)

            def bias_window(n):
                return d["bias_window"][:, bass.ds(2 * n, 2), :]

            for k in range(KT):
                squares(0, k)
            act.wait_ge(bias_sum, 1)
            act.dma_start(d["bias_rows"], bias_rows[:, :]).then_inc(bias_stored, 16)
            act.wait_ge(bias_stored, 16)
            act.dma_start(d["bias_copies"], d["bias_rows"].unsqueeze(1).to_broadcast([QH, P, BIAS_LEN]))\
                .then_inc(bias_spread, 16)
            for l in range(LAYERS):
                norm(l)
                if MIXER[l] == "gdn":
                    gdn(l)
                elif MIXER[l] == "cc":
                    cc(l)
                else:
                    swa(l)
                out_projection(l)
                embedding(l)

        @block.vector
        def _(dve):
            def halves(t, off=0):
                return [t[:, off + half * HALF:off + (half + 1) * HALF] for half in range(2)]

            dve.wait_ge(const_loaded, 16 * len(CONSTS))
            nc.vector.memset(half_e[:, :], 0.5)
            nc.vector.memset(mhalf_e[:, :], -0.5)
            nc.vector.memset(eps[:, :], RMS_EPS)
            nc.vector.memset(ln_eps[:, :], LN_EPS)
            nc.vector.tensor_copy(level_mask[:, :, :], mask_stage[:, 0:LEVELS, :])
            nc.vector.tensor_copy(strict[:, :], mask_stage[:, LEVELS, :])
            nc.vector.tensor_scalar(cc_w[:, :, :], cc_w[:, :, :], 0.5, None, ALU.mult)
            nc.vector.tensor_scalar(gdn_gh[:, :, :], gdn_g[:, :, :], 0.5, None, ALU.mult)
            nc.vector.tensor_copy(ones_r[:, :], ones[:, :])
            nc.vector.tensor_copy(ident_r[:, :], ident[:, :]).then_inc(const_ready, 1)

            def accumulate(l, k):
                if k in (0, KT - 1):
                    return
                dve.wait_ge(sq_done, KT * l + k + 1)
                if k > 1:
                    dve.wait_ge(acc_done, 6 * l + k - 1)
                nc.vector.tensor_tensor(acc[:, :], acc[:, :], (sqt2, sqt)[k % 2][:, :], ALU.add).then_inc(acc_done, 1)

            def norm(l):
                dve.wait_ge(rstd_step, 3 * (l + 1))
                for k in range(KT):
                    nc.vector.scalar_tensor_tensor(hf[k][:, :], x_sb[:, k, :], norm_g[:, l, k:k + 1],
                                                   rstd[:, :], ALU.mult, ALU.mult).then_inc(hf_done, 1)
                for k in range(KT):
                    dve.wait_ge(hf_done, KT * l + k + 1)
                    dve.wait_ge(split_hi, split_at(l, 0, k) + 1)
                    nc.vector.tensor_tensor(a_lo[:, k, :], hf[k][:, :], a_hi[:, k, :].bitcast(F32),
                                            ALU.subtract).then_inc(split_lo, 1)

            def out_projection(l):
                pair0 = (TILE0[l] + LAYER_IN[l]) // 2
                if MIXER[l] == "gdn":
                    for k in range(KT):
                        dve.wait_ge(split_hi, split_at(l, 1, k) + 1)
                        nc.vector.tensor_tensor(b_lo[:, k, :], o_sb[:, k, :], b_hi[:, k, :].bitcast(F32),
                                                ALU.subtract).then_inc(split_lo, 1)
                dve.wait_ge(x_reloaded, 16 * (l + 1))
                with dve.Fori(0, OUT // 2) as i:
                    for j in range(2):
                        dve.wait_ge(tile_done, 2 * (pair0 + i) + j + 1)
                        for half in range(2):
                            cols = bass.ds((2 * i + j) * T + half * HALF, HALF)
                            ins = nc.vector.tensor_tensor(x_flat[:, cols], x_flat[:, cols], PB[j][half][:, :],
                                                          ALU.add)
                        ins.then_inc(pb_free[j], 1)
                        dve.wait_ge(split_hi, split_at(l, 2, 2 * i + j) + 1)
                        cols = bass.ds((2 * i + j) * T, T)
                        hi, lo = (flat(t) for t in PLACES[MIXER[l]][1])
                        nc.vector.tensor_tensor(lo[:, cols], x_flat[:, cols], hi[:, cols].bitcast(F32),
                                                ALU.subtract).then_inc(split_lo, 1)

            def embedding(l):
                dve.wait_ge(p_hi_done, 2 * l + 1)
                em = PLACES[MIXER[l]][2]
                p_th, p_t = em.p_th, em.p_t
                nc.vector.tensor_tensor(flat(em.p_lo), flat(em.p_raw), flat(em.p_hi).bitcast(F32),
                                        ALU.subtract).then_inc(p_split, 1)
                dve.wait_ge(p_hi_done, 2 * l + 2)
                nc.vector.tensor_tensor(flat4(em.pw_lo), flat4(em.pw_raw), flat4(em.pw_hi).bitcast(F32),
                                        ALU.subtract).then_inc(p_split, 1)
                pair0 = (TILE0[l] + LAYER_IN[l] + OUT) // 2
                for n in range(OUT):
                    dve.wait_ge(pb_free[n % 2], pair0 + n // 2 + 1)
                    dve.wait_ge(pp_done, OUT * l + n + 1)
                    if n:
                        dve.wait_ge(x_new, OUT * l + n)
                    for half in range(2):
                        cols = slice(half * HALF, (half + 1) * HALF)
                        ins = nc.vector.scalar_tensor_tensor(p_t[:, cols], p_th[:, cols], 1.0,
                                                             DB[2 * (n % 2) + half][:, :], ALU.add, ALU.mult)
                    ins.then_inc(p_t_done, 1)
                    dve.wait_ge(p_t_done, OUT * l + n + 1)
                    nc.vector.scalar_tensor_tensor(x_sb[:, n, :], p_t[:, :], 0.5, x_sb[:, n, :], ALU.mult,
                                                   ALU.add).then_inc(x_new, 1)
                    if n and l + 1 < LAYERS:
                        accumulate(l + 1, n - 1)
                if l + 1 < LAYERS:
                    accumulate(l + 1, OUT - 1)

            def gdn(l):
                s = gdn_slot(l)
                pair0, h0 = TILE0[l] // 2, HEADS * s
                dve.wait_ge(wb_hi_done, s + 1)
                nc.vector.tensor_tensor(flat(wb_lo), flat(wb_raw), flat(wb_hi).bitcast(F32),
                                        ALU.subtract).then_inc(wb_split, 1)
                def conv(h, r, q, p):
                    hh = h0 + h
                    out = [kq[p][:, :, 0, :], kq[p][:, :, 1, :], vb[p][:, :], zb[p][:, :]][r]
                    if q == 4:
                        dve.wait_ge(th_done, 4 * hh + r + 1)
                        if r == 3:
                            dve.wait_ge(pb_free[1], pair0 + 2 * h + 2)
                            nc.vector.scalar_tensor_tensor(out, th[:, :], 1.0, zb[p][:, :], ALU.add,
                                                           ALU.mult).then_inc(silu_done, 1)
                            return
                        a, b = th[:, :], c_acc[:, :]
                        if r < 2:
                            a, b = (t.rearrange("p (n c) -> p n c", c=CHUNK) for t in (a, b))
                        nc.vector.scalar_tensor_tensor(out, a, 1.0, b, ALU.add, ALU.mult).then_inc(silu_done, 1)
                        return
                    if q == 0:
                        if r == 0:
                            nc.vector.tensor_copy(cw[:, :, :].rearrange("p a b -> p (a b)"),
                                                  conv_flat[:, bass.ds((h0 + h) * 3 * TAPS, 3 * TAPS)])\
                                .then_inc(cw_ready, 1)
                            dve.wait_ge(cw_ready, hh + 1)
                        dve.wait_ge(pb_free[r % 2], pair0 + 2 * h + r // 2 + 1)
                        if r or not isinstance(hh, int) or hh:
                            dve.wait_ge(silu_done, 4 * hh + r)
                        nc.vector.tensor_scalar(c_acc[:, :], c_in[:, TAPS - 1:TAPS - 1 + T],
                                                cw[:, r, TAPS - 1:TAPS], None, ALU.mult).then_inc(conv_step, 1)
                        return
                    t = TAPS - 1 - q
                    dve.wait_ge(conv_step, 9 * hh + 3 * r + q)
                    nc.vector.scalar_tensor_tensor(c_acc[:, :], c_in[:, t:t + T], cw[:, r, t:t + 1], c_acc[:, :],
                                                   ALU.mult, ALU.add)\
                        .then_inc(conv_done if q == TAPS - 1 else conv_step, 1)

                def token_values(h, p):
                    nc.vector.tensor_copy(flat(hv[p]), tok_flat[:, bass.ds(h * KINDS * NCHUNK, KINDS * NCHUNK)])\
                        .then_inc(hv_ready, 1)

                def log_decays(h, p, groups):
                    hh = h0 + h
                    dve.wait_ge(hv_ready, hh + 1)
                    if 0 in groups:
                        nc.vector.tensor_copy(gg_hi[:, :], hv[p][:, GG, :]).then_inc(gg_step, 1)
                        dve.wait_ge(gg_step, 2 * hh + 1)
                        nc.vector.tensor_tensor(gg_lo[:, :], hv[p][:, GG, :], gg_hi[:, :].bitcast(F32), ALU.subtract)\
                            .then_inc(gg_step, 1)
                    dve.wait_ge(gg_step, 2 * hh + 2)
                    for g in groups:
                        for part, gg in ((u_hi, gg_hi[:, :].bitcast(F32)), (u_lo, gg_lo[:, :])):
                            ins = nc.vector.tensor_tensor(
                                part[g][:, :, :], cum_u[:, :].unsqueeze(1).to_broadcast([P, GROUP, P]),
                                gg[:, GROUP * g:GROUP * g + GROUP].unsqueeze(2).to_broadcast([P, GROUP, P]), ALU.mult)
                        ins.then_inc(ug_ready, 1)

                def rows(h, g):
                    dve.wait_ge(rowg_done, 2 * (h0 + h) + g + 1)
                    nc.vector.tensor_tensor(arg[g][:, :, :], DB[g][:, :].rearrange("p (c i) -> p c i", c=GROUP),
                                            mask_t[:, :].unsqueeze(1).to_broadcast([P, GROUP, P]), ALU.add)\
                        .then_inc(arg_ready, 1)

                def norms(h, p):
                    hh = h0 + h
                    dve.wait_ge(ssk_done, NCHUNK * (hh + 1))
                    nc.vector.tensor_scalar(ssk[:, :], ssk[:, :], 4 * RMS_EPS, None, ALU.add).then_inc(ss_read, 1)
                    dve.wait_ge(ss_read, hh + 1)
                    ch = Chain(dve, dve_step, 2 * hh)
                    ch.link(nc.vector.reciprocal(c_tok[:, :], ssk[:, :]))
                    ch.link(nc.vector.tensor_tensor(c_tok[:, :], c_tok[:, :], hv[p][:, BETA, :], ALU.mult))
                    ch.end(2)

                def delta(h, j, last):
                    hh, v, nj = h0 + h, hv[j], 1 - j

                    def conv_next(*steps):
                        if not last:
                            for r, q in steps:
                                conv(h + 1, r, q, nj)

                    for g in range(2):
                        dve.wait_ge(gram_done, 2 * hh + g + 1)
                        dve.wait_ge(dt_ready, 2 * hh + g + 1)
                        for b in range(2):
                            qk = DB[2 * g + b][:, :].rearrange("p (c m i) -> p c m i", c=2, m=2)[:, :, 1, :]
                            nc.vector.tensor_tensor(p_t_m[g][:, 2 * b:2 * b + 2, :], qk, dt_m[g][:, 2 * b:2 * b + 2, :],
                                                    ALU.mult)
                        dve.wait_ge(dts_ready, 2 * hh + g + 1)
                        for c in range(GROUP):
                            ins = nc.vector.scalar_tensor_tensor(
                                nt[g][:, c, :], DB[2 * g + c // 2][:, (c % 2) * 256:(c % 2) * 256 + P],
                                c_tok[:, GROUP * g + c:GROUP * g + c + 1], dts[g][:, c, :], ALU.mult, ALU.mult)
                        ins.then_inc(nt_ready, 1)
                    dve.wait_ge(sqrt_done, hh + 1)
                    for g in range(2):
                        dve.wait_ge(tr_done, 2 * hh + g + 1)
                        nc.vector.scalar_tensor_tensor(
                            r_v[g][:, :, :], DB[2 * g + 1][:, :].rearrange("p (c i) -> p c i", c=GROUP), 0.5,
                            sq_tk[:, GROUP * g:GROUP * g + GROUP].unsqueeze(2).to_broadcast([P, GROUP, P]),
                            ALU.mult, ALU.mult).then_inc(rv_ready, 1)
                    for lv in range(LEVELS):
                        fillers = {4: [(0, 0), (0, 1)], 5: [(0, 2), (0, 3)], 6: [(0, 4)]}.get(lv, [])
                        for g in range(2):
                            e = 2 * (LEVELS * hh + lv) + g
                            dve.wait_ge(pm_done, e + 1)
                            nc.vector.tensor_tensor(p_m[g][:, :, :], DB[2 * g][:, :].rearrange("p (c i) -> p c i", c=GROUP),
                                                    level_mask[:, lv, :].unsqueeze(1).to_broadcast([P, GROUP, P]),
                                                    ALU.mult).then_inc(p_ready, 1)
                        conv_next(*fillers)
                        if lv == 1:
                            conv(h, 3, 4, j)
                            for g in range(2):
                                dve.wait_ge(ntr_ready, 2 * hh + g + 1)
                                nc.vector.tensor_tensor(flat(nt_lo[g]), flat(nt[g]), flat(nt_r[g]).bitcast(F32),
                                                        ALU.subtract).then_inc(ntlo_ready, 1)
                            dve.wait_ge(ssq_done, NCHUNK * (hh + 1))
                            nc.vector.tensor_scalar(tq[:, :], ssq[:, :], RMS_EPS * CHUNK, 4 * RMS_EPS * RMS_EPS * CHUNK,
                                                    ALU.mult, ALU.add).then_inc(tq_ready, 1)
                            dve.wait_ge(tq_ready, hh + 1)
                        if lv == LEVELS - 1 and not last:
                            token_values(h + 1, nj)
                        for g in range(2):
                            e = 2 * (LEVELS * hh + lv) + g
                            if lv == 0:
                                dve.wait_ge(p_ready, e + 1)
                                nc.vector.tensor_tensor(m_m[g][:, :, :], p_m[g][:, :, :].bitcast(F32),
                                                        ident[:, :].unsqueeze(1).to_broadcast([P, GROUP, P]),
                                                        ALU.add).then_inc(m_ready, 1)
                            else:
                                dve.wait_ge(m_done, e + 1)
                                nc.vector.tensor_tensor(flat(m_m[g]), flat(m_m[g]).bitcast(F32), DB[2 * g][:, :],
                                                        ALU.add).then_inc(m_ready, 1)
                    conv_next((1, 0), (1, 1))
                    for g in range(2):
                        dve.wait_ge(m_ready, 2 * (LEVELS * hh + LEVELS - 1) + g + 1)
                        dve.wait_ge(y_done, 2 * hh + g + 1)
                        nc.vector.scalar_tensor_tensor(
                            y_m[g][:, :, :], DB[2 * g][:, :].rearrange("p (c i) -> p c i", c=GROUP), -1.0,
                            ident[:, :].unsqueeze(1).to_broadcast([P, GROUP, P]), ALU.mult, ALU.add)\
                            .then_inc(y_ready, 1)
                    for g in range(2):
                        dve.wait_ge(t_done, 2 * hh + g + 1)
                        nc.vector.tensor_tensor(flat(tt[g]), flat(mt_m[g]).bitcast(F32), DB[2 * g + 1][:, :],
                                                ALU.add).then_inc(tt_ready, 1)
                    nc.vector.memset(state[:, :], 0.0).then_inc(s_ready, 1)
                    for n in range(NCHUNK):
                        g, c, e = n // GROUP, n % GROUP, NCHUNK * hh + n
                        dve.wait_ge(ks_done, e + 1)
                        nc.vector.scalar_tensor_tensor(r4[:, :], DB[0][:, 0:P], v[:, NEG_EG, n:n + 1], r_v[g][:, c, :],
                                                       ALU.mult, ALU.add).then_inc(r4_ready, 1)
                        conv_next(*{0: [(1, 2)], 1: [(1, 3)], 3: [(1, 4)], 6: [(2, 0)], 7: [(2, 1)]}.get(n, []))
                        if n == 2 and not last:
                            log_decays(h + 1, nj, (0,))
                        if n == 4 and not last:
                            log_decays(h + 1, nj, (1,))
                        if n < NCHUNK - 1:
                            dve.wait_ge(ds_done, (NCHUNK - 1) * hh + n + 1)
                            dve.wait_ge(s_ready, e + 1)
                            nc.vector.scalar_tensor_tensor(state[:, :], state[:, :], v[:, EGL, n:n + 1], DB[3][:, 0:P],
                                                           ALU.mult, ALU.add).then_inc(s_ready, 1)
                        dve.wait_ge(op_done, e + 1)
                        nc.vector.tensor_tensor(o_g[g][:, c, :], DB[1][:, 0:P], qs_sb[:, :], ALU.add)\
                            .then_inc(o_ready, 1)
                        if n == 7 and not last:
                            rows(h + 1, 0)
                        if n == 5 or n == 7:
                            m = slice(0, GROUP) if n == 5 else slice(GROUP, NCHUNK)
                            dve.wait_ge(oss_ready, NCHUNK * hh + m.stop)
                            nc.vector.scalar_tensor_tensor(om[:, m], oss[:, m], 1.0 / P, tq[:, m], ALU.mult,
                                                           ALU.add).then_inc(om_ready, 1)
                    if not last:
                        rows(h + 1, 1)
                        norms(h + 1, nj)
                    conv_next((2, 2))
                    for g in range(2):
                        dve.wait_ge(osc_ready, 2 * hh + g + 1)
                        dve.wait_ge(o_ready, NCHUNK * hh + GROUP * (g + 1))
                        nc.vector.tensor_tensor(o_g[g][:, :, :], o_g[g][:, :, :],
                                                osc[:, GROUP * g:GROUP * g + GROUP].unsqueeze(2)
                                                .to_broadcast([P, GROUP, P]), ALU.mult).then_inc(on_ready, 1)
                    conv_next((2, 3))
                    for g in range(2):
                        dve.wait_ge(ot_done, 2 * hh + g + 1)
                        nc.vector.scalar_tensor_tensor(o_flat[:, bass.ds(h * T + g * HALF, HALF)], DB[2 + g][:, :],
                                                       gdn_gh[:, s, :], zb[j][:, g * HALF:(g + 1) * HALF],
                                                       ALU.mult, ALU.mult).then_inc(o_written, 1)
                    conv_next((2, 4))

                nc.vector.memset(c_in[:, 0:TAPS - 1], 0.0).then_inc(pad_ready, 1)
                dve.wait_ge(pad_ready, s + 1)
                for q in range(5):
                    conv(0, 0, q, 0)
                for q in range(4):
                    conv(0, 1, q, 0)
                aa = DB[2][:, 0:2 * 64].rearrange("p (c k) -> p k c", k=16)[:, HEADS:2 * HEADS, :]
                ch = Chain(dve, ba_step, 5 * s)
                dve.wait_ge(ba_act, 5 * s + 1)
                ch.link(nc.vector.tensor_tensor(g_t[5][:, :, :], aa, dt_b[:, s, :, :], ALU.add))
                ch.link(nc.vector.scalar_tensor_tensor(flat(g_t[1]), flat(g_t[5]), -1.0, flat(g_t[5]), ALU.mult,
                                                       ALU.max))
                dve.wait_ge(ba_act, 5 * s + 4)
                ch.link(nc.vector.scalar_tensor_tensor(flat(g_t[1]), flat(g_t[5]), 0.0, flat(g_t[3]), ALU.max,
                                                       ALU.add))
                nc.vector.scalar_tensor_tensor(flat(g_t[5]), flat(g_t[1]), -1.0, flat(g_t[4]), ALU.mult,
                                               ALU.mult).then_inc(g_ready, 1)
                nc.vector.tensor_scalar(tok[:, :, BETA, :], g_t[0][:, :, :], 0.5, 0.5, ALU.mult, ALU.add)
                dve.wait_ge(g_ready, s + 1)
                nc.vector.tensor_copy(tok[:, :, GG, :], g_t[5][:, :, :])
                conv(0, 1, 4, 0)
                dve.wait_ge(ba_act, 5 * s + 5)
                gc = DB[3][:, 0:64].rearrange("p (h c) -> p h c", h=HEADS)
                ch.link(nc.vector.tensor_tensor(g_t[2][:, :, :], g_t[1][:, :, :], gc, ALU.subtract))
                ch.link(nc.vector.tensor_scalar(tok[:, :, NEG_EG, :], tok[:, :, EG, :], -1.0, None, ALU.mult))
                ch.end(5)
                dve.wait_ge(tok_done, s + 1)
                token_values(0, 0)
                log_decays(0, 0, (0, 1))
                conv(0, 2, 0, 0)
                conv(0, 2, 1, 0)
                rows(0, 0)
                rows(0, 1)
                conv(0, 2, 2, 0)
                conv(0, 2, 3, 0)
                norms(0, 0)
                conv(0, 2, 4, 0)
                if any(SPILL[:l]):
                    dve.wait_ge(x_stored, 16 * OUT * sum(SPILL[:l]))
                with dve.Fori(0, (HEADS - 2) // 2) as i:
                    for j in range(2):
                        delta(2 * i + j, j, False)
                delta(HEADS - 2, 0, False)
                delta(HEADS - 1, 1, True)

            def cc(l):
                pair0 = TILE0[l] // 2
                for j in range(2):
                    ins = nc.vector.memset(u_in[j][:, 0:PAD], 0.0)
                ins.then_inc(cc_pad, 1)
                dve.wait_ge(cc_pad, 1)

                def combine(n):
                    dve.wait_ge(tap, (CC_TAPS - CC_SHARED - 1) * (n + 1))
                    dve.wait_ge(cc_added, (CC_SHARED - 1) * (n + 1))
                    nc.vector.tensor_tensor(uc[:, n, :], uc[:, n, :], shared[n % 2][:, :], ALU.add).then_inc(cc_done, 1)

                for n in range(KT):
                    u = u_in[n % 2]
                    t, j = 3 * n, 3 * n % 2
                    dve.wait_ge(tile_done, 2 * pair0 + t + 1)
                    dve.wait_ge(pb_free[1 - j], pair0 + (t + 1) // 2 + 1)
                    if n > 1:
                        dve.wait_ge(cc_done, n - 1)
                    for half in range(2):
                        cols = slice(half * HALF, (half + 1) * HALF)
                        ins = nc.vector.scalar_tensor_tensor(u[:, PAD + half * HALF:PAD + (half + 1) * HALF],
                                                             cc_th[:, cols], 1.0, PB[j][half][:, :], ALU.add, ALU.mult)
                    ins.then_inc(pb_free[j], 1)
                    dve.wait_ge(pb_free[j], pair0 + t // 2 + 1)
                    t = CC_TAPS - 1
                    nc.vector.tensor_scalar(uc[:, n, :], u[:, t:t + T], cc_w[:, n, t:t + 1],
                                            cc_par[:, CC_B, n:n + 1], ALU.mult, ALU.add).then_inc(cc_u_ready, 1)
                    dve.wait_ge(cc_u_ready, n + 1)
                    for t in range(CC_TAPS - 2, CC_SHARED - 1, -1):
                        nc.vector.scalar_tensor_tensor(uc[:, n, :], u[:, t:t + T], cc_w[:, n, t:t + 1],
                                                       uc[:, n, :], ALU.mult, ALU.add).then_inc(tap, 1)
                        dve.wait_ge(tap, (CC_TAPS - CC_SHARED - 1) * n + CC_TAPS - 1 - t)
                        if n and t == CC_TAPS - 5:
                            combine(n - 1)
                combine(KT - 1)
                dve.wait_ge(mu_ready, 1)
                for n in range(KT):
                    nc.vector.tensor_tensor(uc[:, n, :], uc[:, n, :], mu[:, :], ALU.subtract).then_inc(centred, 1)
                    k = n if n == KT - 1 else n - 1
                    if n > 3 and k % 2:
                        dve.wait_ge(cc_sq_ready, k + 1)
                        if k > 3:
                            dve.wait_ge(sq_added[1], k // 2 - 1)
                        nc.vector.tensor_tensor(sq_sum[1][:, :], sq_sum[1][:, :], u_sq[1][:, :], ALU.add)\
                            .then_inc(sq_added[1], 1)
                for j in range(2):
                    dve.wait_ge(sq_added[j], KT // 2 - 1)
                nc.vector.tensor_tensor(sq_sum[1][:, :], sq_sum[1][:, :], sq_sum[0][:, :], ALU.add)\
                    .then_inc(sq_added[1], 1)
                dve.wait_ge(cc_rstd_step, 3)
                dve.wait_ge(tile_done, TILE0[l] + LAYER_IN[l])

                def scale(k):
                    dve.wait_ge(centred, k + 1)
                    nc.vector.tensor_tensor(uc[:, k, :], uc[:, k, :], cc_rstd[:, :], ALU.mult).then_inc(scaled_u, 1)

                def low(k):
                    dve.wait_ge(split_hi, split_at(l, 1, k) + 1)
                    nc.vector.tensor_tensor(a_lo[:, k, :], uc[:, k, :], a_hi[:, k, :].bitcast(F32), ALU.subtract)\
                        .then_inc(split_lo, 1)

                scale(0)
                for k in range(KT):
                    if k + 1 < KT:
                        scale(k + 1)
                    if k:
                        low(k - 1)
                low(KT - 1)

            def swa(l):
                pair0 = TILE0[l] // 2

                def normed(e, dst, g):
                    dve.wait_ge(nrr_ready, e + 1)
                    nc.vector.scalar_tensor_tensor(dst[:, :], dst[:, :], qk_g[:, g:g + 1], qs[:, :], ALU.mult, ALU.mult)\
                        .then_inc(qn_ready, 1)

                def gate(n, p):
                    dve.wait_ge(gth_done, n + 1)
                    for half in range(2):
                        z = halves(zs[p])[half]
                        ins = nc.vector.scalar_tensor_tensor(z, z, 1.0, PB[1][half][:, :], ALU.add, ALU.mult)
                    ins.then_inc(pb_free[1], 1)

                def soft(n, b, j):
                    e, s = NB * n + b, sm[b % 2]
                    keys = slice(WINDOW if b == 0 else 0, 2 * WINDOW)
                    dve.wait_ge(lmm_done, e + 1)
                    if b == 0:
                        dve.wait_ge(bias_loaded[j], 8 * (n - j) + 16)
                    if b > 1:
                        dve.wait_ge(trp_done, e - 1)
                    nc.vector.scalar_tensor_tensor(
                        lg[b % 2][:, :, keys], DB[b % 2][:, :].rearrange("p (h c) -> p h c", h=2)[:, :, keys], HD ** -0.5,
                        bias[:, j, :, keys], ALU.mult, ALU.add).then_inc(lg_ready, 1)
                    dve.wait_ge(lg_ready, e + 1)
                    ch = Chain(dve, soft_step, 3 * e)
                    ch.link(nc.vector.tensor_reduce(s[:, MX, :], lg[b % 2][:, :, keys], AX_X, ALU.max))
                    sink = sinks[:, bass.ds(2 * n, 2)]
                    ch.link(nc.vector.tensor_tensor(s[:, MM, :], s[:, MX, :], sink, ALU.max))
                    ch.link(nc.vector.tensor_scalar(s[:, NEG_M, :], s[:, MM, :], -1.0, None, ALU.mult))
                    nc.vector.tensor_tensor(s[:, SK, :], s[:, NEG_M, :], sink, ALU.add).then_inc(mx_ready, 1)

                def inverse(n, b):
                    e, s = NB * n + b, sm[b % 2]
                    dve.wait_ge(e_ready, 2 * e + 2)
                    dve.wait_ge(esk_ready, e + 1)
                    nc.vector.tensor_tensor(s[:, DEN, :], s[:, ES, :], s[:, ESK, :], ALU.add).then_inc(den_ready, 1)
                    dve.wait_ge(den_ready, e + 1)
                    nc.vector.reciprocal(s[:, RDEN, :], s[:, DEN, :]).then_inc(r_ready, 1)

                def gated(n, m, p):
                    dve.wait_ge(pv_done, NB * n + 4 * m + 4)
                    z = halves(zs[p])[m]
                    nc.vector.scalar_tensor_tensor(z, DB[3][:, :], 0.5, z, ALU.mult, ALU.mult).then_inc(att_ready, 1)

                def low(n, m, p):
                    if m:
                        dve.wait_ge(split_hi, split_at(l, 1, n) + 1)
                    else:
                        dve.wait_ge(half_hi, n + 1)
                    cols = bass.ds(n * T + m * HALF, HALF)
                    nc.vector.tensor_tensor(b_lo_flat[:, cols], halves(zs[p])[m], b_hi_flat[:, cols].bitcast(F32),
                                            ALU.subtract).then_inc(split_lo if m else half_lo, 1)

                def heads(n, j, last):
                    for b in range(NB):
                        if b == 7:
                            gated(n, 0, j)
                        soft(n, b, j)
                        if b:
                            inverse(n, b - 1)
                    inverse(n, NB - 1)
                    low(n, 0, j)
                    if not last:
                        normed(n + 2, q_n[1 - j], 0)
                    gated(n, 1, j)
                    low(n, 1, j)
                    if not last:
                        gate(n + 1, 1 - j)

                dve.wait_ge(split_lo, split_at(l, 0, KT))
                dve.wait_ge(x_stored, 16 * OUT * sum(SPILL[:l]))
                for kv in range(2):
                    for hh in range(2):
                        ins = nc.vector.memset(k_pad[kv][HD * (1 - hh):HD * (1 - hh) + HD, hh, :], 0.0)
                ins.then_inc(k_zeros, 1)
                normed(0, q_n[1], 1)
                normed(1, q_n[0], 0)
                gate(0, 0)
                with dve.Fori(0, 3) as i:
                    for j in range(2):
                        heads(2 * i + j, j, False)
                heads(KT - 2, 0, False)
                heads(KT - 1, 1, True)

            dve.wait_ge(bias_psum, 1)
            nc.vector.tensor_tensor(bias_rows[:, :], DB[3][0:QH, 0:BIAS_LEN], bias_mask[:, :], ALU.add)\
                .then_inc(bias_sum, 1)
            for k in range(KT):
                accumulate(0, k)
            for l in range(LAYERS):
                norm(l)
                if MIXER[l] == "gdn":
                    gdn(l)
                elif MIXER[l] == "cc":
                    cc(l)
                else:
                    swa(l)
                out_projection(l)
                embedding(l)


def _tiles(w, order=None):
    *lead, k, n = w.shape
    w = w.reshape(*lead, k // P, P, n // P, P)
    m = len(lead)
    w = w.transpose(*range(m), m + 2, m + 1, m, m + 3)
    if order is not None:
        w = w[(slice(None),) * m + (order,)]
    return w.reshape(*lead, n // P, P, k)


def _arrays(a):
    a = {k: np.asarray(v) for k, v in a.items()}
    x_t = a["x"][0].T.reshape(KT, P, T).transpose(1, 0, 2).reshape(P, KT * T)
    p_t = a["p"][:, 0].transpose(0, 2, 1).reshape(DEPTH, PLE_K, P, T).transpose(0, 2, 1, 3).reshape(DEPTH, P, PLE_K * T)
    gdn_order = [t * HEADS + h for h in range(HEADS) for t in (1, 0, 2, 3)]
    w_ba = a["gdn_w_in"][:, :, 4 * D:].reshape(2, KT, P, 16).transpose(0, 2, 1, 3).reshape(2, P, KT * 16)
    wp = a["ple_w_proj"].reshape(DEPTH, PLE_K, P, KT, P).transpose(0, 2, 3, 1, 4).reshape(DEPTH, P, KT * PLE_K * P)
    cw = a["gdn_conv_w"].reshape(2, TAPS, 3, HEADS, P)[:, :, [1, 0, 2]].transpose(4, 0, 3, 2, 1).reshape(P, -1)
    per_head = lambda v: np.broadcast_to(v[None, :, :, None], (P, 2, HEADS, NCHUNK)).reshape(P, -1)
    i, j = np.arange(P)[:, None], np.arange(P)[None, :]
    levels = [-((i // (2 << b) == j // (2 << b)) & (i >> b & 1 == 1) & (j >> b & 1 == 0)).astype(np.float32)
              for b in range(LEVELS)]
    f = np.float32
    dist = 2 * P - 1 - np.arange(BIAS_LEN)
    valid = (dist >= 0) & (dist < WINDOW)
    half_b = BUCKETS // 2
    n = np.maximum(dist, half_b)
    bucket = np.where(dist < half_b, np.maximum(dist, 0), np.minimum(
        half_b + np.floor(np.log(n / half_b) / np.log(WINDOW / half_b) * half_b).astype(np.int32), BUCKETS - 1))
    swa_order = [QH // 2, QH // 2 + 1] + [t for n in range(KT) for t in (n, KT + 2 + n)]
    cc_order = [t for n in range(KT) for t in (n, KT + n, 2 * KT + n)]
    per_tile = lambda v: v.reshape(KT, P).T
    out = {
        "w_cc_in": _tiles(a["cc_w_in"], cc_order), "w_cc_out": _tiles(a["cc_w_out"]),
        "w_swa_in": _tiles(a["swa_w_in"], swa_order), "w_swa_out": _tiles(a["swa_w_out"]),
        "c_blk": ((i // HD == j // HD) / HD).astype(f),
        "c_sinks": np.broadcast_to(a["swa_sinks"], (P, QH)),
        "c_qk_g": np.stack([np.tile(a["swa_q_norm_g"][0], 2), np.tile(a["swa_k_norm_g"][0], 2)], 1),
        "c_cc_w": a["cc_dw_w"][0].reshape(CC_TAPS, KT, P).transpose(2, 1, 0).reshape(P, -1),
        "c_cc_par": np.concatenate([per_tile(a["cc_dw_b"][0]), per_tile(a["cc_ln_g"][0]), per_tile(a["cc_ln_b"][0])], 1),
        "c_rel": a["rel_bias"],
        "c_onehot": (valid & (bucket == np.arange(BUCKETS)[:, None])).astype(f),
        "c_bias_mask": np.broadcast_to(np.where(valid, 0, NEG).astype(f), (QH, BIAS_LEN)),
        "x_t": x_t, "p_t": p_t, "w_gdn_in": _tiles(a["gdn_w_in"][:, :, :4 * D], gdn_order),
        "w_gdn_ba": w_ba, "w_gdn_out": _tiles(a["gdn_w_out"]), "w_gate": _tiles(a["ple_w_gate"]), "w_embed": wp,
        "c_ident": np.eye(P, dtype=f), "c_cum_u": (i <= j).astype(f), "c_mask_t": np.where(j >= i, 0, NEG).astype(f),
        "c_ones": np.ones((P, P), f),
        "c_masks": np.concatenate([*levels, (j > i).astype(f)], 1),
        "c_norm_g": a["norm_g"].reshape(DEPTH, KT, P).transpose(2, 0, 1).reshape(P, -1),
        "c_conv_w": cw, "c_a_log": per_head(a["gdn_A_log"]), "c_dt_b": per_head(a["gdn_dt_bias"]),
        "c_gdn_g": a["gdn_norm_g"].T,
    }
    return {k: np.ascontiguousarray(v) for k, v in out.items()}


LAYERS = DEPTH
MIXER = ["gdn", "cc", "swa", "gdn"]
SPILL = [True, True, True, False]
STREAM = TILE0[LAYERS]


def kernel(**inputs):
    import concourse.bacc as bacc
    from concourse.bass_utils import run_bass_kernel_spmd

    nc = bacc.Bacc("TRN2", target_bir_lowering=False, num_devices=1)
    arrays = _arrays(inputs)
    d = {n: nc.dram_tensor("in_" + n, a.shape, mybir.dt.from_np(a.dtype), kind="ExternalInput").ap()
         for n, a in arrays.items()}
    d["out"] = nc.dram_tensor("out_x_t", (P, KT * T), F32, kind="ExternalOutput").ap()
    save = nc.dram_tensor("x_save", (DEPTH, P, KT * T), F32, kind="Internal").ap()
    d["x_save"] = [save[l] for l in range(DEPTH)]
    d["bias_rows"] = nc.dram_tensor("bias_rows_dram", (QH, BIAS_LEN), F32, kind="Internal").ap()
    copies = nc.dram_tensor("bias_copies", (QH, P * BIAS_LEN), F32, kind="Internal").ap()
    d["bias_copies"] = copies.rearrange("h (q m) -> h q m", q=P)
    d["bias_window"] = copies[:, WINDOW - 1:WINDOW - 1 + P * (BIAS_LEN - 1)]\
        .rearrange("h (q m) -> q h m", q=P)[:, :, 0:2 * WINDOW]
    build(nc, d)
    r = run_bass_kernel_spmd(nc, [{"in_" + n: a for n, a in arrays.items()}], core_ids=[0])
    out = r.results[0]["out_x_t"].reshape(P, KT, T)
    return np.ascontiguousarray(out.transpose(2, 1, 0)).reshape(1, T, D)
```
